# Optimizing a Trainium2 kernel written in Bass

```python
import jax, jax.numpy as jnp
from jax import lax
import numpy as np

D_MODEL = 1024
BATCH = 1
SEQ = 512
DEPTH = 2
DEC_BATCH = 8
DEC_SEQ = 1
PAST_LEN = 4096
PAGE_SIZE = 128

GDN_HEADS = D_MODEL // 128
GDN_DK = 128
GDN_DV = 128
GDN_DIM = GDN_HEADS * GDN_DK
CONV_W = 4
GDN_CHUNK = 64
GDN_IN = 4 * GDN_DIM + 2 * GDN_HEADS
MLA_HEADS = D_MODEL // 128
Q_LORA = D_MODEL // 2
KV_LORA = D_MODEL // 4
NOPE_DIM = 128
ROPE_DIM = 64
QK_DIM = NOPE_DIM + ROPE_DIM
V_DIM = 128
MLA_IN = Q_LORA + KV_LORA + ROPE_DIM
ROPE_THETA = 10000.0
ATTN_BLOCK = 128
SOFTMAX_SCALE = QK_DIM ** -0.5
PEER_HEADS = 8
N_KEYS = 128
N_EXPERTS = N_KEYS * N_KEYS
PEER_TOPK = 16
PEER_QDIM = 256
PEER_HALF = PEER_QDIM // 2
PEER_BLOCK = 128
EPS = 1e-6
N_GDN = (DEPTH + 1) // 2
N_MLA = DEPTH // 2

kernel_name = 'hybrid_gdn_mla_peer_step'

def rmsnorm(x, g):
    xf = x.astype(jnp.float32)
    y = xf * lax.rsqrt(jnp.mean(xf * xf, axis=-1, keepdims=True) + EPS)
    return (y * g.astype(jnp.float32)).astype(x.dtype)

def l2norm(x):
    xf = x.astype(jnp.float32)
    return xf * lax.rsqrt(jnp.sum(xf * xf, axis=-1, keepdims=True) + EPS)

def rope(x, pos):
    half = x.shape[-1] // 2
    freq = ROPE_THETA ** (-jnp.arange(half, dtype=jnp.float32) / half)
    ang = pos.astype(jnp.float32)[:, None] * freq[None, :]
    ang = ang.reshape(ang.shape[0], *([1] * (x.ndim - 3)), half)
    cos, sin = jnp.cos(ang).astype(x.dtype), jnp.sin(ang).astype(x.dtype)
    x1, x2 = x[..., :half], x[..., half:]
    return jnp.concatenate([x1 * cos - x2 * sin, x2 * cos + x1 * sin], axis=-1)

def causal_conv(x, buf, w):
    T = x.shape[1]
    xp = jnp.concatenate([buf.astype(x.dtype), x], axis=1)
    y = xp[:, 0:T] * w[0]
    for j in range(1, CONV_W):
        y = y + xp[:, j:j + T] * w[j]
    return y, xp[:, T:]

def gated_delta_chunked(q, k, v, beta, g, S0, chunk):
    B, T, H, _ = q.shape
    nc = T // chunk

    def to_chunks(t):
        return jnp.moveaxis(t.reshape(B, nc, chunk, H, *t.shape[3:]), 3, 1)

    q, k, v, beta, g = (to_chunks(t) for t in (q, k, v, beta, g))
    G = jnp.cumsum(g, axis=-1)
    incl = jnp.tril(jnp.ones((chunk, chunk), bool))
    strict = jnp.tril(jnp.ones((chunk, chunk), bool), -1)
    decay = jnp.exp(jnp.where(incl, G[..., :, None] - G[..., None, :], -jnp.inf))
    kk = jnp.einsum('bhnid,bhnjd->bhnij', k, k)
    a_mat = jnp.where(strict, beta[..., :, None] * kk * decay, 0.0) + jnp.eye(chunk, dtype=jnp.float32)

    def solve(rhs):
        return lax.linalg.triangular_solve(a_mat, rhs, left_side=True, lower=True, unit_diagonal=True)

    w_v = solve(v * beta[..., None])
    w_k = solve(k * (beta * jnp.exp(G))[..., None])
    qk = jnp.einsum('bhnid,bhnjd->bhnij', q, k) * decay
    q_dec = q * jnp.exp(G)[..., None]
    k_dec = k * jnp.exp(G[..., -1:] - G)[..., None]
    g_tot = jnp.exp(G[..., -1])
    xs = tuple(jnp.moveaxis(t, 2, 0) for t in (w_v, w_k, qk, q_dec, k_dec, g_tot))

    def step(S, inp):
        wv, wk, qkn, qd, kd, gt = inp
        u = wv - jnp.einsum('bhck,bhkv->bhcv', wk, S)
        o = jnp.einsum('bhck,bhkv->bhcv', qd, S) + jnp.einsum('bhij,bhjv->bhiv', qkn, u)
        S = S * gt[..., None, None] + jnp.einsum('bhck,bhcv->bhkv', kd, u)
        return S, o

    S, o = lax.scan(step, S0, xs)
    o = jnp.transpose(o, (1, 0, 3, 2, 4)).reshape(B, T, H, v.shape[-1])
    return o, S

def gdn_mixer(xn, conv_buf, S0, w_in, conv_w, a_log, dt_bias, g_out, w_out, chunk):
    B, T, _ = xn.shape
    proj = xn @ w_in
    qkv = proj[..., :3 * GDN_DIM]
    z = proj[..., 3 * GDN_DIM:4 * GDN_DIM].reshape(B, T, GDN_HEADS, GDN_DV)
    b = proj[..., 4 * GDN_DIM:4 * GDN_DIM + GDN_HEADS]
    a = proj[..., 4 * GDN_DIM + GDN_HEADS:]
    qkv, new_buf = causal_conv(qkv, conv_buf, conv_w)
    qkv = jax.nn.silu(qkv)
    q, k, v = jnp.split(qkv, 3, axis=-1)
    q = l2norm(q.reshape(B, T, GDN_HEADS, GDN_DK)) * (GDN_DK ** -0.5)
    k = l2norm(k.reshape(B, T, GDN_HEADS, GDN_DK))
    v = v.reshape(B, T, GDN_HEADS, GDN_DV).astype(jnp.float32)
    beta = jax.nn.sigmoid(b.astype(jnp.float32))
    g = -jnp.exp(a_log.astype(jnp.float32)) * jax.nn.softplus(a.astype(jnp.float32) + dt_bias.astype(jnp.float32))
    o, S = gated_delta_chunked(q, k, v, beta, g, S0.astype(jnp.float32), chunk)
    o = (rmsnorm(o, g_out) * jax.nn.silu(z.astype(jnp.float32))).astype(xn.dtype)
    y = o.reshape(B, T, GDN_DIM) @ w_out
    return y, S.astype(xn.dtype), new_buf

def latent_attention(q_lat, q_rope, c, kr, ksc, q_pos, k_pos):
    B, Tq, H, R = q_lat.shape
    blk = ATTN_BLOCK if Tq % ATTN_BLOCK == 0 else Tq
    nb = Tq // blk
    ks = jnp.transpose(ksc, (0, 2, 1))[:, :, None, :]

    def block(args):
        ql, qr, qp = args
        s = (jnp.einsum('bqhr,bkr->bhqk', ql, c, preferred_element_type=jnp.float32)
             + jnp.einsum('bqhp,bkp->bhqk', qr, kr, preferred_element_type=jnp.float32))
        s = s * ks.astype(jnp.float32) * SOFTMAX_SCALE
        s = jnp.where(k_pos[None, :] <= qp[:, None], s, -jnp.inf)
        p = jax.nn.softmax(s, axis=-1)
        return jnp.einsum('bhqk,bkr->bqhr', p.astype(c.dtype), c)

    qlb = jnp.moveaxis(q_lat.reshape(B, nb, blk, H, R), 1, 0)
    qrb = jnp.moveaxis(q_rope.reshape(B, nb, blk, H, q_rope.shape[-1]), 1, 0)
    o = lax.map(block, (qlb, qrb, q_pos.reshape(nb, blk)))
    return jnp.moveaxis(o, 0, 1).reshape(B, Tq, H, R)

def mla_mixer(xn, past_c, past_kr, past_ks, w_in, g_cq, g_ckv, w_uq, g_qn, g_kn, w_uk, w_uv, w_out):
    B, T, _ = xn.shape
    past = 0 if past_c is None else past_c.shape[1]
    q_pos = past + jnp.arange(T)
    proj = xn @ w_in
    cq = rmsnorm(proj[..., :Q_LORA], g_cq)
    ckv = rmsnorm(proj[..., Q_LORA:Q_LORA + KV_LORA], g_ckv)
    kr = rope(proj[..., Q_LORA + KV_LORA:], q_pos)
    q = (cq @ w_uq).reshape(B, T, MLA_HEADS, QK_DIM)
    q = jnp.concatenate([q[..., :NOPE_DIM], rope(q[..., NOPE_DIM:], q_pos)], axis=-1)
    q = rmsnorm(q, g_qn) * g_kn
    k_nope = jnp.einsum('btr,rhd->bthd', ckv, w_uk).astype(jnp.float32)
    krf = kr.astype(jnp.float32)
    ksq = jnp.sum(k_nope * k_nope, -1) + jnp.sum(krf * krf, -1)[..., None]
    ksc = lax.rsqrt(ksq / QK_DIM + EPS).astype(xn.dtype)
    q_lat = jnp.einsum('bthd,rhd->bthr', q[..., :NOPE_DIM], w_uk)
    q_rope = q[..., NOPE_DIM:]
    if past_c is None:
        c_all, kr_all, ks_all = ckv, kr, ksc
    else:
        c_all = jnp.concatenate([past_c.astype(ckv.dtype), ckv], axis=1)
        kr_all = jnp.concatenate([past_kr.astype(kr.dtype), kr], axis=1)
        ks_all = jnp.concatenate([past_ks.astype(ksc.dtype), ksc], axis=1)
    k_pos = jnp.arange(past + T)
    o_lat = latent_attention(q_lat, q_rope, c_all, kr_all, ks_all, q_pos, k_pos)
    o = jnp.einsum('bthr,rhd->bthd', o_lat, w_uv).reshape(B, T, MLA_HEADS * V_DIM)
    return o @ w_out, ckv, kr, ksc

def peer_ffn(xn, w_q, sub_keys, u_tab, v_tab):
    lead = xn.shape[:-1]
    x2 = xn.reshape(-1, xn.shape[-1])
    T = x2.shape[0]
    q = (x2 @ w_q).reshape(T, PEER_HEADS, 2, PEER_HALF)
    s = jnp.einsum('thpd,hpnd->thpn', q, sub_keys, preferred_element_type=jnp.float32)
    sv, si = lax.top_k(s, PEER_TOPK)
    cand = (sv[:, :, 0, :, None] + sv[:, :, 1, None, :]).reshape(T, PEER_HEADS, PEER_TOPK * PEER_TOPK)
    cidx = (si[:, :, 0, :, None] * N_KEYS + si[:, :, 1, None, :]).reshape(T, PEER_HEADS, PEER_TOPK * PEER_TOPK)
    top_s, top_i = lax.top_k(cand, PEER_TOPK)
    idx = jnp.take_along_axis(cidx, top_i, axis=-1).reshape(T, PEER_HEADS * PEER_TOPK)
    gate = jax.nn.softmax(top_s, axis=-1).reshape(T, PEER_HEADS * PEER_TOPK)
    blk = PEER_BLOCK if T % PEER_BLOCK == 0 else T
    nb = T // blk

    def block(args):
        xb, ib, gb = args
        h = jnp.einsum('td,ted->te', xb, u_tab[ib], preferred_element_type=jnp.float32)
        act = jax.nn.gelu(h, approximate=False) * gb
        return jnp.einsum('te,ted->td', act.astype(xb.dtype), v_tab[ib])

    out = lax.map(block, (x2.reshape(nb, blk, -1), idx.reshape(nb, blk, -1), gate.reshape(nb, blk, -1)))
    return out.reshape(*lead, x2.shape[-1])

def setup_inputs(seed: int = 0) -> dict:
    key = jax.random.key(seed)
    ks = jax.random.split(key, 32)
    f32 = jnp.float32

    def nrm(i, shape, scale):
        return jax.random.normal(ks[i], shape, f32) * scale

    def gain(i, shape):
        return 1.0 + 0.01 * jax.random.normal(ks[i], shape, f32)

    n_pages = PAST_LEN // PAGE_SIZE
    n_used = DEC_BATCH * n_pages
    n_pool = n_used + max(1, n_used // 4)
    page_table = jax.random.permutation(ks[5], n_pool)[:n_used].reshape(DEC_BATCH, n_pages).astype(jnp.int32)
    dt = jax.random.uniform(ks[12], (N_GDN, GDN_HEADS), f32, 1e-3, 1e-1)
    return {
        'x_prompt': nrm(0, (BATCH, SEQ, D_MODEL), 1.0),
        'x_sample': nrm(1, (DEC_BATCH, DEC_SEQ, D_MODEL), 1.0),
        'cache_latent': nrm(2, (N_MLA, n_pool, PAGE_SIZE, KV_LORA), 1.0),
        'cache_krope': nrm(3, (N_MLA, n_pool, PAGE_SIZE, ROPE_DIM), 1.0),
        'cache_kscale': jax.random.uniform(ks[4], (N_MLA, n_pool, PAGE_SIZE, MLA_HEADS), f32, 0.8, 1.2),
        'page_table': page_table,
        'state_ssm': nrm(6, (N_GDN, DEC_BATCH, GDN_HEADS, GDN_DK, GDN_DV), 0.1),
        'state_conv': nrm(7, (N_GDN, DEC_BATCH, CONV_W - 1, 3 * GDN_DIM), 1.0),
        'norm_mix': gain(8, (DEPTH, D_MODEL)),
        'norm_ffn': gain(9, (DEPTH, D_MODEL)),
        'gdn_w_in': nrm(10, (N_GDN, D_MODEL, GDN_IN), D_MODEL ** -0.5),
        'gdn_conv_w': nrm(11, (N_GDN, CONV_W, 3 * GDN_DIM), CONV_W ** -0.5),
        'gdn_a_log': jnp.log(jax.random.uniform(ks[13], (N_GDN, GDN_HEADS), f32, 1.0, 16.0)),
        'gdn_dt_bias': jnp.log(jnp.expm1(dt)),
        'gdn_out_norm': gain(14, (N_GDN, GDN_DV)),
        'gdn_w_out': nrm(15, (N_GDN, GDN_DIM, D_MODEL), GDN_DIM ** -0.5),
        'mla_w_in': nrm(16, (N_MLA, D_MODEL, MLA_IN), D_MODEL ** -0.5),
        'mla_cq_norm': gain(17, (N_MLA, Q_LORA)),
        'mla_ckv_norm': gain(18, (N_MLA, KV_LORA)),
        'mla_w_uq': nrm(19, (N_MLA, Q_LORA, MLA_HEADS * QK_DIM), Q_LORA ** -0.5),
        'mla_q_norm': gain(20, (N_MLA, QK_DIM)),
        'mla_k_norm': gain(21, (N_MLA, QK_DIM)),
        'mla_w_uk': nrm(22, (N_MLA, KV_LORA, MLA_HEADS, NOPE_DIM), KV_LORA ** -0.5),
        'mla_w_uv': nrm(23, (N_MLA, KV_LORA, MLA_HEADS, V_DIM), KV_LORA ** -0.5),
        'mla_w_out': nrm(24, (N_MLA, MLA_HEADS * V_DIM, D_MODEL), (MLA_HEADS * V_DIM) ** -0.5),
        'peer_w_q': nrm(25, (DEPTH, D_MODEL, PEER_HEADS * PEER_QDIM), D_MODEL ** -0.5),
        'peer_sub_keys': nrm(26, (DEPTH, PEER_HEADS, 2, N_KEYS, PEER_HALF), PEER_HALF ** -0.5),
        'peer_u': nrm(27, (DEPTH, N_EXPERTS, D_MODEL), D_MODEL ** -0.5),
        'peer_v': nrm(28, (DEPTH, N_EXPERTS, D_MODEL), (PEER_HEADS * PEER_TOPK) ** -0.5),
    }

def reference(x_prompt, x_sample, cache_latent, cache_krope, cache_kscale, page_table, state_ssm, state_conv,
              norm_mix, norm_ffn, gdn_w_in, gdn_conv_w, gdn_a_log, gdn_dt_bias, gdn_out_norm, gdn_w_out,
              mla_w_in, mla_cq_norm, mla_ckv_norm, mla_w_uq, mla_q_norm, mla_k_norm, mla_w_uk, mla_w_uv, mla_w_out,
              peer_w_q, peer_sub_keys, peer_u, peer_v):
    xp, xs = x_prompt, x_sample
    bp, bs = xp.shape[0], xs.shape[0]
    past_len = page_table.shape[1] * cache_latent.shape[2]
    lat_p, kr_p, ksc_p, ssm_p, conv_p = [], [], [], [], []
    lat_s, kr_s, ksc_s, ssm_s, conv_s = [], [], [], [], []
    for i in range(DEPTH):
        j = i // 2
        hp = rmsnorm(xp, norm_mix[i])
        hs = rmsnorm(xs, norm_mix[i])
        if i % 2 == 0:
            gw = (gdn_w_in[j], gdn_conv_w[j], gdn_a_log[j], gdn_dt_bias[j], gdn_out_norm[j], gdn_w_out[j])
            buf0 = jnp.zeros((bp, CONV_W - 1, 3 * GDN_DIM), xp.dtype)
            s0 = jnp.zeros((bp, GDN_HEADS, GDN_DK, GDN_DV), xp.dtype)
            yp, sp, cp = gdn_mixer(hp, buf0, s0, *gw, chunk=GDN_CHUNK)
            ys, ss, cs = gdn_mixer(hs, state_conv[j], state_ssm[j], *gw, chunk=xs.shape[1])
            ssm_p.append(sp); conv_p.append(cp); ssm_s.append(ss); conv_s.append(cs)
        else:
            mw = (mla_w_in[j], mla_cq_norm[j], mla_ckv_norm[j], mla_w_uq[j], mla_q_norm[j], mla_k_norm[j],
                  mla_w_uk[j], mla_w_uv[j], mla_w_out[j])
            yp, lp, rp, kp = mla_mixer(hp, None, None, None, *mw)
            past_c = cache_latent[j][page_table].reshape(bs, past_len, KV_LORA)
            past_r = cache_krope[j][page_table].reshape(bs, past_len, ROPE_DIM)
            past_k = cache_kscale[j][page_table].reshape(bs, past_len, MLA_HEADS)
            ys, ls, rs, kss = mla_mixer(hs, past_c, past_r, past_k, *mw)
            lat_p.append(lp); kr_p.append(rp); ksc_p.append(kp)
            lat_s.append(ls); kr_s.append(rs); ksc_s.append(kss)
        xp = xp + yp
        xs = xs + ys
        pw = (peer_w_q[i], peer_sub_keys[i], peer_u[i], peer_v[i])
        xp = xp + peer_ffn(rmsnorm(xp, norm_ffn[i]), *pw)
        xs = xs + peer_ffn(rmsnorm(xs, norm_ffn[i]), *pw)
    return (xp, xs,
            jnp.stack(lat_p), jnp.stack(kr_p), jnp.stack(ksc_p), jnp.stack(ssm_p), jnp.stack(conv_p),
            jnp.stack(lat_s), jnp.stack(kr_s), jnp.stack(ksc_s), jnp.stack(ssm_s), jnp.stack(conv_s))


_drawn_inputs = setup_inputs


def setup_inputs(seed=0):
    import zlib

    import numpy as np

    out = dict(_drawn_inputs(seed))
    spreads = {}
    factors = {'cache_krope': 4.128,
     'cache_kscale': 7.535,
     'norm_mix': 3.418,
     'norm_ffn': 63.0,
     'gdn_out_norm': 8.0,
     'mla_cq_norm': 24.669,
     'mla_ckv_norm': 18.736,
     'mla_q_norm': 24.926,
     'mla_k_norm': 24.145}
    for name, (base, spread) in spreads.items():
        noise = np.random.default_rng([zlib.crc32(name.encode()), seed]).standard_normal(out[name].shape)
        drawn = base * np.exp(spread * noise) if base else spread * noise
        out[name] = __import__('jax').numpy.asarray(drawn.astype(out[name].dtype))
    for name, factor in factors.items():
        out[name] = (out[name] * factor).astype(out[name].dtype)
    return out
```

```python
from contextlib import ExitStack

import concourse.bass as bass
from concourse import mybir

ALU = mybir.AluOpType
ACT = mybir.ActivationFunctionType
AX = mybir.AxisListType
F32 = mybir.dt.float32
U32 = mybir.dt.uint32
ds = bass.ds

P = 128
D = 1024
KD = D // P
SEQ = 512
NT = SEQ // P
NS = 8
ROWS = SEQ + NS
H = 8
HD = 128
KINDS = 4
QKV = 3 * H
CW = 4
QL, KL, RD = 512, 256, 64
QK = HD + RD
MIN = QL + KL + RD
PAST = 4096
PAGE = 128
PER = PAST // P
GRP = PAGE // PER
TOPK = 16
NK = 128
EPS = 1e-6
ROPE_THETA = 10000.0
NEG = -1.0e30
RING = 8

C_ID, C_ONE, C_UP, C_STRICT, C_NEG, C_LEVEL = 0, 1, 2, 3, 4, 5
LEVELS = 7
N_CONST = C_LEVEL + LEVELS


def after(eng, *waits):
    for sem, value in waits:
        eng.wait_ge(sem, value)


class Apart:

    def __call__(self, eng, *waits):
        waits = [(sem, value if isinstance(value, int) else eng.to_reg(value)) for sem, value in waits]
        if not isinstance(waits[0][1], int):
            eng.wait_ge(self.idle, 0)
        after(eng, *waits)


apart = Apart()


class Core:

    def __init__(self, nc, ctx, ins, outs):
        self.nc, self.ctx, self.i, self.o = nc, ctx, ins, outs
        self.n = 0
        self.phase = 0
        apart.idle = nc.alloc_semaphore("idle")
        self.x = self.sbuf(ctx, "x", [P, NT, D])
        self.xs = self.sbuf(ctx, "xs", [NS, D])
        self.const = self.sbuf(ctx, "const", [P, N_CONST, P])
        self.ident = self.const[:, C_ID, :]
        self.ones = self.const[:, C_ONE, :]
        self.eps = self.sbuf(ctx, "eps", [P, 1])[:, 0:1]

    def sbuf(self, ctx, name, shape, dtype=F32):
        self.n += 1
        return ctx.enter_context(self.nc.sbuf_tensor(f"{name}_{self.n}", shape, dtype))

    def psum(self, ctx, name, shape):
        self.n += 1
        return ctx.enter_context(self.nc.psum_tensor(f"{name}_{self.n}", shape, F32))



class Marks:

    def __init__(self, core, prefix, **per):
        self.core, self.per = core, per
        self.sems = {n: core.nc.alloc_semaphore(f"{prefix}_{n}_{core.phase}") for n in per}
        core.phase += 1

    def __getitem__(self, name):
        return self.sems[name]

    def at(self, name, i, k):
        return self.sems[name], i * self.per[name] + k

    def __enter__(self):
        return self

    def __exit__(self, *error):
        if error[0] is None:
            self.core.nc.clear_and_free_semaphores(list(self.sems.values()))
            self.core.nc.all_engine_barrier()


def rows_of(core, t):
    return (core.x[:, t, :], P) if t < NT else (core.xs[:, :], NS)


def norm(core, gain, xn, xns, xnT):
    nc = core.nc
    T = NT + 1
    with Marks(core, "norm", gain=16, sum=T, root=T, inv=2 * T, row=T, turned=2 * T, copied=T, copied2=T) as s, ExitStack() as ctx:
        g = core.sbuf(ctx, "gain", [P, D])
        junk = core.sbuf(ctx, "junk", [P, D])
        stat = core.sbuf(ctx, "stat", [P, 3, NT + 1])
        bank = [core.psum(ctx, "turn", [P, 4, P]) for _ in range(4)]

        def normed(t):
            return xn[:, t, :] if t < NT else xns[:, :]

        with nc.Block() as block:
            @block.sync
            def _(sp):
                sp.dma_start(g[:, :], gain.to_broadcast([P, D])).then_inc(s["gain"], 16)

            @block.scalar
            def _(act):
                for t in range(NT + 1):
                    x, n = rows_of(core, t)
                    if t:
                        act.wait_ge(s["sum"], t)
                    act.activation(junk[:n, :], x, ACT.Square, accum_out=stat[:n, 0, t:t + 1]).then_inc(s["sum"], 1)
                for t in range(NT + 1):
                    n = rows_of(core, t)[1]
                    act.wait_ge(s["inv"], 2 * (t) + 1)
                    act.activation(stat[:n, 1, t:t + 1], stat[:n, 1, t:t + 1], ACT.Sqrt).then_inc(s["root"], 1)
                for t in range(NT + 1):
                    n = rows_of(core, t)[1]
                    act.wait_ge(s["turned"], 2 * (t) + 1)
                    act.activation(xnT[:, 0:4, P * t:P * t + n], bank[2 * (t % 2)][:, :, :n], ACT.Copy).then_inc(s["copied"], 1)

            @block.vector
            def _(dve):
                for t in range(NT + 1):
                    n = rows_of(core, t)[1]
                    dve.wait_ge(s["sum"], t + 1)
                    dve.tensor_scalar(stat[:n, 1, t:t + 1], stat[:n, 0, t:t + 1], 1.0 / D, EPS, ALU.mult, ALU.add).then_inc(s["inv"], 1)
                    dve.wait_ge(s["root"], t + 1)
                    dve.reciprocal(stat[:n, 2, t:t + 1], stat[:n, 1, t:t + 1]).then_inc(s["inv"], 1)
                    if t == 0:
                        dve.wait_ge(s["gain"], 16)
                    x, n = rows_of(core, t)
                    dve.wait_ge(s["inv"], 2 * (t + 1))
                    dve.scalar_tensor_tensor(normed(t), x, stat[:n, 2, t:t + 1], g[:n, :], ALU.mult, ALU.mult).then_inc(s["row"], 1)
                for t in range(NT + 1):
                    n = rows_of(core, t)[1]
                    dve.wait_ge(s["turned"], 2 * (t) + 2)
                    dve.tensor_copy(xnT[:, 4:8, P * t:P * t + n], bank[2 * (t % 2) + 1][:, :, :n]).then_inc(s["copied2"], 1)

            @block.tensor
            def _(pe):
                for t in range(NT + 1):
                    n = rows_of(core, t)[1]
                    pe.wait_ge(s["row"], t + 1)
                    if t >= 2:
                        pe.wait_ge(s["copied"], t - 1)
                        pe.wait_ge(s["copied2"], t - 1)
                    for k in range(KD):
                        last = pe.transpose(bank[2 * (t % 2) + k // 4][:, k % 4, :n], normed(t)[:, P * k:P * k + P],
                                            core.const[:n, C_ID, :n])
                        if k % 4 == 3:
                            last.then_inc(s["turned"], 1)


def part(tile, n, width):
    dims = " ".join("abcd"[:len(tile.shape) - 1])
    flat = tile[:].rearrange(f"p {dims} -> p ({dims})") if len(tile.shape) > 2 else tile
    return flat[:, ds(n * width, width)]


def gdn_in(core, xnT, F, Fs, taps, ba):
    nc = core.nc
    W = 4
    NC, PAD = KINDS * H, CW - 1
    with Marks(core, "gdn", **{f"landed{w}": 16 for w in range(W)}, small=48, made=1, raw=1, sraw=1, kept=1, conved=1, silu=1,
               sconv=1, stored=32, bas=1, bac=2, zero=3) as s, ExitStack() as ctx:
        landed = [s[f"landed{w}"] for w in range(W)]
        small, made, raw, sraw, kept, conved, silu, sconv, stored, bas, bac, zero = (
            s[n] for n in ("small", "made", "raw", "sraw", "kept", "conved", "silu", "sconv", "stored", "bas", "bac", "zero"))
        w = core.sbuf(ctx, "w", [P, W, KD, P])
        wba = core.sbuf(ctx, "wba", [P, KD, 2 * H])
        cw = core.sbuf(ctx, "cw", [P, QKV * CW])
        inp = core.sbuf(ctx, "inp", [P, 2, PAD + SEQ])
        y = core.sbuf(ctx, "y", [P, 2, SEQ])
        keep = core.sbuf(ctx, "keep", [P, QKV, PAD])
        prod = core.sbuf(ctx, "prod", [P, QKV, CW, NS])
        acc = [core.psum(ctx, "acc", [P, SEQ]) for _ in range(2)]
        accs = [core.psum(ctx, "accs", [P, NS]) for _ in range(2)]
        pba = core.psum(ctx, "pba", [P, NT + 1, 2 * H])
        with nc.Block() as block:
            @block.sync
            def _(sp):
                sp.dma_start(wba[:, :, :], core.i["w_ba"]).then_inc(small, 16)
                sp.dma_start(cw[:, :], core.i["conv_w"]).then_inc(small, 16)
                sp.dma_start(taps[:, :, 0:PAD, :], core.i["state_conv"]).then_inc(small, 16)
                for c in range(W):
                    sp.dma_start(w[:, c, :, :], core.i["w_gdn"][c]).then_inc(landed[c], 16)
                with sp.Fori(1, NC // W) as i:
                    for c in range(W):
                        after(sp, (made, i * W + (c - W + 1)))
                        sp.dma_start(w[:, c, :, :], core.i["w_gdn"][ds(i * W + c, 1), :, :, :].rearrange("o p k n -> (o p) k n")).then_inc(landed[c], 16)
                sp.wait_ge(kept, QKV)
                sp.dma_start(core.o["conv_p"], keep[:, :, :]).then_inc(stored, 16)
                sp.wait_ge(sraw, NC)
                sp.dma_start(core.o["conv_s"], taps[:, :, 1:CW, :]).then_inc(stored, 16)
                sp.wait_ge(stored, 32)

            @block.tensor
            def _(pe):
                pe.wait_ge(small, 48)
                for t in range(NT + 1):
                    n = P if t < NT else NS
                    for k in range(KD):
                        last = pe.matmul(pba[:n, t, :], xnT[:, k, P * t:P * t + n], wba[:, k, :], start=k == 0, stop=k == KD - 1)
                last.then_inc(bas, 1)
                with pe.Fori(0, NC // W) as i:
                    for c in range(W):
                        after(pe, (landed[c], (i + 1) * 16), (raw, i * W + max(c - 1, 0)), (sraw, i * W + max(c - 1, 0)))
                        for k in range(KD):
                            pe.matmul(acc[c % 2][:, :], w[:, c, k, :], xnT[:, k, 0:SEQ], start=k == 0, stop=k == KD - 1)
                        for k in range(KD):
                            last = pe.matmul(accs[c % 2][:, :], w[:, c, k, :], xnT[:, k, SEQ:ROWS], start=k == 0, stop=k == KD - 1)
                        last.then_inc(made, 1)

            @block.vector
            def _(dve):
                dve.memset(ba[:, :, :], 0.0).then_inc(zero, 1)
                for c in range(2):
                    dve.memset(inp[:, c, 0:PAD], 0.0).then_inc(zero, 1)
                dve.wait_ge(zero, 3)
                dve.wait_ge(bas, 1)
                dve.tensor_copy(ba[:, 0:NT, :], pba[:, 0:NT, :]).then_inc(bac, 1)
                dve.tensor_copy(ba[:NS, NT, :], pba[:NS, NT, :]).then_inc(bac, 1)
                with dve.Fori(0, QKV // W) as i:
                    for c in range(W):
                        n, b = i * W + c, c % 2
                        after(dve, (made, n + 1))
                        dve.tensor_copy(part(taps, n * CW + PAD, NS), accs[b][:, :]).then_inc(sraw, 1)
                        after(dve, (raw, n + 1))
                        dve.tensor_copy(part(keep, n, PAD), inp[:, b, SEQ:SEQ + PAD]).then_inc(kept, 1)
                        after(dve, (silu, i * W + max(c - 1, 0)))
                        dve.tensor_scalar(y[:, b, :], inp[:, b, PAD:PAD + SEQ], part(cw, n * CW + PAD, 1), None, ALU.mult).then_inc(conved, 1)
                        for j in range(PAD):
                            after(dve, (conved, n * CW + (j + 1)))
                            dve.scalar_tensor_tensor(y[:, b, :], inp[:, b, j:j + SEQ], part(cw, n * CW + j, 1),
                                                     y[:, b, :], ALU.mult, ALU.add).then_inc(conved, 1)
                with dve.Fori(QKV // W, NC // W) as i:
                    for c in range(W):
                        after(dve, (made, i * W + (c + 1)))
                        dve.tensor_copy(part(Fs, i * W + c, NS), accs[c % 2][:, :]).then_inc(sraw, 1)
                dve.wait_ge(sraw, NC)
                dve.tensor_tensor(prod[:, :, :, :], taps[:, :, :, :],
                                  cw[:, :].rearrange("p (c j o) -> p c j o", j=CW, o=1).to_broadcast([P, QKV, CW, NS]), ALU.mult).then_inc(sconv, 1)
                dve.wait_ge(sconv, 1)
                dve.tensor_reduce(Fs[:, 0:QKV, :], prod[:, :, :, :].rearrange("p c j b -> p c b j"), AX.X, ALU.add).then_inc(sconv, 1)

            @block.scalar
            def _(act):
                act.wait_ge(zero, 3)

                def copy(i, c):
                    after(act, (made, i * W + (c + 1)), (conved, (i * W + max(c - 1, 0)) * CW), (kept, i * W + max(c - 1, 0)))
                    act.activation(inp[:, c % 2, PAD:PAD + SEQ], acc[c % 2][:, :], ACT.Copy).then_inc(raw, 1)

                def smooth(i, c):
                    after(act, (conved, (i * W + (c + 1)) * CW))
                    act.activation(part(F, i * W + c, SEQ), y[:, c % 2, :], ACT.Silu).then_inc(silu, 1)

                with act.Fori(0, QKV // W) as i:
                    copy(i, 0)
                    for c in range(1, W):
                        copy(i, c)
                        smooth(i, c - 1)
                    smooth(i, W - 1)
                with act.Fori(QKV // W, NC // W) as i:
                    for c in range(W):
                        after(act, (made, i * W + (c + 1)))
                        act.activation(part(F, i * W + c, SEQ), acc[c % 2][:, :], ACT.Silu).then_inc(raw, 1)
                act.wait_ge(sconv, 2)
                act.activation(Fs[:, :, :], Fs[:, :, :], ACT.Silu).then_inc(silu, 1)


def gdn_gate(core, ba, cols, srep, gout):
    nc = core.nc
    N = NT * H
    with Marks(core, "gate", inp=32, step=17, acts=6, summed=2) as s, ExitStack() as ctx:
        inp, step, acts, summed = (s[n] for n in ("inp", "step", "acts", "summed"))
        bias = core.sbuf(ctx, "bias", [P, H])
        alog = core.sbuf(ctx, "alog", [P, H])
        a = core.sbuf(ctx, "a", [P, NT + 1, H])
        neg = core.sbuf(ctx, "neg", [P, NT + 1, H])
        g = core.sbuf(ctx, "g", [P, NT + 1, H])
        beta = core.sbuf(ctx, "beta", [P, NT + 1, H])
        ex = core.sbuf(ctx, "ex", [P, 3, N])
        spread = core.sbuf(ctx, "spread", [NS, 2, H, NS])
        psum = core.psum(ctx, "sums", [P, 3, 2 * H * NS])
        with nc.Block() as block:
            @block.sync
            def _(sp):
                sp.dma_start(bias[:, :], core.i["dt_bias"].to_broadcast([P, H])).then_inc(inp, 16)
                sp.dma_start(alog[:, :], core.i["a_log"].to_broadcast([P, H])).then_inc(inp, 16)
                sp.dma_start(gout[:, :], core.i["g_out"]).then_inc(inp, 16)
                sp.wait_ge(inp, 48)

            @block.scalar
            def _(act):
                act.wait_ge(inp, 48)
                act.activation(beta[:, :, :], ba[:, :, 0:H], ACT.Sigmoid).then_inc(acts, 1)
                act.activation(alog[:, :], alog[:, :], ACT.Exp).then_inc(acts, 1)
                act.wait_ge(step, 3)
                act.activation(neg[:, :, :], neg[:, :, :], ACT.Exp).then_inc(acts, 1)
                act.wait_ge(step, 4)
                act.activation(neg[:, :, :], neg[:, :, :], ACT.Ln).then_inc(acts, 1)
                act.wait_ge(step, 10)
                act.activation(ex[:, :, :], ex[:, :, :], ACT.Exp).then_inc(acts, 1)
                act.wait_ge(acts, 5)
                act.wait_ge(summed, 2)
                act.activation(srep[:, 1, :], psum[:, 2, H * NS:], ACT.Exp).then_inc(acts, 1)

            @block.vector
            def _(dve):
                n = [0]

                def then(ins):
                    ins.then_inc(step, 1)
                    n[0] += 1
                    dve.wait_ge(step, n[0])

                dve.wait_ge(inp, 48)
                then(dve.tensor_tensor(a[:, :, :], ba[:, :, H:], bias[:, :].rearrange("p (o h) -> p o h", o=1).to_broadcast([P, NT + 1, H]), ALU.add))
                then(dve.tensor_scalar(neg[:, :, :], a[:, :, :], -1.0, None, ALU.mult))
                then(dve.tensor_tensor(neg[:, :, :], neg[:, :, :], a[:, :, :], ALU.min))
                dve.wait_ge(acts, 3)
                then(dve.tensor_scalar(neg[:, :, :], neg[:, :, :], 1.0, None, ALU.add))
                dve.wait_ge(acts, 4)
                then(dve.scalar_tensor_tensor(g[:, :, :], a[:, :, :], 0.0, neg[:, :, :], ALU.max, ALU.add))
                then(dve.scalar_tensor_tensor(g[:, :, :], g[:, :, :], -1.0,
                                              alog[:, :].rearrange("p (o h) -> p o h", o=1).to_broadcast([P, NT + 1, H]), ALU.mult, ALU.mult))
                dve.wait_ge(summed, 1)
                then(dve.tensor_copy(cols[:, 2, :], psum[:, 0, 0:N]))
                then(dve.tensor_copy(ex[:, 0, :], cols[:, 2, :]))
                then(dve.tensor_tensor(ex[:, 1, :], psum[:, 1, 0:N], cols[:, 2, :], ALU.subtract))
                then(dve.tensor_copy(ex[:, 2, :], psum[:, 1, 0:N]))
                then(dve.tensor_copy(cols[:, 0, :], beta[:, 0:NT, :].rearrange("p t h -> p (t h)")))
                then(dve.tensor_copy(cols[:, 1, :], g[:, 0:NT, :].rearrange("p t h -> p (t h)")))
                dve.wait_ge(acts, 5)
                then(dve.tensor_tensor(cols[:, 3, :], cols[:, 0, :], ex[:, 0, :], ALU.mult))
                then(dve.tensor_copy(cols[:, 4:6, :], ex[:, 1:3, :]))
                sel = core.const[:NS, C_ID, 0:NS].rearrange("p (o b) -> p o b", o=1).to_broadcast([NS, H, NS])
                for j, src in enumerate((beta, g)):
                    then(dve.tensor_tensor(spread[:, j, :, :], sel, src[:NS, NT, :].rearrange("p (h o) -> p h o", o=1).to_broadcast([NS, H, NS]), ALU.mult))
                dve.wait_ge(acts, 6)
                then(dve.tensor_copy(srep[:, 0, :], psum[:, 2, 0:H * NS]))
                then(dve.tensor_tensor(srep[:, 2, :], srep[:, 0, :], srep[:, 1, :], ALU.mult))

            @block.tensor
            def _(pe):
                pe.wait_ge(step, 6)
                rows = g[:, 0:NT, :].rearrange("p t h -> p (t h)")
                pe.matmul(psum[:, 0, 0:N], core.const[:, C_UP, :], rows, start=True, stop=True)
                pe.matmul(psum[:, 1, 0:N], core.ones, rows, start=True, stop=True).then_inc(summed, 1)
                pe.wait_ge(step, 16)
                pe.matmul(psum[:, 2, :], core.ones[:NS, :], spread[:, :, :, :].rearrange("p a h b -> p (a h b)"), start=True, stop=True).then_inc(summed, 1)


def gdn_seq(core, F, cols, gout):
    nc = core.nc
    LV = LEVELS - 1

    def mask(j):
        return core.const[:, j:j + 1, :].to_broadcast([P, NT, P])

    def flat(tile):
        return tile[:, :, :].rearrange("p t c -> p (t c)")

    def col(kind, h):
        c = cols[:, kind, :].rearrange("p (t h) -> p t h", h=H)[:, :, ds(h, 1)]
        return c.to_broadcast([P, NT, P])

    with Marks(core, "seq", rowed=4, squared=4, staged=2, summed=2, rooted=4, diff=4, decay=4, masks=4, normed=10, signed=2,
               crossed=2, turned=2, products=4, scaled=6, seeded=4, flipped=2 * LV, flip_out=2 * LV, lmask=2 * LV, joined=2 * LV,
               joined_out=2 * LV, stepped=2 * LV, grown=2 * LV, wk=2, wk_out=2, u_made=2 * NT, u_out=2 * NT, s_made=2 * NT,
               state=2 * NT, o_made=2 * NT, stored=32, o_square=2, o_stat=6, o_root=2, o_norm=2, o_turned=2,
               gated=2) as s, ExitStack() as ctx:
        def two(name, shape=(P, NT, P)):
            return [core.sbuf(ctx, name, list(shape)) for _ in range(2)]

        gU, bI = two("gU"), two("bI")
        sqk, sqq, vT = two("sqk"), two("sqq"), two("vT")
        kT, qT, qdT = two("kT"), two("qT"), two("qdT")
        eG, dec, nA, qk = two("eG"), two("dec"), two("nA"), two("qk")
        Kb, kd, Vb, u = two("Kb"), two("kd"), two("Vb"), two("u")
        T, U, X = two("T"), two("U"), two("X")
        S = two("S", (P, NT + 1, P))
        st = two("st", (P, 3, NT))
        pA, pB, pC, pD = ([core.psum(ctx, n, [P, NT, P]) for _ in range(2)] for n in ("pA", "pB", "pC", "pD"))
        at = s.at

        with nc.Block() as block:
            @block.gpsimd
            def _(pool):
                with pool.Fori(0, H // 2) as i:
                    for a in range(2):
                        after(pool, at("joined", i, 0))
                        pool.tensor_tensor(gU[a][:, :, :], mask(C_UP), col(1, 2 * i + a), ALU.mult).then_inc(s["rowed"], 1)
                        pool.tensor_tensor(bI[a][:, :, :], mask(C_ID), col(0, 2 * i + a), ALU.mult).then_inc(s["rowed"], 1)
                    for a in range(2):
                        after(pool, at("decay", i, 2 * a + 2))
                        pool.tensor_tensor(dec[a][:, :, :], dec[a][:, :, :], mask(C_UP), ALU.mult).then_inc(s["masks"], 1)
                        after(pool, at("masks", i, 2 * a + 1), at("o_stat", i, 0))
                        pool.tensor_tensor(X[a][:, :, :], dec[a][:, :, :], mask(C_STRICT), ALU.mult).then_inc(s["masks"], 1)
                    for j in range(LV):
                        for a in range(2):
                            if j == 0:
                                after(pool, at("products", i, 2 * a + 1))
                            if j >= 2:
                                after(pool, at("joined", i, 2 * (j - 2) + a + 1))
                            pool.tensor_tensor((gU, bI)[j % 2][a][:, :, :], nA[a][:, :, :], mask(C_LEVEL + 1 + j), ALU.mult).then_inc(s["lmask"], 1)

            @block.scalar
            def _(act):
                with act.Fori(0, H // 2) as i:
                    for a in range(2):
                        h = 2 * i + a
                        after(act, at("normed", i, 0))
                        act.activation(flat(sqk[a]), part(F, h + H, SEQ), ACT.Square).then_inc(s["squared"], 1)
                        act.activation(flat(sqq[a]), part(F, h, SEQ), ACT.Square).then_inc(s["squared"], 1)
                        act.activation(flat(vT[a]), part(F, h + 2 * H, SEQ), ACT.Copy).then_inc(s["staged"], 1)
                    for a in range(2):
                        after(act, at("summed", i, a + 1))
                        act.activation(sqk[a][:, :, :], pC[a][:, :, :], ACT.Sqrt, bias=core.eps).then_inc(s["rooted"], 1)
                        act.activation(sqq[a][:, :, :], pD[a][:, :, :], ACT.Sqrt, bias=core.eps).then_inc(s["rooted"], 1)
                    for a in range(2):
                        after(act, at("diff", i, 2 * a + 2))
                        act.activation(eG[a][:, :, :], pA[a][:, :, :], ACT.Exp).then_inc(s["decay"], 1)
                        act.activation(dec[a][:, :, :], dec[a][:, :, :], ACT.Exp).then_inc(s["decay"], 1)
                    for j in range(LV):
                        for a in range(2):
                            after(act, at("flipped", i, 2 * j + a + 1))
                            act.activation(T[a][:, :, :], pC[a][:, :, :], ACT.Copy).then_inc(s["flip_out"], 1)
                        for a in range(2):
                            after(act, at("joined", i, 2 * j + a + 1))
                            act.activation(X[a][:, :, :], pA[a][:, :, :], ACT.Copy).then_inc(s["joined_out"], 1)
                    for a in range(2):
                        after(act, at("wk", i, a + 1))
                        act.activation(T[a][:, :, :], pA[a][:, :, :], ACT.Copy, scale=-1.0).then_inc(s["wk_out"], 1)
                    for a in range(2):
                        after(act, at("o_made", i, 2 * (NT - 1) + a + 1))
                        act.activation(X[a][:, :, :], pC[a][:, :, :], ACT.Square).then_inc(s["o_square"], 1)
                    for a in range(2):
                        after(act, at("o_stat", i, 3 * a + 2))
                        act.activation(st[a][:, 1, :], st[a][:, 1, :], ACT.Sqrt).then_inc(s["o_root"], 1)

            @block.tensor
            def _(pe):
                def each(out, lhs, rhs):
                    for t in range(NT):
                        last = pe.matmul(out[:, t, :], lhs[:, t, :], rhs[:, t, :], start=True, stop=True)
                    return last

                def turn(out, src):
                    for t in range(NT):
                        last = pe.transpose(out[:, t, :], src[:, t, :], core.ident)
                    return last

                with pe.Fori(0, H // 2) as i:
                    for a in range(2):
                        after(pe, at("rowed", i, 2 * a + 2), at("gated", i, 0), at("squared", i, 2 * a + 2))
                        pe.matmul(flat(pA[a]), core.ones, flat(gU[a]), start=True, stop=True)
                        pe.matmul(flat(pB[a]), core.ones, flat(bI[a]), start=True, stop=True)
                        pe.matmul(flat(pC[a]), core.ones, flat(sqk[a]), start=True, stop=True)
                        pe.matmul(flat(pD[a]), core.ones, flat(sqq[a]), start=True, stop=True).then_inc(s["summed"], 1)
                    for a in range(2):
                        after(pe, at("normed", i, 5 * a + 5))
                        each(pC[a], kT[a], kT[a])
                        each(pD[a], kT[a], qT[a]).then_inc(s["crossed"], 1)
                        turn(pA[a], kT[a])
                        after(pe, at("signed", i, a + 1), at("staged", i, a + 1))
                        turn(pB[a], vT[a]).then_inc(s["turned"], 1)
                    for j in range(LV):
                        for a in range(2):
                            after(pe, at("seeded", i, 2 * a + 2) if j == 0 else at("grown", i, 2 * (j - 1) + a + 1))
                            turn(pC[a], U[a]).then_inc(s["flipped"], 1)
                        for a in range(2):
                            after(pe, at("flip_out", i, 2 * j + a + 1), at("lmask", i, 2 * j + a + 1))
                            if j == 0:
                                after(pe, at("scaled", i, 3 * a + 3))
                            each(pA[a], (gU, bI)[j % 2][a], T[a]).then_inc(s["joined"], 1)
                        for a in range(2):
                            after(pe, at("joined_out", i, 2 * j + a + 1))
                            each(pB[a], X[a], U[a]).then_inc(s["stepped"], 1)
                    for a in range(2):
                        after(pe, at("grown", i, 2 * (LV - 1) + a + 1))
                        each(pA[a], Kb[a], U[a]).then_inc(s["wk"], 1)
                    for t in range(NT):
                        for a in range(2):
                            if t:
                                after(pe, at("state", i, 2 * (t - 1) + a + 1), at("wk_out", i, a + 1))
                            last = pe.matmul(pB[a][:, t, :], U[a][:, t, :], Vb[a][:, t, :], start=True, stop=t == 0)
                            if t:
                                last = pe.matmul(pB[a][:, t, :], T[a][:, t, :], S[a][:, t, :], start=False, stop=True)
                            last.then_inc(s["u_made"], 1)
                        for a in range(2):
                            after(pe, at("u_out", i, 2 * t + a + 1))
                            pe.matmul(pD[a][:, t, :], kd[a][:, t, :], u[a][:, t, :], start=True, stop=True).then_inc(s["s_made"], 1)
                        for a in range(2):
                            if t:
                                pe.matmul(pC[a][:, t, :], qdT[a][:, t, :], S[a][:, t, :], start=True, stop=False)
                            pe.matmul(pC[a][:, t, :], qk[a][:, t, :], u[a][:, t, :], start=t == 0, stop=True).then_inc(s["o_made"], 1)
                    for a in range(2):
                        after(pe, at("o_norm", i, a + 1))
                        turn(pA[a], kT[a]).then_inc(s["o_turned"], 1)

            @block.vector
            def _(dve):
                with dve.Fori(0, H // 2) as i:
                    for a in range(2):
                        h = 2 * i + a
                        after(dve, at("summed", i, a + 1), at("products", i, 0))
                        dve.tensor_tensor(dec[a][:, :, :], pA[a][:, :, :], col(2, h), ALU.min).then_inc(s["diff"], 1)
                        after(dve, at("diff", i, 2 * a + 1))
                        dve.tensor_tensor(dec[a][:, :, :], dec[a][:, :, :], col(2, h), ALU.subtract).then_inc(s["diff"], 1)
                    for a in range(2):
                        h = 2 * i + a
                        after(dve, at("rooted", i, 2 * a + 1))
                        dve.reciprocal(flat(sqk[a]), flat(sqk[a])).then_inc(s["normed"], 1)
                        after(dve, at("normed", i, 5 * a + 1), at("o_turned", i, 0))
                        dve.tensor_tensor(flat(kT[a]), part(F, h + H, SEQ), flat(sqk[a]), ALU.mult).then_inc(s["normed"], 1)
                        after(dve, at("rooted", i, 2 * a + 2))
                        dve.reciprocal(flat(sqq[a]), flat(sqq[a])).then_inc(s["normed"], 1)
                        after(dve, at("normed", i, 5 * a + 3))
                        dve.scalar_tensor_tensor(flat(qT[a]), part(F, h, SEQ), HD ** -0.5, flat(sqq[a]), ALU.mult, ALU.mult).then_inc(s["normed"], 1)
                        after(dve, at("normed", i, 5 * a + 4), at("decay", i, 2 * a + 1))
                        dve.tensor_tensor(qdT[a][:, :, :], qT[a][:, :, :], eG[a][:, :, :], ALU.mult).then_inc(s["normed"], 1)
                        after(dve, at("masks", i, 2 * a + 2))
                        dve.scalar_tensor_tensor(flat(nA[a]), flat(pB[a]), -1.0, flat(X[a]), ALU.mult, ALU.mult).then_inc(s["signed"], 1)
                    for a in range(2):
                        h = 2 * i + a
                        after(dve, at("crossed", i, a + 1), at("signed", i, a + 1))
                        dve.tensor_tensor(nA[a][:, :, :], pC[a][:, :, :], nA[a][:, :, :], ALU.mult).then_inc(s["products"], 1)
                        dve.tensor_tensor(qk[a][:, :, :], pD[a][:, :, :], dec[a][:, :, :], ALU.mult).then_inc(s["products"], 1)
                        after(dve, at("products", i, 2 * a + 1))
                        dve.tensor_tensor(U[a][:, :, :], nA[a][:, :, :], mask(C_LEVEL), ALU.mult).then_inc(s["seeded"], 1)
                        after(dve, at("seeded", i, 2 * a + 1))
                        dve.tensor_tensor(U[a][:, :, :], U[a][:, :, :], mask(C_ID), ALU.add).then_inc(s["seeded"], 1)
                        after(dve, at("turned", i, a + 1))
                        dve.tensor_tensor(Kb[a][:, :, :], pA[a][:, :, :], col(3, h), ALU.mult).then_inc(s["scaled"], 1)
                        dve.tensor_tensor(kd[a][:, :, :], pA[a][:, :, :], col(4, h), ALU.mult).then_inc(s["scaled"], 1)
                        dve.tensor_tensor(Vb[a][:, :, :], pB[a][:, :, :], col(0, h), ALU.mult).then_inc(s["scaled"], 1)
                    for j in range(LV):
                        for a in range(2):
                            after(dve, at("stepped", i, 2 * j + a + 1))
                            dve.tensor_tensor(U[a][:, :, :], pB[a][:, :, :], U[a][:, :, :], ALU.add).then_inc(s["grown"], 1)
                    for t in range(NT):
                        for a in range(2):
                            after(dve, at("u_made", i, 2 * t + a + 1))
                            dve.tensor_copy(u[a][:, t, :], pB[a][:, t, :]).then_inc(s["u_out"], 1)
                        for a in range(2):
                            after(dve, at("s_made", i, 2 * t + a + 1), at("stored", i, 0))
                            if t == 0:
                                dve.tensor_copy(S[a][:, 1, :], pD[a][:, 0, :]).then_inc(s["state"], 1)
                            else:
                                after(dve, at("state", i, 2 * (t - 1) + a + 1))
                                dve.scalar_tensor_tensor(S[a][:, t + 1, :], S[a][:, t, :], part(cols, 2 * i + a + (5 * NT * H + t * H), 1),
                                                         pD[a][:, t, :], ALU.mult, ALU.add).then_inc(s["state"], 1)
                    for a in range(2):
                        after(dve, at("o_square", i, a + 1))
                        dve.tensor_reduce(st[a][:, 0, :], X[a][:, :, :], AX.X, ALU.add).then_inc(s["o_stat"], 1)
                        after(dve, at("o_stat", i, 3 * a + 1))
                        dve.tensor_scalar(st[a][:, 1, :], st[a][:, 0, :], 1.0 / HD, EPS, ALU.mult, ALU.add).then_inc(s["o_stat"], 1)
                        after(dve, at("o_root", i, a + 1))
                        dve.reciprocal(st[a][:, 2, :], st[a][:, 1, :]).then_inc(s["o_stat"], 1)
                        after(dve, at("o_stat", i, 3 * a + 3))
                        dve.tensor_tensor(kT[a][:, :, :], pC[a][:, :, :],
                                          st[a][:, 2, :].rearrange("p (t o) -> p t o", o=1).to_broadcast([P, NT, P]), ALU.mult).then_inc(s["o_norm"], 1)
                    for a in range(2):
                        h = 2 * i + a
                        after(dve, at("o_turned", i, a + 1))
                        dve.scalar_tensor_tensor(part(F, h, SEQ), flat(pA[a]), gout[:, 0:1], part(F, h + 3 * H, SEQ), ALU.mult, ALU.mult).then_inc(s["gated"], 1)

            @block.sync
            def _(sp):
                with sp.Fori(0, H // 2) as i:
                    for a in range(2):
                        after(sp, at("state", i, 2 * (NT - 1) + a + 1))
                        sp.dma_start(core.o["ssm_p"][ds(2 * i + a, 1), :, :].rearrange("o k v -> (o k) v"), S[a][:, NT, :]).then_inc(s["stored"], 16)
                sp.wait_ge(s["stored"], 16 * H)


def gdn_dec(core, Fs, srep, gout, os):
    nc = core.nc
    G, N = 4, H * NS
    with Marks(core, "dec", square=3, sums=2, root=2, prep=7, spread=4, state=1, landed0=16, landed1=16, u_made=2, tmp=6,
               o_made=2, o_out=2, stored=32, post=6) as s, ExitStack() as ctx:
        at = s.at
        q = core.sbuf(ctx, "q", [P, N])
        k = core.sbuf(ctx, "k", [P, N])
        nkb = core.sbuf(ctx, "nkb", [P, N])
        bv = core.sbuf(ctx, "bv", [P, N])
        sq = core.sbuf(ctx, "sq", [P, 2 * N])
        o = core.sbuf(ctx, "o", [P, N])
        S0 = [core.sbuf(ctx, "S0", [P, G, P]) for _ in range(2)]
        S1 = [core.sbuf(ctx, "S1", [P, G, P]) for _ in range(2)]
        t1 = [core.sbuf(ctx, "t1", [P, G, P]) for _ in range(2)]
        nkB = [core.sbuf(ctx, "nkB", [P, G, P]) for _ in range(2)]
        bvB = [core.sbuf(ctx, "bvB", [P, G, P]) for _ in range(2)]
        pS = core.psum(ctx, "pS", [P, 2 * N])
        pU = [core.psum(ctx, "pU", [P, G, P]) for _ in range(2)]
        pO = [core.psum(ctx, "pO", [P, G]) for _ in range(2)]
        f = Fs[:, :, :].rearrange("p c b -> p (c b)")

        def wide(tile, g):
            return part(tile, g, G).rearrange("p (j o) -> p j o", o=1).to_broadcast([P, G, P])

        with nc.Block() as block:
            @block.sync
            def _(sp):
                with sp.Fori(0, N // G // 2) as i:
                    for a in range(2):
                        after(sp, at("tmp", i, 0))
                        sp.dma_start(S0[a][:, :, :], core.i["state_ssm"][ds((2 * i + a) * G, G), :, :].rearrange("j k v -> k j v")).then_inc(s[f"landed{a}"], 16)
                    for a in range(2):
                        after(sp, at("tmp", i, 3 * a + 3))
                        sp.dma_start(core.o["ssm_s"][ds((2 * i + a) * G, G), :, :].rearrange("j k v -> k j v"), S1[a][:, :, :]).then_inc(s["stored"], 16)
                sp.wait_ge(s["stored"], 16 * (N // G))

            @block.gpsimd
            def _(pool):
                pool.wait_ge(s["prep"], 5)
                with pool.Fori(0, N // G // 2) as i:
                    for a in range(2):
                        after(pool, at("u_made", i, 0))
                        pool.tensor_copy(nkB[a][:, :, :], wide(nkb, 2 * i + a)).then_inc(s["spread"], 1)
                        pool.tensor_copy(bvB[a][:, :, :], wide(bv, 2 * i + a)).then_inc(s["spread"], 1)

            @block.scalar
            def _(act):
                act.activation(sq[:, :], f[:, 0:2 * N], ACT.Square).then_inc(s["square"], 1)
                act.wait_ge(s["sums"], 1)
                act.activation(sq[:, :], pS[:, :], ACT.Sqrt, bias=core.eps).then_inc(s["root"], 1)
                with act.Fori(0, N // G // 2) as i:
                    for a in range(2):
                        after(act, at("o_made", i, a + 1))
                        act.activation(part(o, 2 * i + a, G), pO[a][:, :], ACT.Copy).then_inc(s["o_out"], 1)
                act.wait_ge(s["o_out"], N // G)
                act.activation(sq[:, 0:N], o[:, :], ACT.Square).then_inc(s["square"], 1)
                act.wait_ge(s["post"], 1)
                act.activation(sq[:, 0:N], sq[:, 0:N], ACT.Sqrt).then_inc(s["root"], 1)

            @block.tensor
            def _(pe):
                pe.wait_ge(s["square"], 1)
                pe.matmul(pS[:, :], core.ones, sq[:, :], start=True, stop=True).then_inc(s["sums"], 1)
                pe.wait_ge(s["prep"], 5)
                with pe.Fori(0, N // G // 2) as i:
                    for a in range(2):
                        after(pe, (s[f"landed{a}"], i * 16 + 16), at("spread", i, 2 * a + 2), at("tmp", i, 0))
                        for j in range(G):
                            pe.matmul(pU[a][:, j, :], nkB[a][:, j, :], S0[a][:, j, :], start=True, stop=False)
                            last = pe.matmul(pU[a][:, j, :], bvB[a][:, j, :], core.ident, start=False, stop=True)
                        last.then_inc(s["u_made"], 1)
                    for a in range(2):
                        after(pe, at("tmp", i, 3 * a + 3), at("o_out", i, 0))
                        for j in range(G):
                            last = pe.matmul(pO[a][:, j:j + 1], S1[a][:, j, :], q[:, ds((2 * i + a) * G + j, 1)], start=True, stop=True)
                        last.then_inc(s["o_made"], 1)
                pe.wait_ge(s["square"], 2)
                pe.matmul(pS[:, 0:N], core.ones, sq[:, 0:N], start=True, stop=True).then_inc(s["sums"], 1)

            @block.vector
            def _(dve):
                dve.wait_ge(s["root"], 1)
                dve.reciprocal(sq[:, :], sq[:, :]).then_inc(s["prep"], 1)
                dve.wait_ge(s["prep"], 1)
                dve.scalar_tensor_tensor(q[:, :], f[:, 0:N], HD ** -0.5, sq[:, 0:N], ALU.mult, ALU.mult).then_inc(s["prep"], 1)
                dve.tensor_tensor(k[:, :], f[:, N:2 * N], sq[:, N:2 * N], ALU.mult).then_inc(s["prep"], 1)
                dve.wait_ge(s["prep"], 3)
                dve.scalar_tensor_tensor(nkb[:, :], k[:, :], -1.0, srep[:, 2, :], ALU.mult, ALU.mult).then_inc(s["prep"], 1)
                dve.tensor_tensor(bv[:, :], f[:, 2 * N:3 * N], srep[:, 0, :], ALU.mult).then_inc(s["prep"], 1)
                with dve.Fori(0, N // G // 2) as i:
                    for a in range(2):
                        g = 2 * i + a
                        after(dve, at("u_made", i, a + 1), at("stored", i, 0), at("o_made", i, 0))
                        dve.tensor_tensor(t1[a][:, :, :], pU[a][:, :, :], wide(k, g), ALU.mult).then_inc(s["tmp"], 1)
                        dve.tensor_tensor(S1[a][:, :, :], S0[a][:, :, :],
                                          srep[:, 1, :][:, ds(g * G, G)].rearrange("p (j o) -> p j o", o=1).to_broadcast([P, G, P]), ALU.mult).then_inc(s["tmp"], 1)
                        after(dve, at("tmp", i, 3 * a + 2))
                        dve.tensor_tensor(S1[a][:, :, :], S1[a][:, :, :], t1[a][:, :, :], ALU.add).then_inc(s["tmp"], 1)
                dve.wait_ge(s["sums"], 2)
                dve.tensor_scalar(sq[:, 0:N], pS[:, 0:N], 1.0 / HD, EPS, ALU.mult, ALU.add).then_inc(s["post"], 1)
                dve.wait_ge(s["root"], 2)
                dve.reciprocal(sq[:, 0:N], sq[:, 0:N]).then_inc(s["post"], 1)
                dve.wait_ge(s["post"], 2)
                dve.tensor_tensor(o[:, :], o[:, :], sq[:, 0:N], ALU.mult).then_inc(s["post"], 1)
                dve.wait_ge(s["post"], 3)
                dve.scalar_tensor_tensor(os[:, :], o[:, :], gout[:, 0:1], f[:, 3 * N:4 * N], ALU.mult, ALU.mult).then_inc(s["post"], 1)


def out_proj(core, rows, weight):
    nc = core.nc
    HALF = D // 2
    B = 4
    with Marks(core, "out", landed0=16, landed1=16, made=1, added=1) as s, ExitStack() as ctx:
        w = core.sbuf(ctx, "w", [P, KD, D])
        bank = [core.psum(ctx, "bank", [P, HALF]) for _ in range(B)]
        with nc.Block() as block:
            @block.sync
            def _(sp):
                for c in range(2):
                    sp.dma_start(w[:, :, HALF * c:HALF * c + HALF], weight.rearrange("(k p) n -> p k n", p=P)[:, :, HALF * c:HALF * c + HALF]).then_inc(s[f"landed{c}"], 16)

            @block.tensor
            def _(pe):
                for c in range(2):
                    pe.wait_ge(s[f"landed{c}"], 16)
                    for t in range(NT + 1):
                        j = c * (NT + 1) + t
                        n = P if t < NT else NS
                        if j >= B:
                            pe.wait_ge(s["added"], j - B + 1)
                        for k in range(KD):
                            last = pe.matmul(bank[j % B][:n, :], rows(k, t), w[:, k, HALF * c:HALF * c + HALF], start=k == 0, stop=k == KD - 1)
                        last.then_inc(s["made"], 1)

            @block.vector
            def _(dve):
                for c in range(2):
                    for t in range(NT + 1):
                        j = c * (NT + 1) + t
                        x, n = rows_of(core, t)
                        x = x[:, HALF * c:HALF * c + HALF]
                        dve.wait_ge(s["made"], j + 1)
                        dve.tensor_tensor(x, bank[j % B][:n, :], x, ALU.add).then_inc(s["added"], 1)


def peer_q(core, xnT, weight, qT, qTs):
    nc = core.nc
    W = 4
    SIDES = 2 * H
    with Marks(core, "pq", **{f"landed{c}": 16 for c in range(W)}, made=W, out=W, sout=W) as s, ExitStack() as ctx:
        w = core.sbuf(ctx, "w", [P, W, KD, P])
        acc = [core.psum(ctx, "acc", [P, NT, P]) for _ in range(W)]
        accs = [core.psum(ctx, "accs", [P, NS]) for _ in range(W)]
        with nc.Block() as block:
            @block.sync
            def _(sp):
                for c in range(W):
                    sp.dma_start(w[:, c, :, :], weight[c]).then_inc(s[f"landed{c}"], 16)
                with sp.Fori(1, SIDES // W) as i:
                    for c in range(W):
                        after(sp, s.at("made", i, c - W + 1))
                        sp.dma_start(w[:, c, :, :], weight[ds(i * W + c, 1), :, :, :].rearrange("o p k n -> (o p) k n")).then_inc(s[f"landed{c}"], 16)

            @block.tensor
            def _(pe):
                with pe.Fori(0, SIDES // W) as i:
                    for c in range(W):
                        after(pe, (s[f"landed{c}"], (i + 1) * 16), s.at("out", i, 0), s.at("sout", i, 0))
                        for k in range(KD):
                            pe.matmul(acc[c][:, :, :].rearrange("p t r -> p (t r)"), w[:, c, k, :], xnT[:, k, 0:SEQ], start=k == 0, stop=k == KD - 1)
                        for k in range(KD):
                            last = pe.matmul(accs[c][:, :], w[:, c, k, :], xnT[:, k, SEQ:ROWS], start=k == 0, stop=k == KD - 1)
                        last.then_inc(s["made"], 1)

            @block.scalar
            def _(act):
                with act.Fori(0, SIDES // W) as i:
                    for c in range(W):
                        after(act, s.at("made", i, c + 1))
                        act.activation(qT[:, :, ds(i * W + c, 1), :].rearrange("p t o r -> p t (o r)"), acc[c][:, :, :], ACT.Copy).then_inc(s["out"], 1)

            @block.vector
            def _(dve):
                with dve.Fori(0, SIDES // W) as i:
                    for c in range(W):
                        after(dve, s.at("made", i, c + 1))
                        dve.tensor_copy(part(qTs, i * W + c, NS), accs[c][:, :]).then_inc(s["sout"], 1)


TOP_STEPS = 27


class TopK:

    def __init__(self, core, ctx, n):
        sb = core.sbuf
        self.n = n
        self.sv = sb(ctx, "sv", [n, 2, TOPK])
        self.si = sb(ctx, "si", [n, 2, TOPK], U32)
        self.sif = sb(ctx, "sif", [n, 2, TOPK])
        self.rest = sb(ctx, "rest", [n, 2, NK])
        self.cand = sb(ctx, "cand", [n, TOPK, TOPK])
        self.crest = sb(ctx, "crest", [n, TOPK, TOPK])
        self.tv = sb(ctx, "tv", [n, TOPK])
        self.ti = sb(ctx, "ti", [n, TOPK], U32)
        self.tab = sb(ctx, "tab", [n, 2, TOPK], U32)
        self.tabf = sb(ctx, "tabf", [n, 2, TOPK])
        self.hit = sb(ctx, "hit", [n, 2, TOPK, TOPK])
        self.pick = sb(ctx, "pick", [n, 2, TOPK])
        self.low = sb(ctx, "low", [n, 1])
        self.e = sb(ctx, "e", [n, TOPK])
        self.z = sb(ctx, "z", [n, 2])


def top_k(dve, s, name, v, k, scores, counting, index):
    n = k.n
    done = [0]

    def step(ins):
        ins.then_inc(s[name], 1)
        done[0] += 1

    def then(ins):
        step(ins)
        apart(dve, s.at(name, v, done[0]))

    def best(lots):
        for values, numbers, data, rest in lots:
            last = dve.max(values[:, 0:8], data)
            (then if data is lots[-1][2] else step)(last)
        for values, numbers, data, rest in lots:
            step(dve.max_index(numbers[:, 0:8], values[:, 0:8], data))
        for values, numbers, data, rest in lots:
            last = dve.match_replace(rest, values[:, 0:8], data, -3.0e38)
            (then if data is lots[-1][2] else step)(last)
        for values, numbers, data, rest in lots:
            last = dve.max(values[:, 8:16], rest)
            (then if data is lots[-1][2] else step)(last)
        for values, numbers, data, rest in lots:
            last = dve.max_index(numbers[:, 8:16], values[:, 8:16], rest)
            (then if data is lots[-1][2] else step)(last)

    def wide(col):
        return col.rearrange("p (a o) -> p a o", o=1).to_broadcast([n, TOPK, TOPK])

    best([(k.sv[:, p, :], k.si[:, p, :], scores[:n, p, :], k.rest[:, p, :]) for p in range(2)])
    step(dve.tensor_copy(k.sif[:, :, :], k.si[:, :, :]))
    then(dve.tensor_tensor(k.cand[:, :, :], wide(k.sv[:, 0, :]), k.sv[:, 1:2, :].to_broadcast([n, TOPK, TOPK]), ALU.add))
    best([(k.tv[:, :], k.ti[:, :], k.cand[:, :, :].rearrange("p a b -> p (a b)"), k.crest[:, :, :].rearrange("p a b -> p (a b)"))])
    step(dve.tensor_scalar(k.low[:, :], k.tv[:, 0:1], -1.0, None, ALU.mult))
    assert done[0] == TOP_LOW
    step(dve.tensor_scalar(k.tab[:, 0, :], k.ti[:, :], 4, None, ALU.logical_shift_right))
    then(dve.tensor_scalar(k.tab[:, 1, :], k.ti[:, :], TOPK - 1, None, ALU.bitwise_and))
    then(dve.tensor_copy(k.tabf[:, :, :], k.tab[:, :, :]))
    for p in range(2):
        last = dve.tensor_tensor(k.hit[:, p, :, :], wide(k.tabf[:, p, :]),
                                 counting[:n, :].rearrange("p (o b) -> p o b", o=1).to_broadcast([n, TOPK, TOPK]), ALU.is_equal)
        (then if p else step)(last)
    for p in range(2):
        last = dve.tensor_tensor(k.hit[:, p, :, :], k.hit[:, p, :, :], k.sif[:, p:p + 1, :].to_broadcast([n, TOPK, TOPK]), ALU.mult)
        (then if p else step)(last)
    then(dve.tensor_reduce(k.pick[:, :, :], k.hit[:, :, :, :], AX.X, ALU.add))
    step(dve.scalar_tensor_tensor(index, k.pick[:, 0, :], float(NK), k.pick[:, 1, :], ALU.mult, ALU.add))
    assert done[0] == TOP_STEPS, done[0]


TOP_LOW = 18


def peer(core, xn, xns, qT, qTs, keys, uv):
    nc = core.nc
    HALF = D // 2
    GRPS = TOPK // 4
    UNITS = NT * H
    with Marks(core, "peer", inp=48, staged=1, scored=1, top=TOP_STEPS, exped=1, gate=2, dot=TOPK, gelu=GRPS, acted=GRPS,
               diag=TOPK, pv=TOPK, added=1, sstaged=1, sscored=1, stop=TOP_STEPS, sexped=1, sgate=2, flip=1, flipped=2,
               rowed=1, sdot=1, sgelu=1, sact=2, spv=1, sadded=1,
               **{f"landed{r}": 32 for r in range(RING)}) as s, ExitStack() as ctx:
        at = s.at
        sk = core.sbuf(ctx, "sk", [P, 2 * H, NK])
        counting = core.sbuf(ctx, "counting", [P, TOPK])
        same = core.sbuf(ctx, "same", [P, NS, NS])
        ring = core.sbuf(ctx, "ring", [P, RING, 2 * D])
        qs = [core.sbuf(ctx, "qs", [P, 2, P]) for _ in range(2)]
        k = TopK(core, ctx, P)
        idx = [core.sbuf(ctx, "idx", [P, TOPK], U32) for _ in range(2)]
        gate = [core.sbuf(ctx, "gate", [P, TOPK]) for _ in range(2)]
        hs = [core.sbuf(ctx, "hs", [P, TOPK]) for _ in range(2)]
        hg = [core.sbuf(ctx, "hg", [P, TOPK]) for _ in range(2)]
        ac = [core.sbuf(ctx, "ac", [P, TOPK]) for _ in range(2)]
        diag = core.sbuf(ctx, "diag", [P, RING, P])
        qss = core.sbuf(ctx, "qss", [P, 2, NS])
        ks = TopK(core, ctx, NS)
        sidx = core.sbuf(ctx, "sidx", [NS, H * TOPK])
        sgate = core.sbuf(ctx, "sgate", [NS, H * TOPK])
        sidxT = core.sbuf(ctx, "sidxT", [P, NS], U32)
        sgateT = core.sbuf(ctx, "sgateT", [P, NS])
        shs = core.sbuf(ctx, "shs", [P, 3, NS])
        sac = core.sbuf(ctx, "sac", [P, NS, NS])
        pS = core.psum(ctx, "pS", [P, 2, NK])
        pT = core.psum(ctx, "pT", [P, 2, NK])
        po = [core.psum(ctx, "po", [P, D]) for _ in range(2)]

        def turns(eng, unit):
            unit(0, 0, None, True)
            for first, last in ((0, H), (H, UNITS // 2 - 1)):
                with eng.Fori(first, last) as i:
                    unit(2 * i + 1, 1, i if last == H else None, True)
                    unit(2 * i + 2, 0, None, True)
            unit(UNITS - 1, 1, None, False)

        with nc.Block() as block:
            @block.sync
            def _(sp):
                sp.dma_start(sk[:, :, :], keys).then_inc(s["inp"], 16)
                sp.dma_start(counting[:, :], core.i["counting"]).then_inc(s["inp"], 16)
                sp.dma_start(same[:, :, :], core.i["same"]).then_inc(s["inp"], 16)

            @block.gpsimd
            def _(pool):
                def gathers(u, a, e):
                    apart(pool, at("top", u, TOP_STEPS))
                    for j in range(RING):
                        if e or not isinstance(u, int) or u:
                            apart(pool, at("pv", u, RING * e + j - RING + 1))
                        c = RING * e + j
                        pool.indirect_dma_start(out=ring[:, j, :], out_offset=None, in_=uv,
                                                in_offset=bass.IndirectOffsetOnAxis(ap=idx[a][:, c:c + 1], axis=0)).then_inc(s[f"landed{j}"], 16)

                def unit(u, a, head, more):
                    gathers(u, a, 0)
                    gathers(u, a, 1)

                turns(pool, unit)
                pool.wait_ge(s["flipped"], 2)
                for j in range(NS):
                    pool.wait_ge(s["pv"], UNITS * TOPK - RING + j + 1)
                    pool.indirect_dma_start(out=ring[:, j, :], out_offset=None, in_=uv,
                                            in_offset=bass.IndirectOffsetOnAxis(ap=sidxT[:, j:j + 1], axis=0)).then_inc(s[f"landed{j}"], 16)

            @block.scalar
            def _(act):
                def stage(v, a):
                    if not isinstance(v, int):
                        apart(act, at("scored", v - 1, 0))
                    act.activation(qs[a][:, :, :].rearrange("p a r -> p (a r)"), part(qT, v, 2 * P), ACT.Copy).then_inc(s["staged"], 1)

                def weigh(v):
                    after(act, at("top", v, TOP_LOW))
                    if not isinstance(v, int):
                        after(act, at("gate", v, 0))
                    act.activation(k.e[:, :], k.tv[:, :], ACT.Exp, bias=k.low[:, 0:1], accum_out=k.z[:, 0:1]).then_inc(s["exped"], 1)

                stage(0, 0)
                weigh(0)

                def unit(u, a, head, more):
                    if more:
                        stage(u + 1, 1 - a)
                    if head is not None:
                        apart(act, at("sscored", head, 0))
                        act.activation(qss[:, :, :].rearrange("p a r -> p (a r)"), part(qTs, head, 2 * NS), ACT.Copy).then_inc(s["sstaged"], 1)
                    for g in range(GRPS):
                        after(act, at("dot", u, 4 * g + 4))
                        act.activation(hg[a][:, 4 * g:4 * g + 4], hs[a][:, 4 * g:4 * g + 4], ACT.Gelu).then_inc(s["gelu"], 1)
                        after(act, at("acted", u, g + 1))
                        for c in range(4 * g, 4 * g + 4):
                            act.activation(diag[:, c % RING, :], core.ident, ACT.Copy, scale=ac[a][:, c:c + 1]).then_inc(s["diag"], 1)
                        if g == 0 and more:
                            weigh(u + 1)
                        if g == 1 and head is not None:
                            after(act, at("stop", head, TOP_LOW))
                            act.activation(ks.e[:, :], ks.tv[:, :], ACT.Exp, bias=ks.low[:, 0:1], accum_out=ks.z[:, 0:1]).then_inc(s["sexped"], 1)

                turns(act, unit)
                act.wait_ge(s["sdot"], NS)
                act.activation(shs[:, 1, :], shs[:, 0, :], ACT.Gelu).then_inc(s["sgelu"], 1)

            @block.vector
            def _(dve):
                def weighed(v, b):
                    after(dve, at("exped", v, 1))
                    dve.reciprocal(k.z[:, 1:2], k.z[:, 0:1]).then_inc(s["gate"], 1)
                    after(dve, at("gate", v, 1))
                    dve.tensor_scalar(gate[b][:, :], k.e[:, :], k.z[:, 1:2], None, ALU.mult).then_inc(s["gate"], 1)

                dve.wait_ge(s["inp"], 48)
                dve.wait_ge(s["scored"], 1)
                top_k(dve, s, "top", 0, k, pS, counting, idx[0][:, :])
                weighed(0, 0)

                def add(u, b):
                    x = part(core.x, u // H, D)
                    dve.tensor_tensor(x, po[b][:, :], x, ALU.add).then_inc(s["added"], 1)

                def unit(u, a, head, more):
                    rows = part(xn, u // H, D)
                    for g in range(GRPS):
                        for c in range(4 * g, 4 * g + 4):
                            after(dve, at(f"landed{c % RING}", u, 16 * (c // RING + 1)))
                            dve.scalar_tensor_tensor(ring[:, c % RING, 0:D], ring[:, c % RING, 0:D], 1.0, rows,
                                                     ALU.mult, ALU.mult, accum_out=hs[a][:, c:c + 1]).then_inc(s["dot"], 1)
                        after(dve, at("gelu", u, g + 1), at("gate", u, 2))
                        dve.tensor_tensor(ac[a][:, 4 * g:4 * g + 4], hg[a][:, 4 * g:4 * g + 4], gate[a][:, 4 * g:4 * g + 4], ALU.mult).then_inc(s["acted"], 1)
                        if g == 0:
                            if more:
                                apart(dve, at("scored", u + 1, 1))
                                top_k(dve, s, "top", u + 1, k, pS, counting, idx[1 - a][:, :])
                        if g == 1:
                            if more:
                                weighed(u + 1, 1 - a)
                            if not isinstance(u, int) or u:
                                after(dve, at("pv", u - 1, TOPK))
                                add(u - 1, 1 - a)
                            if head is not None:
                                apart(dve, at("sscored", head, 1))
                                top_k(dve, s, "stop", head, ks, pT, counting, part(sidx, head, TOPK))
                        if g == 2 and head is not None:
                            after(dve, at("sexped", head, 1))
                            dve.reciprocal(ks.z[:, 1:2], ks.z[:, 0:1]).then_inc(s["sgate"], 1)
                            after(dve, at("sgate", head, 1))
                            dve.tensor_scalar(part(sgate, head, TOPK), ks.e[:, :], ks.z[:, 1:2], None, ALU.mult).then_inc(s["sgate"], 1)

                turns(dve, unit)
                dve.wait_ge(s["pv"], UNITS * TOPK)
                add(UNITS - 1, 1)
                dve.wait_ge(s["flip"], 1)
                dve.tensor_copy(sidxT[:, :], pT[:, 0, 0:NS]).then_inc(s["flipped"], 1)
                dve.tensor_copy(sgateT[:, :], pT[:, 1, 0:NS]).then_inc(s["flipped"], 1)
                for b in range(NS):
                    dve.wait_ge(s["rowed"], b + 1)
                    dve.wait_ge(s[f"landed{b}"], 32 * UNITS + 16)
                    dve.scalar_tensor_tensor(ring[:, b, 0:D], ring[:, b, 0:D], 1.0, po[b % 2][:, :], ALU.mult, ALU.mult,
                                             accum_out=shs[:, 0, b:b + 1]).then_inc(s["sdot"], 1)
                dve.wait_ge(s["sgelu"], 1)
                dve.wait_ge(s["flipped"], 2)
                dve.tensor_tensor(shs[:, 2, :], shs[:, 1, :], sgateT[:, :], ALU.mult).then_inc(s["sact"], 1)
                dve.wait_ge(s["sact"], 1)
                dve.tensor_tensor(sac[:, :, :], same[:, :, :], shs[:, 2, :].rearrange("p (b o) -> p b o", o=1).to_broadcast([P, NS, NS]), ALU.mult).then_inc(s["sact"], 1)
                dve.wait_ge(s["spv"], 1)
                dve.tensor_tensor(core.xs[:, :], po[0][:NS, :], core.xs[:, :], ALU.add).then_inc(s["sadded"], 1)

            @block.tensor
            def _(pe):
                def score(v, a):
                    after(pe, at("staged", v, 1))
                    if not isinstance(v, int):
                        after(pe, at("top", v, 0))
                    for p in range(2):
                        last = pe.matmul(pS[:, p, :], qs[a][:, p, :], sk[:, :, :].rearrange("p s n -> p (s n)")[:, ds((v % H) * (2 * NK) + p * NK, NK)], start=True, stop=True)
                    last.then_inc(s["scored"], 1)

                pe.wait_ge(s["inp"], 48)
                score(0, 0)

                def unit(u, a, head, more):
                    if not isinstance(u, int) or u >= 2:
                        after(pe, at("added", u - 1, 0))
                    for c in range(TOPK):
                        after(pe, at("diag", u, c + 1))
                        for e in range(2):
                            last = pe.matmul(po[a][:, HALF * e:HALF * e + HALF], diag[:, c % RING, :], ring[:, c % RING, D + HALF * e:D + HALF * e + HALF],
                                             start=c == 0, stop=c == TOPK - 1)
                        last.then_inc(s["pv"], 1)
                        if c == 0 and more:
                            score(u + 1, 1 - a)
                        if c == 1 and head is not None:
                            after(pe, at("sstaged", head, 1), at("stop", head, 0))
                            for p in range(2):
                                last = pe.matmul(pT[:NS, p, :], qss[:, p, :], sk[:, :, :].rearrange("p s n -> p (s n)")[:, ds(head * (2 * NK) + p * NK, NK)], start=True, stop=True)
                            last.then_inc(s["sscored"], 1)

                turns(pe, unit)
                pe.wait_ge(s["sgate"], 2 * H)
                pe.transpose(pT[:, 0, 0:NS], sidx[:, :], core.const[:NS, C_ID, 0:NS])
                pe.transpose(pT[:, 1, 0:NS], sgate[:, :], core.const[:NS, C_ID, 0:NS]).then_inc(s["flip"], 1)
                pe.wait_ge(s["added"], UNITS)
                for b in range(NS):
                    if b >= 2:
                        pe.wait_ge(s["sdot"], b - 1)
                    for e in range(2):
                        last = pe.matmul(po[b % 2][:, HALF * e:HALF * e + HALF], core.const[:NS, C_ID, b:b + 1].to_broadcast([NS, P]),
                                         xns[:, HALF * e:HALF * e + HALF], start=True, stop=True)
                    last.then_inc(s["rowed"], 1)
                pe.wait_ge(s["sact"], 2)
                for e in range(2):
                    for b in range(NS):
                        last = pe.matmul(po[0][:NS, HALF * e:HALF * e + HALF], sac[:, b, :], ring[:, b, D + HALF * e:D + HALF * e + HALF], start=b == 0, stop=b == NS - 1)
                last.then_inc(s["spv"], 1)


SCALE = QK ** -0.5


def turned_by(x, cos, sin, t1, t2, rope):
    def half(a, j):
        return a[:, :, j:j + 1, :]
    return [lambda dve: dve.tensor_tensor(t1, x, cos, ALU.mult),
            lambda dve: dve.tensor_tensor(half(t2, 0), half(x, 1), half(sin, 0), ALU.mult),
            lambda dve: dve.tensor_tensor(half(t2, 1), half(x, 0), half(sin, 1), ALU.mult),
            lambda dve: dve.tensor_tensor(rope, t1, t2, ALU.add)]


def mla_in(core, xnT, lat, kr, cqT, ckvT, krTs, cos, sin):
    nc = core.nc
    T = NT + 1
    HR = RD // 2
    with Marks(core, "min", w=32, gain=64, proj=1, square=2, mean=1, root=1, inv=1, normed=2, rope=4, turned=1, copied=3,
               stored=32) as s, ExitStack() as ctx:
        at = s.at
        w = core.sbuf(ctx, "w", [P, KD, MIN])
        gq = core.sbuf(ctx, "gq", [P, QL])
        gk = core.sbuf(ctx, "gk", [P, KL])
        junk = core.sbuf(ctx, "junk", [P, QL + KL])
        st = core.sbuf(ctx, "st", [P, T, 3, 2])
        cq = core.sbuf(ctx, "cq", [P, T, QL])
        t1 = core.sbuf(ctx, "t1", [P, T, RD])
        t2 = core.sbuf(ctx, "t2", [P, T, RD])
        pq = [core.psum(ctx, "pq", [P, QL]) for _ in range(2)]
        pk = [core.psum(ctx, "pk", [P, KL + RD]) for _ in range(2)]
        pt = core.psum(ctx, "pt", [P, 4, P])
        pu = core.psum(ctx, "pu", [P, 3, P])
        with nc.Block() as block:
            @block.sync
            def _(sp):
                wd = core.i["w_mla_in"].rearrange("(k p) n -> p k n", p=P)
                sp.dma_start(w[:, :, 0:QL], wd[:, :, 0:QL]).then_inc(s["w"], 16)
                sp.dma_start(w[:, :, QL:], wd[:, :, QL:]).then_inc(s["w"], 16)
                sp.dma_start(gq[:, :], core.i["g_cq"].to_broadcast([P, QL])).then_inc(s["gain"], 16)
                sp.dma_start(gk[:, :], core.i["g_ckv"].to_broadcast([P, KL])).then_inc(s["gain"], 16)
                sp.dma_start(cos[:, :, :], core.i["cos"]).then_inc(s["gain"], 16)
                sp.dma_start(sin[:, :, :], core.i["sin"]).then_inc(s["gain"], 16)
                sp.wait_ge(s["normed"], 2 * T)
                sp.wait_ge(s["rope"], 4 * T)
                for name, tile in (("lat", lat), ("kr", kr)):
                    sp.dma_start(core.o[name + "_p"].rearrange("(t p) r -> p t r", p=P), tile[:, 0:NT, :]).then_inc(s["stored"], 16)
                    sp.dma_start(core.o[name + "_s"], tile[:NS, NT, :]).then_inc(s["stored"], 16)
                sp.wait_ge(s["stored"], 64)

            @block.tensor
            def _(pe):
                pe.wait_ge(s["w"], 32)
                for t in range(T + 1):
                    if t < T:
                        n = P if t < NT else NS
                        if t >= 2:
                            after(pe, at("rope", t - 1, 0), at("normed", t - 1, 0))
                        for k in range(KD):
                            pe.matmul(pq[t % 2][:n, :], xnT[:, k, P * t:P * t + n], w[:, k, 0:QL], start=k == 0, stop=k == KD - 1)
                        for k in range(KD):
                            last = pe.matmul(pk[t % 2][:n, :], xnT[:, k, P * t:P * t + n], w[:, k, QL:], start=k == 0, stop=k == KD - 1)
                        last.then_inc(s["proj"], 1)
                    if t:
                        u = t - 1
                        n = P if u < NT else NS
                        after(pe, at("normed", u, 2), at("rope", u, 4), at("copied", u, 0))
                        eye = core.const[:n, C_ID, :n]
                        for j in range(4):
                            pe.transpose(pt[:, j, :n], cq[:n, u, P * j:P * j + P], eye)
                        for j in range(2):
                            last = pe.transpose(pu[:, j, :n], lat[:n, u, P * j:P * j + P], eye)
                        if u == NT:
                            last = pe.transpose(pu[:RD, 2, :n], kr[:n, u, :], eye)
                        last.then_inc(s["turned"], 1)

            @block.scalar
            def _(act):
                for t in range(T + 1):
                    if t < T:
                        n = P if t < NT else NS
                        after(act, at("proj", t, 1))
                        if t:
                            after(act, at("square", t, 0))
                        act.activation(junk[:n, 0:QL], pq[t % 2][:n, :], ACT.Square, accum_out=st[:n, t, 0, 0:1]).then_inc(s["square"], 1)
                        act.activation(junk[:n, QL:], pk[t % 2][:n, 0:KL], ACT.Square, accum_out=st[:n, t, 0, 1:2]).then_inc(s["square"], 1)
                        after(act, at("mean", t, 1))
                        act.activation(st[:n, t, 1, :], st[:n, t, 1, :], ACT.Sqrt).then_inc(s["root"], 1)
                    if t:
                        u = t - 1
                        n = P if u < NT else NS
                        after(act, at("turned", u, 1))
                        act.activation(cqT[:, :, P * u:P * u + n], pt[:, :, :n], ACT.Copy).then_inc(s["copied"], 1)
                        act.activation(ckvT[:, :, P * u:P * u + n], pu[:, 0:2, :n], ACT.Copy).then_inc(s["copied"], 1)
                        act.activation(krTs[:, :], pu[:RD, 2, 0:NS] if u == NT else core.const[:RD, C_ID, 0:NS], ACT.Copy).then_inc(s["copied"], 1)
                        if u < NT:
                            after(act, at("copied", u, 3))

            @block.vector
            def _(dve):
                dve.wait_ge(s["gain"], 64)
                for t in range(T):
                    n = P if t < NT else NS
                    after(dve, at("square", t, 2))
                    dve.tensor_scalar(st[:n, t, 1, 0:1], st[:n, t, 0, 0:1], 1.0 / QL, EPS, ALU.mult, ALU.add)
                    dve.tensor_scalar(st[:n, t, 1, 1:2], st[:n, t, 0, 1:2], 1.0 / KL, EPS, ALU.mult, ALU.add).then_inc(s["mean"], 1)
                    after(dve, at("root", t, 1))
                    dve.reciprocal(st[:n, t, 2, :], st[:n, t, 1, :]).then_inc(s["inv"], 1)
                    after(dve, at("inv", t, 1))
                    dve.scalar_tensor_tensor(cq[:n, t, :], pq[t % 2][:n, :], st[:n, t, 2, 0:1], gq[:n, :], ALU.mult, ALU.mult).then_inc(s["normed"], 1)
                    dve.scalar_tensor_tensor(lat[:n, t, :], pk[t % 2][:n, 0:KL], st[:n, t, 2, 1:2], gk[:n, :], ALU.mult, ALU.mult).then_inc(s["normed"], 1)

                    def four(a):
                        return a.rearrange("p (o j c) -> p o j c", o=1, j=2)
                    ops = turned_by(four(pk[t % 2][:n, KL:]), four(cos[:n, t, :]), four(sin[:n, t, :]), four(t1[:n, t, :]), four(t2[:n, t, :]), four(kr[:n, t, :]))
                    for j, op in enumerate(ops):
                        if j == 3:
                            after(dve, at("rope", t, 3))
                        op(dve).then_inc(s["rope"], 1)


def mla_qkv(core, lat, kr, cqT, ckvT, cos, sin, q, kn, kr8, v, ksc, wuv):
    nc = core.nc
    T = NT + 1
    QW = H * QK
    with Marks(core, "qkv", w=48, gain=32, gains=1, q_made=1, q_out=1, k_made=1, v_made=1, v_out=1, k_square=2, q_square=1, rope=4, stat=11,
               root=2, k_out=3, q_done=2, stored=32) as s, ExitStack() as ctx:
        at = s.at
        wq = core.sbuf(ctx, "wq", [P, 4, QW])
        wk = core.sbuf(ctx, "wk", [P, 2, H * HD])
        g = core.sbuf(ctx, "g", [P, 3, QK])
        sq = core.sbuf(ctx, "sq", [P, H, QK])
        sqk = core.sbuf(ctx, "sqk", [P, H, HD])
        t1 = core.sbuf(ctx, "t1", [P, H, RD])
        t2 = core.sbuf(ctx, "t2", [P, H, RD])
        krs = core.sbuf(ctx, "krs", [P, T])
        junk = core.sbuf(ctx, "junk", [P, RD])
        st = core.sbuf(ctx, "st", [P, 6, H])
        pq = core.psum(ctx, "pq", [P, QW])
        pk = core.psum(ctx, "pk", [P, H, HD])
        pv = core.psum(ctx, "pv", [P, H, HD])
        with nc.Block() as block:
            @block.sync
            def _(sp):
                sp.dma_start(wk[:, :, :], core.i["w_uk"].rearrange("(k p) n -> p k n", p=P)).then_inc(s["w"], 16)
                sp.dma_start(wuv[:, :, :], core.i["w_uv"].rearrange("(k p) n -> p k n", p=P)).then_inc(s["w"], 16)
                sp.dma_start(wq[:, :, :], core.i["w_uq"].rearrange("(k p) n -> p k n", p=P)).then_inc(s["w"], 16)
                sp.dma_start(g[:, 0, :], core.i["g_q"].to_broadcast([P, QK])).then_inc(s["gain"], 16)
                sp.dma_start(g[:, 1, :], core.i["g_k"].to_broadcast([P, QK])).then_inc(s["gain"], 16)
                sp.wait_ge(s["stat"], 11 * T)
                sp.dma_start(core.o["ksc_p"].rearrange("(t p) r -> p t r", p=P), ksc[:, 0:NT, :]).then_inc(s["stored"], 16)
                sp.dma_start(core.o["ksc_s"], ksc[:NS, NT, :]).then_inc(s["stored"], 16)
                sp.wait_ge(s["stored"], 32)

            @block.tensor
            def _(pe):
                pe.wait_ge(s["w"], 48)
                for t in range(T):
                    n = P if t < NT else NS

                    def project(out, k_count, xT, w, width):
                        for c in range(0, width, SEQ):
                            for k in range(k_count):
                                last = pe.matmul(out[:n, c:c + SEQ], xT[:, k, P * t:P * t + n], w[:, k, c:c + SEQ], start=k == 0, stop=k == k_count - 1)
                        return last

                    after(pe, at("k_out", t, 0))
                    project(pk[:, :, :].rearrange("p h d -> p (h d)"), 2, ckvT, wk, H * HD).then_inc(s["k_made"], 1)
                    after(pe, at("q_out", t, 0))
                    project(pq, 4, cqT, wq, QW).then_inc(s["q_made"], 1)
                    if t < NT:
                        after(pe, at("v_out", t, 0))
                        project(pv[:, :, :].rearrange("p h d -> p (h d)"), 2, ckvT, wuv, H * HD).then_inc(s["v_made"], 1)

            @block.scalar
            def _(act):
                for t in range(T):
                    n = P if t < NT else NS
                    after(act, at("k_made", t, 1), at("stat", t, 0), at("k_square", t, 0))
                    act.activation(sqk[:n, :, :], pk[:n, :, :], ACT.Square).then_inc(s["k_square"], 1)
                    act.activation(junk[:n, :], kr[:n, t, :], ACT.Square, accum_out=krs[:n, t:t + 1]).then_inc(s["k_square"], 1)
                    after(act, at("q_made", t, 1))
                    act.activation(q[:n, t, :, :], pq[:n, :].rearrange("p (h d) -> p h d", h=H), ACT.Copy).then_inc(s["q_out"], 1)
                    if t < NT:
                        after(act, at("v_made", t, 1))
                        act.activation(v[:n, t, :, :], pv[:n, :, :], ACT.Copy).then_inc(s["v_out"], 1)
                    after(act, at("stat", t, 3))
                    act.activation(st[:n, 0, :], st[:n, 1, :], ACT.Sqrt).then_inc(s["root"], 1)
                    after(act, at("rope", t, 4))
                    act.activation(sq[:n, :, :], q[:n, t, :, :], ACT.Square).then_inc(s["q_square"], 1)
                    after(act, at("stat", t, 10))
                    act.activation(st[:n, 4, :], st[:n, 4, :], ACT.Sqrt).then_inc(s["root"], 1)

            @block.vector
            def _(dve):
                dve.wait_ge(s["gain"], 32)
                dve.tensor_tensor(g[:, 2, :], g[:, 0, :], g[:, 1, :], ALU.mult).then_inc(s["gains"], 1)
                for t in range(T):
                    n = P if t < NT else NS

                    def wide(a, width):
                        return a.rearrange("p (h o) -> p h o", o=1).to_broadcast([n, H, width])

                    after(dve, at("k_square", t, 2))
                    dve.tensor_reduce(st[:n, 0, :], sqk[:n, :, :], AX.X, ALU.add).then_inc(s["stat"], 1)
                    after(dve, at("stat", t, 1))
                    dve.tensor_scalar(st[:n, 1, :], st[:n, 0, :], krs[:n, t:t + 1], 1.0 / QK, ALU.add, ALU.mult).then_inc(s["stat"], 1)
                    after(dve, at("stat", t, 2))
                    dve.tensor_scalar(st[:n, 1, :], st[:n, 1, :], EPS, None, ALU.add).then_inc(s["stat"], 1)
                    after(dve, at("q_out", t, 1), at("rope", t, 0))

                    def four(a):
                        return a.rearrange("p h (j c) -> p h j c", j=2)
                    rot = four(q[:n, t, :, HD:])
                    c4, s4 = (a[:n, t:t + 1, :].rearrange("p o (j c) -> p o j c", j=2).to_broadcast([n, H, 2, RD // 2]) for a in (cos, sin))
                    for j, op in enumerate(turned_by(rot, c4, s4, four(t1[:n, :, :]), four(t2[:n, :, :]), rot)):
                        if j == 3:
                            after(dve, at("rope", t, 3))
                        op(dve).then_inc(s["rope"], 1)
                    after(dve, at("root", t, 1))
                    dve.reciprocal(ksc[:n, t, :], st[:n, 0, :]).then_inc(s["stat"], 1)
                    after(dve, at("stat", t, 4))
                    dve.tensor_tensor(st[:n, 2, :], ksc[:n, t, :], ksc[:n, t, :], ALU.mult).then_inc(s["stat"], 1)
                    after(dve, at("stat", t, 5))
                    dve.tensor_tensor(st[:n, 2, :], st[:n, 2, :], st[:n, 1, :], ALU.mult).then_inc(s["stat"], 1)
                    after(dve, at("stat", t, 6))
                    dve.tensor_scalar(st[:n, 2, :], st[:n, 2, :], -0.5, 1.5, ALU.mult, ALU.add).then_inc(s["stat"], 1)
                    after(dve, at("stat", t, 7))
                    dve.tensor_tensor(ksc[:n, t, :], ksc[:n, t, :], st[:n, 2, :], ALU.mult).then_inc(s["stat"], 1)
                    after(dve, at("stat", t, 8))
                    dve.tensor_scalar(st[:n, 2, :], ksc[:n, t, :], SCALE, None, ALU.mult).then_inc(s["k_out"], 1)
                    after(dve, at("k_out", t, 1))
                    if t < NT:
                        dve.tensor_tensor(kn[:n, t, :, :], pk[:n, :, :], wide(st[:n, 2, :], HD), ALU.mult).then_inc(s["k_out"], 1)
                        dve.tensor_tensor(kr8[:n, t, :, :], kr[:n, t:t + 1, :].to_broadcast([n, H, RD]), wide(st[:n, 2, :], RD), ALU.mult).then_inc(s["k_out"], 1)
                    after(dve, at("q_square", t, 1))
                    dve.tensor_reduce(st[:n, 3, :], sq[:n, :, :], AX.X, ALU.add).then_inc(s["stat"], 1)
                    after(dve, at("stat", t, 9))
                    dve.tensor_scalar(st[:n, 4, :], st[:n, 3, :], 1.0 / QK, EPS, ALU.mult, ALU.add).then_inc(s["stat"], 1)
                    after(dve, at("root", t, 2))
                    dve.reciprocal(st[:n, 5, :], st[:n, 4, :]).then_inc(s["stat"], 1)
                    after(dve, at("stat", t, 11))
                    dve.tensor_tensor(q[:n, t, :, :], q[:n, t, :, :], wide(st[:n, 5, :], QK), ALU.mult).then_inc(s["q_done"], 1)
                    after(dve, at("q_done", t, 1), at("gains", 0, 1))
                    dve.tensor_tensor(q[:n, t, :, :], q[:n, t, :, :], g[:n, 2:3, :].to_broadcast([n, H, QK]), ALU.mult).then_inc(s["q_done"], 1)


def mla_seq(core, q, kn, kr8, v, oT):
    nc = core.nc
    with Marks(core, "att", q_staged=4, k_staged=6, q_turned=2, k_turned=2, q_copied=4, k_copied=4, scored=2 * NT, low=2 * NT, exped=2 * NT,
               inv=2 * NT, p_done=2 * NT, p_turned=2 * NT, p_even=NT, p_odd=NT, summed=2, out=2) as s, ExitStack() as ctx:
        at = s.at

        def two(name, shape):
            return [core.sbuf(ctx, name, list(shape)) for _ in range(2)]

        qn, qr, knh, krh, vh = (two(n, (P, NT, w)) for n, w in (("qn", P), ("qr", RD), ("knh", P), ("krh", RD), ("vh", P)))
        qnT, knT = two("qnT", (P, SEQ)), two("knT", (P, SEQ))
        qrT, krT = two("qrT", (RD, SEQ)), two("krT", (RD, SEQ))
        p = two("p", (P, NT, SEQ))
        pT = two("pT", (P, NT, SEQ))
        st = two("st", (P, 3, NT))
        bank = [[core.psum(ctx, "bank", [P, SEQ]) for _ in range(4)] for _ in range(2)]

        def head(tile, h, lo, hi):
            return tile[:, 0:NT, ds(h, 1), lo:hi].rearrange("p t o d -> p t (o d)")

        with nc.Block() as block:
            @block.gpsimd
            def _(pool):
                with pool.Fori(0, H // 2) as i:
                    for a in range(2):
                        after(pool, at("summed", i, 0))
                        for dst, src, w in ((knh, kn, HD), (krh, kr8, RD), (vh, v, HD)):
                            pool.tensor_copy(dst[a][:, :, :], head(src, 2 * i + a, 0, w)).then_inc(s["k_staged"], 1)

            @block.scalar
            def _(act):
                with act.Fori(0, H // 2) as i:
                    for a in range(2):
                        apart(act, at("q_turned", i, 0))
                        act.activation(qn[a][:, :, :], head(q, 2 * i + a, 0, HD), ACT.Copy).then_inc(s["q_staged"], 1)
                        act.activation(qr[a][:, :, :], head(q, 2 * i + a, HD, QK), ACT.Copy).then_inc(s["q_staged"], 1)
                    for a in range(2):
                        after(act, at("q_turned", i, a + 1))
                        act.activation(qnT[a][:, :], bank[a][0][:, :], ACT.Copy).then_inc(s["q_copied"], 1)
                        act.activation(qrT[a][:, :], bank[a][1][:RD, :], ACT.Copy).then_inc(s["q_copied"], 1)
                    for t in range(NT):
                        for a in range(2):
                            n = P * (t + 1)
                            after(act, at("low", i, 2 * t + a + 1))
                            act.activation(p[a][:, t, 0:n], bank[a][t][:, 0:n], ACT.Exp, bias=st[a][:, 0, t:t + 1],
                                           accum_out=st[a][:, 1, t:t + 1]).then_inc(s["exped"], 1)
                    for t in range(0, NT, 2):
                        for a in range(2):
                            after(act, at("p_turned", i, 2 * t + a + 1))
                            act.activation(pT[a][:, t, 0:P * (t + 1)], bank[a][t][:, 0:P * (t + 1)], ACT.Copy).then_inc(s["p_even"], 1)
                    for a in range(2):
                        apart(act, at("summed", i, a + 1))
                        act.activation(part(oT, 2 * i + a, SEQ), bank[a][0][:, :], ACT.Copy).then_inc(s["out"], 1)

            @block.vector
            def _(dve):
                with dve.Fori(0, H // 2) as i:
                    for a in range(2):
                        after(dve, at("k_turned", i, a + 1))
                        dve.tensor_copy(knT[a][:, :], bank[a][2][:, :]).then_inc(s["k_copied"], 1)
                        dve.tensor_copy(krT[a][:, :], bank[a][3][:RD, :]).then_inc(s["k_copied"], 1)
                    for t in range(NT):
                        for a in range(2):
                            after(dve, at("scored", i, 2 * t + a + 1))
                            dve.tensor_reduce(st[a][:, 0, t:t + 1], bank[a][t][:, 0:P * (t + 1)], AX.X, ALU.max, negate=True).then_inc(s["low"], 1)
                    for t in range(NT):
                        for a in range(2):
                            n = P * (t + 1)
                            after(dve, at("exped", i, 2 * t + a + 1))
                            dve.reciprocal(st[a][:, 2, t:t + 1], st[a][:, 1, t:t + 1]).then_inc(s["inv"], 1)
                            after(dve, at("inv", i, 2 * t + a + 1))
                            dve.tensor_scalar(p[a][:, t, 0:n], p[a][:, t, 0:n], st[a][:, 2, t:t + 1], None, ALU.mult).then_inc(s["p_done"], 1)
                    for t in range(1, NT, 2):
                        for a in range(2):
                            after(dve, at("p_turned", i, 2 * t + a + 1))
                            dve.tensor_copy(pT[a][:, t, 0:P * (t + 1)], bank[a][t][:, 0:P * (t + 1)]).then_inc(s["p_odd"], 1)

            @block.tensor
            def _(pe):
                def turn(out, src, width):
                    for t in range(NT):
                        last = pe.transpose(out[:width, P * t:P * t + P], src[:, t, 0:width], core.ident)
                    return last

                with pe.Fori(0, H // 2) as i:
                    for a in range(2):
                        after(pe, at("q_staged", i, 2 * a + 2), at("out", i, 0))
                        turn(bank[a][0], qn[a], HD)
                        turn(bank[a][1], qr[a], RD).then_inc(s["q_turned"], 1)
                        after(pe, at("k_staged", i, 3 * a + 3))
                        turn(bank[a][2], knh[a], HD)
                        turn(bank[a][3], krh[a], RD).then_inc(s["k_turned"], 1)
                    for t in range(NT):
                        n = P * (t + 1)
                        for a in range(2):
                            if t == 0:
                                after(pe, at("q_copied", i, 2 * a + 2), at("k_copied", i, 2 * a + 2))
                            out = bank[a][t]
                            rows = slice(P * t, P * t + P)
                            pe.matmul(out[:, 0:n], qnT[a][:, rows], knT[a][:, 0:n], start=True, stop=False)
                            pe.matmul(out[:, 0:n], qrT[a][:, rows], krT[a][:, 0:n], start=False, stop=False)
                            pe.matmul(out[:, rows], core.ident, core.const[:, C_NEG, :], start=False, stop=True).then_inc(s["scored"], 1)
                    for t in range(NT):
                        for a in range(2):
                            after(pe, at("p_done", i, 2 * t + a + 1))
                            for j in range(t + 1):
                                last = pe.transpose(bank[a][t][:, P * j:P * j + P], p[a][:, t, P * j:P * j + P], core.ident)
                            last.then_inc(s["p_turned"], 1)
                    for a in range(2):
                        after(pe, at("p_even", i, NT - 2 + a + 1), at("p_odd", i, NT - 2 + a + 1))
                        for t in range(NT):
                            for j in range(t + 1):
                                last = pe.matmul(bank[a][0][:, P * t:P * t + P], vh[a][:, j, :], pT[a][:, t, P * j:P * j + P], start=j == 0, stop=j == t)
                        last.then_inc(s["summed"], 1)


def mla_dec(core, q, ckvT, krTs, ksc, wuv, os):
    nc = core.nc
    N = NS * H
    BQ = 4
    NG = PER // BQ
    T0 = SEQ
    with Marks(core, "pag", inp=96, step=13, turned=1, lat_made=1, self_made=1,
               idx=2, lc0=16, lc1=16, lr0=16, lr1=16, lk0=16, lk1=16,
               flip=2 * NG, half0=2 * NG, half1=2 * NG, keyr=2 * NG, scored=2, soft0=10, soft1=10, maxed=2, spread=2, exped=4, lsum=2, pv=2, o=6,
               final=1) as s, ExitStack() as ctx:
        at = s.at
        wukT = core.sbuf(ctx, "wukT", [P, H, KL])
        ptab = core.sbuf(ctx, "ptab", [P, NS], mybir.dt.int32)
        rest = core.sbuf(ctx, "rest", [P, 1])
        ptf = core.sbuf(ctx, "ptf", [P, NS])
        idx = [core.sbuf(ctx, "idx", [P, 1], U32) for _ in range(2)]
        c = [core.sbuf(ctx, "c", [P, PER, KL]) for _ in range(2)]
        kr = [core.sbuf(ctx, "kr", [P, PER, RD]) for _ in range(2)]
        ks = [core.sbuf(ctx, "ks", [P, PER, H]) for _ in range(2)]
        qnT = core.sbuf(ctx, "qnT", [P, H, NS])
        qrT = core.sbuf(ctx, "qrT", [RD, NS, H])
        qlat = core.sbuf(ctx, "qlat", [P, 2, NS, H])
        prod = core.sbuf(ctx, "prod", [P, 3, NS, H])
        spread = core.sbuf(ctx, "spread", [NS, NS, H])
        sself = core.sbuf(ctx, "sself", [P, N])
        krep = core.sbuf(ctx, "krep", [P, N])
        cT = [core.sbuf(ctx, "cT", [P, 2, BQ, P]) for _ in range(2)]
        rT = [core.sbuf(ctx, "rT", [RD, BQ, P]) for _ in range(2)]
        S = [core.sbuf(ctx, "S", [P, PER, H]) for _ in range(2)]
        m = [core.sbuf(ctx, "m", [P, 6, H]) for _ in range(2)]
        mx = [core.sbuf(ctx, "mx", [H, 1 + H]) for _ in range(2)]
        olat = core.sbuf(ctx, "olat", [P, 2, NS, H])
        b0 = [core.psum(ctx, "b0", [P, BQ, P]) for _ in range(2)]
        b1 = [core.psum(ctx, "b1", [P, BQ, P]) for _ in range(2)]
        b2 = core.psum(ctx, "b2", [P, BQ, P])
        pS = core.psum(ctx, "pS", [P, PER, H])
        pM = core.psum(ctx, "pM", [P, P + 2 * H])
        pO = core.psum(ctx, "pO", [P, 2, N])

        def flat(tile):
            return tile[:, :, :].rearrange("p a b -> p (a b)")

        with nc.Block() as block:
            @block.sync
            def _(sp):
                with nc.allow_non_contiguous_dma(reason="a page number for each partition"):
                    for r in range(GRP):
                        sp.dma_start(ptab[r:P:GRP, :], core.i["page_table"].rearrange("b g -> g b")).then_inc(s["inp"], 16)
                sp.dma_start(rest[:, :], core.i["rest"]).then_inc(s["inp"], 16)
                sp.dma_start(wukT[:, :, :], core.i["w_ukT"]).then_inc(s["inp"], 16)

            @block.gpsimd
            def _(pool):
                def gather(a):
                    for dst, src, name in ((c, "cache_latent", "lc"), (kr, "cache_krope", "lr"), (ks, "cache_kscale", "lk")):
                        pool.indirect_dma_start(out=flat(dst[a]), out_offset=None, in_=core.i[src],
                                                in_offset=bass.IndirectOffsetOnAxis(ap=idx[a][:, 0:1], axis=0)).then_inc(s[f"{name}{a}"], 16)

                for a in range(2):
                    pool.wait_ge(s["idx"], a + 1)
                    gather(a)
                with pool.Fori(1, NS // 2) as i:
                    for a in range(2):
                        apart(pool, at("idx", i, a + 1), at("pv", i, a - 1))
                        gather(a)

            @block.scalar
            def _(act):
                def soften(i, a):
                    after(act, at(f"soft{a}", i, 7))
                    act.activation(S[a][:, :, :], S[a][:, :, :], ACT.Exp).then_inc(s["exped"], 1)
                    act.activation(m[a][:, 3, :], m[a][:, 2, :], ACT.Exp).then_inc(s["exped"], 1)

                with act.Fori(0, NS // 2) as i:
                    for a in range(2):
                        for g in range(NG):
                            after(act, at("flip", i, NG * a + g + 1))
                            act.activation(cT[g % 2][:, 0, :, :], b0[g % 2][:, :, :], ACT.Copy).then_inc(s["half0"], 1)
                            act.activation(rT[g % 2][:, :, :], b2[:RD, :, :], ACT.Copy).then_inc(s["keyr"], 1)
                            if a == 1 and g == 0:
                                soften(i, 0)
                    soften(i, 1)

            @block.tensor
            def _(pe):
                pe.wait_ge(s["inp"], 96)
                eye = core.const[:NS, C_ID, 0:NS]
                for h in range(H):
                    pe.transpose(pM[:, NS * h:NS * h + NS], q[:NS, NT, h, 0:HD], eye)
                for h in range(H):
                    last = pe.transpose(pS[:RD, h, :], q[:NS, NT, h, HD:QK], eye)
                last.then_inc(s["turned"], 1)
                pe.wait_ge(s["step"], 2)
                for h in range(H):
                    for e in range(2):
                        last = pe.matmul(pO[:, e, NS * h:NS * h + NS], wukT[:, h, P * e:P * e + P], qnT[:, h, :], start=True, stop=True)
                last.then_inc(s["lat_made"], 1)
                pe.wait_ge(s["step"], 8)
                pe.matmul(pS[:, 0:NS, :].rearrange("p b h -> p (b h)"), core.ones, prod[:, 0, :, :].rearrange("p b h -> p (b h)"), start=True, stop=False)
                pe.matmul(pS[:, 0:NS, :].rearrange("p b h -> p (b h)"), core.ones, prod[:, 1, :, :].rearrange("p b h -> p (b h)"), start=False, stop=False)
                pe.matmul(pS[:, 0:NS, :].rearrange("p b h -> p (b h)"), core.ones[:RD, :], prod[:RD, 2, :, :].rearrange("p b h -> p (b h)"), start=False, stop=True)
                pe.matmul(pM[:, 0:N], core.ones[:NS, :], spread[:, :, :].rearrange("p b h -> p (b h)"), start=True, stop=True).then_inc(s["self_made"], 1)
                pe.wait_ge(s["step"], 10)

                def flip(i, a, g):
                    if g == 0:
                        after(pe, (s[f"lc{a}"], i * 16 + 16), (s[f"lr{a}"], i * 16 + 16))
                    k = NG * a + g
                    if k:
                        after(pe, at("keyr", i, k))
                        if k >= 2:
                            after(pe, at("half0", i, k - 1), at("half1", i, k - 1))
                    else:
                        after(pe, at("keyr", i, 0), at("half1", i, 0), at("half0", i, 0))
                    for j in range(BQ):
                        pe.transpose(b0[g % 2][:, j, :], c[a][:, BQ * g + j, 0:P], core.ident)
                        pe.transpose(b1[g % 2][:, j, :], c[a][:, BQ * g + j, P:], core.ident)
                        last = pe.transpose(b2[:RD, j, :], kr[a][:, BQ * g + j, :], core.ident)
                    last.then_inc(s["flip"], 1)

                def score(i, a, g):
                    b = 2 * i + a
                    k = NG * a + g + 1
                    after(pe, at("half0", i, k), at("half1", i, k), at("keyr", i, k))
                    if g == 0:
                        after(pe, at("soft0", i, 1) if a else at("soft1", i, 0))
                    for j in range(BQ):
                        out = pS[:, BQ * g + j, :]
                        pe.matmul(out, cT[g % 2][:, 0, j, :], part(qlat, b, H), start=True, stop=False)
                        pe.matmul(out, cT[g % 2][:, 1, j, :], part(qlat, NS + b, H), start=False, stop=False)
                        last = pe.matmul(out, rT[g % 2][:, j, :], part(qrT, b, H), start=False, stop=True)
                    if g == NG - 1:
                        last.then_inc(s["scored"], 1)

                def scores(i, a):
                    flip(i, a, 0)
                    for g in range(1, NG):
                        flip(i, a, g)
                        score(i, a, g - 1)
                        if a == 1 and g == 4:
                            values(i, 0)
                    score(i, a, NG - 1)

                def maximum(i, a):
                    after(pe, at(f"soft{a}", i, 2), at("soft0", i, 9) if a else at("soft1", i, 0))
                    pe.transpose(pM[:H, 0:P], m[a][:, 0, :], core.ident).then_inc(s["maxed"], 1)
                    after(pe, at(f"soft{a}", i, 4))
                    pe.matmul(pM[:, P:P + H], core.ones[:H, :], mx[a][:, 1:1 + H], start=True, stop=True).then_inc(s["spread"], 1)

                def values(i, a):
                    after(pe, at(f"soft{a}", i, 8))
                    pe.matmul(pM[:, P + H:P + 2 * H], core.ones, m[a][:, 4, :], start=True, stop=True).then_inc(s["lsum"], 1)
                    after(pe, at("o", i, 3 * a))
                    for e in range(2):
                        for j in range(PER):
                            last = pe.matmul(pO[:, e, 0:H], c[a][:, j, P * e:P * e + P], S[a][:, j, :], start=j == 0, stop=j == PER - 1)
                    last.then_inc(s["pv"], 1)

                with pe.Fori(0, NS // 2) as i:
                    scores(i, 0)
                    maximum(i, 0)
                    scores(i, 1)
                    maximum(i, 1)
                    values(i, 1)
                pe.wait_ge(s["o"], 3 * NS)
                for h in range(H):
                    for e in range(2):
                        last = pe.matmul(pO[:, 0, NS * h:NS * h + NS], wuv[:, e, HD * h:HD * h + HD], olat[:, e, :, h], start=e == 0, stop=e == 1)
                last.then_inc(s["final"], 1)

            @block.vector
            def _(dve):
                done = [0]

                def then(ins):
                    ins.then_inc(s["step"], 1)
                    done[0] += 1
                    dve.wait_ge(s["step"], done[0])

                dve.wait_ge(s["turned"], 1)
                then(dve.tensor_copy(qnT[:, :, :], pM[:, 0:N].rearrange("p (h b) -> p h b", h=H)))
                then(dve.tensor_copy(qrT[:, :, :], pS[:RD, 0:H, :].rearrange("p h b -> p b h")))
                dve.wait_ge(s["lat_made"], 1)
                for e in range(2):
                    then(dve.tensor_copy(qlat[:, e, :, :], pO[:, e, :].rearrange("p (h b) -> p b h", h=H)))
                for e in range(2):
                    then(dve.tensor_tensor(prod[:, e, :, :], qlat[:, e, :, :], ckvT[:, e, T0:T0 + NS].rearrange("p (b o) -> p b o", o=1).to_broadcast([P, NS, H]), ALU.mult))
                then(dve.tensor_tensor(prod[:RD, 2, :, :], qrT[:, :, :], krTs[:, :].rearrange("p (b o) -> p b o", o=1).to_broadcast([RD, NS, H]), ALU.mult))
                then(dve.tensor_tensor(spread[:, :, :], core.const[:NS, C_ID, 0:NS].rearrange("p (b o) -> p b o", o=1).to_broadcast([NS, NS, H]),
                                       ksc[:NS, NT:NT + 1, :].to_broadcast([NS, NS, H]), ALU.mult))
                dve.wait_ge(s["self_made"], 1)
                then(dve.tensor_copy(krep[:, :], pM[:, 0:N]))
                then(dve.scalar_tensor_tensor(sself[:, :], pS[:, 0:NS, :].rearrange("p b h -> p (b h)"), SCALE, krep[:, :], ALU.mult, ALU.mult))
                dve.wait_ge(s["inp"], 96)
                then(dve.tensor_copy(ptf[:, :], ptab[:, :]))
                then(dve.scalar_tensor_tensor(ptf[:, :], ptf[:, :], float(GRP), rest[:, 0:1].to_broadcast([P, NS]), ALU.mult, ALU.add))

                def soft(a, ins):
                    ins.then_inc(s[f"soft{a}"], 1)

                def number(v, a):
                    dve.tensor_copy(idx[a][:, :], part(ptf, v, 1)).then_inc(s["idx"], 1)

                def minus(a, k):
                    return m[a][:, k:k + 1, :].to_broadcast([P, PER, H])

                def first(i, a):
                    after(dve, at("scored", i, a + 1), (s[f"lk{a}"], i * 16 + 16), at("pv", i, 0))
                    soft(a, dve.scalar_tensor_tensor(flat(S[a]), flat(pS), SCALE, flat(ks[a]), ALU.mult, ALU.mult))
                    after(dve, at(f"soft{a}", i, 1))
                    soft(a, dve.tensor_reduce(m[a][:, 0, :], S[a][:, :, :].rearrange("p j h -> p h j"), AX.X, ALU.max))
                    after(dve, at("maxed", i, a + 1))
                    soft(a, dve.tensor_reduce(mx[a][:, 0:1], pM[:H, 0:P], AX.X, ALU.max))
                    after(dve, at(f"soft{a}", i, 3))
                    soft(a, dve.tensor_scalar(mx[a][:, 1:1 + H], core.const[:H, C_ID, 0:H], mx[a][:, 0:1], None, ALU.mult))
                    after(dve, at("spread", i, a + 1))
                    soft(a, dve.tensor_tensor(m[a][:, 1, :], pM[:, P:P + H], part(sself, 2 * i + a, H), ALU.max))
                    after(dve, at(f"soft{a}", i, 5))
                    soft(a, dve.tensor_tensor(m[a][:, 2, :], part(sself, 2 * i + a, H), m[a][:, 1, :], ALU.subtract))
                    soft(a, dve.tensor_tensor(S[a][:, :, :], S[a][:, :, :], minus(a, 1), ALU.subtract))

                def second(i, a):
                    after(dve, at("exped", i, 2 * a + 2))
                    soft(a, dve.tensor_reduce(m[a][:, 4, :], S[a][:, :, :].rearrange("p j h -> p h j"), AX.X, ALU.add))

                def third(i, a):
                    after(dve, at("lsum", i, a + 1))
                    soft(a, dve.tensor_tensor(m[a][:, 5, :], pM[:, P + H:P + 2 * H], m[a][:, 3, :], ALU.add))
                    after(dve, at(f"soft{a}", i, 9))
                    soft(a, dve.reciprocal(m[a][:, 5, :], m[a][:, 5, :]))
                    after(dve, at("pv", i, a + 1), at(f"soft{a}", i, 10))
                    for e in range(2):
                        out = part(olat, e * NS + 2 * i + a, H)
                        dve.scalar_tensor_tensor(out, m[a][:, 3, :], part(ckvT, e * ROWS + T0 + 2 * i + a, 1), pO[:, e, 0:H], ALU.mult, ALU.add).then_inc(s["o"], 1)
                    after(dve, at("o", i, 3 * a + 2))
                    both = olat[:, :, ds(2 * i + a, 1), :].rearrange("p e o h -> p e (o h)")
                    dve.tensor_tensor(both, both, m[a][:, 5:6, :].to_broadcast([P, 2, H]), ALU.mult).then_inc(s["o"], 1)

                def turn(i, more):
                    for a in range(2):
                        for g in range(NG):
                            after(dve, at("flip", i, NG * a + g + 1))
                            dve.tensor_copy(cT[g % 2][:, 1, :, :], b1[g % 2][:, :, :]).then_inc(s["half1"], 1)
                            if a == 1 and g == 2:
                                second(i, 0)
                            if a == 1 and g == 5:
                                third(i, 0)
                                if more:
                                    apart(dve, at("lc0", i, 16), at("lr0", i, 16), at("lk0", i, 16))
                                    number(2 * i + 2, 0)
                        first(i, a)
                    second(i, 1)
                    third(i, 1)
                    if more:
                        apart(dve, at("lc1", i, 16), at("lr1", i, 16), at("lk1", i, 16))
                        number(2 * i + 3, 1)

                for a in range(2):
                    number(a, a)
                with dve.Fori(0, NS // 2 - 1) as i:
                    turn(i, True)
                turn(NS // 2 - 1, False)
                dve.wait_ge(s["final"], 1)
                dve.tensor_copy(os[:, :], pO[:, 0, :]).then_inc(s["step"], 1)


def load(core):
    nc = core.nc
    with Marks(core, "load", all=48, eps=1) as s, nc.Block() as block:
        @block.sync
        def _(sp):
            sp.dma_start(core.const[:, :, :], core.i["const"]).then_inc(s["all"], 16)
            sp.dma_start(core.x[:, :, :], core.i["x_prompt"].rearrange("(t p) d -> p t d", p=P)).then_inc(s["all"], 16)
            sp.dma_start(core.xs[:, :], core.i["x_sample"]).then_inc(s["all"], 16)
            sp.wait_ge(s["all"], 48)

        @block.vector
        def _(dve):
            dve.memset(core.eps, EPS).then_inc(s["eps"], 1)


def store(core):
    nc = core.nc
    with Marks(core, "store", all=32) as s, nc.Block() as block:
        @block.sync
        def _(sp):
            sp.dma_start(core.o["y_prompt"].rearrange("(t p) d -> p t d", p=P), core.x[:, :, :]).then_inc(s["all"], 16)
            sp.dma_start(core.o["y_sample"], core.xs[:, :]).then_inc(s["all"], 16)
            sp.wait_ge(s["all"], 32)


def gdn_layer(core):
    with ExitStack() as ctx:
        F = core.sbuf(ctx, "F", [P, KINDS * H, SEQ])
        Fs = core.sbuf(ctx, "Fs", [P, KINDS * H, NS])
        os = core.sbuf(ctx, "os", [P, H * NS])
        gout = core.sbuf(ctx, "gout", [P, 1])
        cols = core.sbuf(ctx, "cols", [P, 6, NT * H])
        srep = core.sbuf(ctx, "srep", [P, 3, H * NS])
        with ExitStack() as early:
            ba = core.sbuf(early, "ba", [P, NT + 1, 2 * H])
            taps = core.sbuf(early, "taps", [P, QKV, CW, NS])
            xnT = core.sbuf(early, "xnT", [P, KD, ROWS])
            with ExitStack() as rows:
                xn = core.sbuf(rows, "xn", [P, NT, D])
                xns = core.sbuf(rows, "xns", [NS, D])
                norm(core, core.i["norm_mix"][0:1, :], xn, xns, xnT)
            gdn_in(core, xnT, F, Fs, taps, ba)
            gdn_gate(core, ba, cols, srep, gout)
        gdn_dec(core, Fs, srep, gout, os)
        gdn_seq(core, F, cols, gout)
        out_proj(core, lambda k, t: F[:, k, P * t:P * t + P] if t < NT else os[:, k * NS:k * NS + NS], core.i["w_gdn_out"])


def mla_layer(core):
    with ExitStack() as ctx:
        oT = core.sbuf(ctx, "oT", [P, H, SEQ])
        os = core.sbuf(ctx, "os", [P, H * NS])
        ckvT = core.sbuf(ctx, "ckvT", [P, 2, ROWS])
        krTs = core.sbuf(ctx, "krTs", [RD, NS])
        ksc = core.sbuf(ctx, "ksc", [P, NT + 1, H])
        wuv = core.sbuf(ctx, "wuv", [P, 2, H * HD])
        q = core.sbuf(ctx, "q", [P, NT + 1, H, QK])
        with ExitStack() as keys:
            kn = core.sbuf(keys, "kn", [P, NT, H, HD])
            kr8 = core.sbuf(keys, "kr8", [P, NT, H, RD])
            v = core.sbuf(keys, "v", [P, NT, H, HD])
            with ExitStack() as early:
                lat = core.sbuf(early, "lat", [P, NT + 1, KL])
                kr = core.sbuf(early, "kr", [P, NT + 1, RD])
                cqT = core.sbuf(early, "cqT", [P, QL // P, ROWS])
                cos = core.sbuf(early, "cos", [P, NT + 1, RD])
                sin = core.sbuf(early, "sin", [P, NT + 1, RD])
                with ExitStack() as normed:
                    xnT = core.sbuf(normed, "xnT", [P, KD, ROWS])
                    with ExitStack() as rows:
                        xn = core.sbuf(rows, "xn", [P, NT, D])
                        xns = core.sbuf(rows, "xns", [NS, D])
                        norm(core, core.i["norm_mix"][1:2, :], xn, xns, xnT)
                    mla_in(core, xnT, lat, kr, cqT, ckvT, krTs, cos, sin)
                mla_qkv(core, lat, kr, cqT, ckvT, cos, sin, q, kn, kr8, v, ksc, wuv)
            mla_seq(core, q, kn, kr8, v, oT)
        mla_dec(core, q, ckvT, krTs, ksc, wuv, os)
        out_proj(core, lambda k, t: oT[:, k, P * t:P * t + P] if t < NT else os[:, k * NS:k * NS + NS], core.i["w_mla_out"])


def peer_layer(core, layer):
    with ExitStack() as ctx:
        xn = core.sbuf(ctx, "xn", [P, NT, D])
        xns = core.sbuf(ctx, "xns", [NS, D])
        qT = core.sbuf(ctx, "qT", [P, NT, 2 * H, P])
        qTs = core.sbuf(ctx, "qTs", [P, 2 * H, NS])
        with ExitStack() as early:
            xnT = core.sbuf(early, "xnT", [P, KD, ROWS])
            norm(core, core.i["norm_ffn"][layer:layer + 1, :], xn, xns, xnT)
            peer_q(core, xnT, core.i[f"w_peer{layer}"], qT, qTs)
        peer(core, xn, xns, qT, qTs, core.i[f"keys{layer}"], core.i[f"uv{layer}"])


def program(nc, ins, outs):
    with ExitStack() as ctx:
        core = Core(nc, ctx, ins, outs)
        load(core)
        gdn_layer(core)
        peer_layer(core, 0)
        mla_layer(core)
        peer_layer(core, 1)
        store(core)


def host(x):
    import numpy as np

    def c(a):
        return np.ascontiguousarray(a)

    def slices(w):
        k, n = w.shape
        return c(w.reshape(k // P, P, n // P, P).transpose(2, 1, 0, 3))

    j, i = np.arange(P)[:, None], np.arange(P)[None, :]
    tiles = [i == j, j >= 0, i >= j, i > j, np.where(i <= j, 0.0, NEG)]
    tiles += [(i // (2 << l) == j // (2 << l)) & ((i >> l) % 2 == 1) & ((j >> l) % 2 == 0) for l in range(LEVELS)]
    w = np.asarray(x["gdn_w_in"])[0]
    where = np.concatenate([np.arange(SEQ).reshape(NT, P), np.full((1, P), PAST)]).T.astype(np.float32)
    freq = np.float32(ROPE_THETA) ** (-np.arange(RD // 2, dtype=np.float32) / np.float32(RD // 2))
    angle = where[:, :, None] * freq
    cos, sin = np.cos(angle), np.sin(angle)
    return {
        "const": c(np.stack([np.broadcast_to(t, (P, P)).astype(np.float32) for t in tiles], 1)),
        "x_prompt": c(x["x_prompt"][0]), "x_sample": c(x["x_sample"][:, 0]),
        "norm_mix": c(x["norm_mix"]), "norm_ffn": c(x["norm_ffn"]),
        "w_gdn": slices(w[:, :KINDS * H * P]), "w_ba": c(w[:, KINDS * H * P:].reshape(KD, P, 2 * H).transpose(1, 0, 2)),
        "conv_w": c(x["gdn_conv_w"][0].reshape(CW, QKV, P).transpose(2, 1, 0).reshape(P, QKV * CW)),
        "state_conv": c(x["state_conv"][0].reshape(NS, CW - 1, QKV, P).transpose(3, 2, 1, 0)),
        "dt_bias": c(x["gdn_dt_bias"]), "a_log": c(x["gdn_a_log"]), "g_out": c(x["gdn_out_norm"][0].reshape(P, 1)),
        "state_ssm": c(x["state_ssm"][0].transpose(1, 0, 2, 3).reshape(H * NS, P, P)),
        "w_gdn_out": c(x["gdn_w_out"][0]),
        "counting": c(np.broadcast_to(np.arange(TOPK, dtype=np.float32), (P, TOPK))),
        "same": c(np.broadcast_to(np.eye(NS, dtype=np.float32), (P, NS, NS))),
        "w_mla_in": c(x["mla_w_in"][0]), "g_cq": c(x["mla_cq_norm"]), "g_ckv": c(x["mla_ckv_norm"]),
        "cos": c(np.concatenate([cos, cos], 2)), "sin": c(np.concatenate([-sin, sin], 2)),
        "w_uk": c(x["mla_w_uk"][0].reshape(KL, H * HD)), "w_ukT": c(x["mla_w_uk"][0].transpose(2, 1, 0)),
        "w_uv": c(x["mla_w_uv"][0].reshape(KL, H * HD)), "w_uq": c(x["mla_w_uq"][0]),
        "g_q": c(x["mla_q_norm"]), "g_k": c(x["mla_k_norm"]), "w_mla_out": c(x["mla_w_out"][0]),
        "page_table": c(x["page_table"]), "rest": (np.arange(P) % GRP).astype(np.float32).reshape(P, 1),
        "cache_latent": c(x["cache_latent"][0].reshape(-1, PER * KL)), "cache_krope": c(x["cache_krope"][0].reshape(-1, PER * RD)),
        "cache_kscale": c(x["cache_kscale"][0].reshape(-1, PER * H)),
        **{f"w_peer{l}": slices(x["peer_w_q"][l]) for l in range(2)},
        **{f"keys{l}": c(x["peer_sub_keys"][l].reshape(2 * H, NK, P).transpose(2, 0, 1)) for l in range(2)},
        **{f"uv{l}": np.concatenate([x["peer_u"][l], x["peer_v"][l]], 1) for l in range(2)},
    }


OUTS = {
    "y_prompt": (SEQ, D), "y_sample": (NS, D),
    "lat_p": (SEQ, KL), "kr_p": (SEQ, RD), "ksc_p": (SEQ, H), "lat_s": (NS, KL), "kr_s": (NS, RD), "ksc_s": (NS, H),
    "ssm_p": (H, P, P), "conv_p": (P, QKV, CW - 1), "ssm_s": (H * NS, P, P), "conv_s": (P, QKV, CW - 1, NS),
}


def kernel(**inputs):
    import numpy as np
    import concourse.bacc as bacc
    from concourse.bass_utils import run_bass_kernel_spmd

    nc = bacc.Bacc("TRN2", target_bir_lowering=False, num_devices=1)
    arrays = {f"in_{n}": a for n, a in host({n: np.asarray(a) for n, a in inputs.items()}).items()}
    ins = {n[3:]: nc.dram_tensor(n, a.shape, mybir.dt.from_np(a.dtype), kind="ExternalInput").ap() for n, a in arrays.items()}
    outs = {n: nc.dram_tensor(f"out_{n}", shape, F32, kind="ExternalOutput").ap() for n, shape in OUTS.items()}
    program(nc, ins, outs)
    result = run_bass_kernel_spmd(nc, [arrays], core_ids=[0]).results[0]
    o = {n: np.asarray(result[f"out_{n}"]) for n in OUTS}
    return (o["y_prompt"][None], o["y_sample"][:, None],
            o["lat_p"][None, None], o["kr_p"][None, None], o["ksc_p"][None, None],
            o["ssm_p"][None, None], o["conv_p"].transpose(2, 1, 0).reshape(1, 1, CW - 1, QKV * P),
            o["lat_s"][None, :, None], o["kr_s"][None, :, None], o["ksc_s"][None, :, None],
            o["ssm_s"].reshape(H, NS, P, P).transpose(1, 0, 2, 3)[None],
            o["conv_s"].transpose(3, 2, 1, 0).reshape(1, NS, CW - 1, QKV * P))
```

```python
from contextlib import ExitStack

import concourse.bass as bass
from concourse import mybir

ALU = mybir.AluOpType
ACT = mybir.ActivationFunctionType
AX = mybir.AxisListType
F32 = mybir.dt.float32
U32 = mybir.dt.uint32
ds = bass.ds

P = 128
D = 1024
KD = D // P
SEQ = 512
NT = SEQ // P
NS = 8
ROWS = SEQ + NS
H = 8
HD = 128
KINDS = 4
QKV = 3 * H
CW = 4
QL, KL, RD = 512, 256, 64
QK = HD + RD
MIN = QL + KL + RD
PAST = 4096
PAGE = 128
PER = PAST // P
GRP = PAGE // PER
TOPK = 16
NK = 128
EPS = 1e-6
ROPE_THETA = 10000.0
NEG = -1.0e30
RING = 8

C_ID, C_ONE, C_UP, C_STRICT, C_NEG, C_LEVEL = 0, 1, 2, 3, 4, 5
LEVELS = 7
N_CONST = C_LEVEL + LEVELS


def after(eng, *waits):
    for sem, value in waits:
        if not isinstance(value, int) or value > 0:
            eng.wait_ge(sem, value)


class Apart:

    def __call__(self, eng, *waits):
        waits = [(sem, value if isinstance(value, int) else eng.to_reg(value)) for sem, value in waits]
        if not isinstance(waits[0][1], int):
            eng.wait_ge(self.idle, 0)
        after(eng, *waits)


apart = Apart()


class Core:

    def __init__(self, nc, ctx, ins, outs):
        self.nc, self.ctx, self.i, self.o = nc, ctx, ins, outs
        self.n = 0
        self.phase = 0
        apart.idle = nc.alloc_semaphore("idle")
        self.x = self.sbuf(ctx, "x", [P, NT, D])
        self.xs = self.sbuf(ctx, "xs", [NS, D])
        self.const = self.sbuf(ctx, "const", [P, N_CONST, P])
        self.ident = self.const[:, C_ID, :]
        self.ones = self.const[:, C_ONE, :]
        self.eps = self.sbuf(ctx, "eps", [P, 1])[:, 0:1]

    def sbuf(self, ctx, name, shape, dtype=F32):
        self.n += 1
        return ctx.enter_context(self.nc.sbuf_tensor(f"{name}_{self.n}", shape, dtype))

    def psum(self, ctx, name, shape):
        self.n += 1
        return ctx.enter_context(self.nc.psum_tensor(f"{name}_{self.n}", shape, F32))



class Marks:

    def __init__(self, core, prefix, **per):
        self.core, self.per = core, per
        self.sems = {n: core.nc.alloc_semaphore(f"{prefix}_{n}_{core.phase}") for n in per}
        core.phase += 1

    def __getitem__(self, name):
        return self.sems[name]

    def at(self, name, i, k):
        return self.sems[name], i * self.per[name] + k

    def __enter__(self):
        return self

    def __exit__(self, *error):
        if error[0] is None:
            self.core.nc.clear_and_free_semaphores(list(self.sems.values()))
            self.core.nc.all_engine_barrier()


def rows_of(core, t):
    return (core.x[:, t, :], P) if t < NT else (core.xs[:, :], NS)


def norm(core, gain, xn, xns, xnT):
    nc = core.nc
    T = NT + 1
    with Marks(core, "norm", gain=16, sum=T, root=T, inv=2 * T, row=T, turned=2 * T, copied=T, copied2=T) as s, ExitStack() as ctx:
        g = core.sbuf(ctx, "gain", [P, D])
        junk = core.sbuf(ctx, "junk", [P, D])
        stat = core.sbuf(ctx, "stat", [P, 3, NT + 1])
        bank = [core.psum(ctx, "turn", [P, 4, P]) for _ in range(4)]

        def normed(t):
            return xn[:, t, :] if t < NT else xns[:, :]

        with nc.Block() as block:
            @block.sync
            def _(sp):
                sp.dma_start(g[:, :], gain.to_broadcast([P, D])).then_inc(s["gain"], 16)

            @block.scalar
            def _(act):
                for t in range(NT + 1):
                    x, n = rows_of(core, t)
                    if t:
                        act.wait_ge(s["sum"], t)
                    act.activation(junk[:n, :], x, ACT.Square, accum_out=stat[:n, 0, t:t + 1]).then_inc(s["sum"], 1)
                for t in range(NT + 1):
                    n = rows_of(core, t)[1]
                    act.wait_ge(s["inv"], 2 * (t) + 1)
                    act.activation(stat[:n, 1, t:t + 1], stat[:n, 1, t:t + 1], ACT.Sqrt).then_inc(s["root"], 1)
                for t in range(NT + 1):
                    n = rows_of(core, t)[1]
                    act.wait_ge(s["turned"], 2 * (t) + 1)
                    act.activation(xnT[:, 0:4, P * t:P * t + n], bank[2 * (t % 2)][:, :, :n], ACT.Copy).then_inc(s["copied"], 1)

            @block.vector
            def _(dve):
                for t in range(NT + 1):
                    n = rows_of(core, t)[1]
                    dve.wait_ge(s["sum"], t + 1)
                    dve.tensor_scalar(stat[:n, 1, t:t + 1], stat[:n, 0, t:t + 1], 1.0 / D, EPS, ALU.mult, ALU.add).then_inc(s["inv"], 1)
                    dve.wait_ge(s["root"], t + 1)
                    dve.reciprocal(stat[:n, 2, t:t + 1], stat[:n, 1, t:t + 1]).then_inc(s["inv"], 1)
                    if t == 0:
                        dve.wait_ge(s["gain"], 16)
                    x, n = rows_of(core, t)
                    dve.wait_ge(s["inv"], 2 * (t + 1))
                    dve.scalar_tensor_tensor(normed(t), x, stat[:n, 2, t:t + 1], g[:n, :], ALU.mult, ALU.mult).then_inc(s["row"], 1)
                for t in range(NT + 1):
                    n = rows_of(core, t)[1]
                    dve.wait_ge(s["turned"], 2 * (t) + 2)
                    dve.tensor_copy(xnT[:, 4:8, P * t:P * t + n], bank[2 * (t % 2) + 1][:, :, :n]).then_inc(s["copied2"], 1)

            @block.tensor
            def _(pe):
                for t in range(NT + 1):
                    n = rows_of(core, t)[1]
                    pe.wait_ge(s["row"], t + 1)
                    if t >= 2:
                        pe.wait_ge(s["copied"], t - 1)
                        pe.wait_ge(s["copied2"], t - 1)
                    for k in range(KD):
                        last = pe.transpose(bank[2 * (t % 2) + k // 4][:, k % 4, :n], normed(t)[:, P * k:P * k + P],
                                            core.const[:n, C_ID, :n])
                        if k % 4 == 3:
                            last.then_inc(s["turned"], 1)


def part(tile, n, width):
    dims = " ".join("abcd"[:len(tile.shape) - 1])
    flat = tile[:].rearrange(f"p {dims} -> p ({dims})") if len(tile.shape) > 2 else tile
    return flat[:, ds(n * width, width)]


def gdn_in(core, xnT, F, Fs, taps, ba):
    nc = core.nc
    W = 4
    NC, PAD = KINDS * H, CW - 1
    with Marks(core, "gdn", **{f"landed{w}": 16 for w in range(W)}, small=48, made=1, raw=1, sraw=1, kept=1, conved=1, silu=1,
               sconv=1, stored=32, bas=1, bac=2, zero=3) as s, ExitStack() as ctx:
        landed = [s[f"landed{w}"] for w in range(W)]
        small, made, raw, sraw, kept, conved, silu, sconv, stored, bas, bac, zero = (
            s[n] for n in ("small", "made", "raw", "sraw", "kept", "conved", "silu", "sconv", "stored", "bas", "bac", "zero"))
        w = core.sbuf(ctx, "w", [P, W, KD, P])
        wba = core.sbuf(ctx, "wba", [P, KD, 2 * H])
        cw = core.sbuf(ctx, "cw", [P, QKV * CW])
        inp = core.sbuf(ctx, "inp", [P, 2, PAD + SEQ])
        y = core.sbuf(ctx, "y", [P, 2, SEQ])
        keep = core.sbuf(ctx, "keep", [P, QKV, PAD])
        prod = core.sbuf(ctx, "prod", [P, QKV, CW, NS])
        acc = [core.psum(ctx, "acc", [P, SEQ]) for _ in range(2)]
        accs = [core.psum(ctx, "accs", [P, NS]) for _ in range(2)]
        pba = core.psum(ctx, "pba", [P, NT + 1, 2 * H])
        with nc.Block() as block:
            @block.sync
            def _(sp):
                sp.dma_start(wba[:, :, :], core.i["w_ba"]).then_inc(small, 16)
                sp.dma_start(cw[:, :], core.i["conv_w"]).then_inc(small, 16)
                sp.dma_start(taps[:, :, 0:PAD, :], core.i["state_conv"]).then_inc(small, 16)
                for c in range(W):
                    sp.dma_start(w[:, c, :, :], core.i["w_gdn"][c]).then_inc(landed[c], 16)
                with sp.Fori(1, NC // W) as i:
                    for c in range(W):
                        after(sp, (made, i * W + (c - W + 1)))
                        sp.dma_start(w[:, c, :, :], core.i["w_gdn"][ds(i * W + c, 1), :, :, :].rearrange("o p k n -> (o p) k n")).then_inc(landed[c], 16)
                sp.wait_ge(kept, QKV)
                sp.dma_start(core.o["conv_p"], keep[:, :, :]).then_inc(stored, 16)
                sp.wait_ge(sraw, NC)
                sp.dma_start(core.o["conv_s"], taps[:, :, 1:CW, :]).then_inc(stored, 16)
                sp.wait_ge(stored, 32)

            @block.tensor
            def _(pe):
                pe.wait_ge(small, 48)
                for t in range(NT + 1):
                    n = P if t < NT else NS
                    for k in range(KD):
                        last = pe.matmul(pba[:n, t, :], xnT[:, k, P * t:P * t + n], wba[:, k, :], start=k == 0, stop=k == KD - 1)
                last.then_inc(bas, 1)
                with pe.Fori(0, NC // W) as i:
                    for c in range(W):
                        after(pe, (landed[c], (i + 1) * 16), (raw, i * W + max(c - 1, 0)), (sraw, i * W + max(c - 1, 0)))
                        for k in range(KD):
                            pe.matmul(acc[c % 2][:, :], w[:, c, k, :], xnT[:, k, 0:SEQ], start=k == 0, stop=k == KD - 1)
                        for k in range(KD):
                            last = pe.matmul(accs[c % 2][:, :], w[:, c, k, :], xnT[:, k, SEQ:ROWS], start=k == 0, stop=k == KD - 1)
                        last.then_inc(made, 1)

            @block.vector
            def _(dve):
                dve.memset(ba[:, :, :], 0.0).then_inc(zero, 1)
                for c in range(2):
                    dve.memset(inp[:, c, 0:PAD], 0.0).then_inc(zero, 1)
                dve.wait_ge(zero, 3)
                dve.wait_ge(bas, 1)
                dve.tensor_copy(ba[:, 0:NT, :], pba[:, 0:NT, :]).then_inc(bac, 1)
                dve.tensor_copy(ba[:NS, NT, :], pba[:NS, NT, :]).then_inc(bac, 1)
                with dve.Fori(0, QKV // W) as i:
                    for c in range(W):
                        n, b = i * W + c, c % 2
                        after(dve, (made, n + 1))
                        dve.tensor_copy(part(taps, n * CW + PAD, NS), accs[b][:, :]).then_inc(sraw, 1)
                        after(dve, (raw, n + 1))
                        dve.tensor_copy(part(keep, n, PAD), inp[:, b, SEQ:SEQ + PAD]).then_inc(kept, 1)
                        after(dve, (silu, i * W + max(c - 1, 0)))
                        dve.tensor_scalar(y[:, b, :], inp[:, b, PAD:PAD + SEQ], part(cw, n * CW + PAD, 1), None, ALU.mult).then_inc(conved, 1)
                        for j in range(PAD):
                            after(dve, (conved, n * CW + (j + 1)))
                            dve.scalar_tensor_tensor(y[:, b, :], inp[:, b, j:j + SEQ], part(cw, n * CW + j, 1),
                                                     y[:, b, :], ALU.mult, ALU.add).then_inc(conved, 1)
                with dve.Fori(QKV // W, NC // W) as i:
                    for c in range(W):
                        after(dve, (made, i * W + (c + 1)))
                        dve.tensor_copy(part(Fs, i * W + c, NS), accs[c % 2][:, :]).then_inc(sraw, 1)
                dve.wait_ge(sraw, NC)
                dve.tensor_tensor(prod[:, :, :, :], taps[:, :, :, :],
                                  cw[:, :].rearrange("p (c j o) -> p c j o", j=CW, o=1).to_broadcast([P, QKV, CW, NS]), ALU.mult).then_inc(sconv, 1)
                dve.wait_ge(sconv, 1)
                dve.tensor_reduce(Fs[:, 0:QKV, :], prod[:, :, :, :].rearrange("p c j b -> p c b j"), AX.X, ALU.add).then_inc(sconv, 1)

            @block.scalar
            def _(act):
                act.wait_ge(zero, 3)

                def copy(i, c):
                    after(act, (made, i * W + (c + 1)), (conved, (i * W + max(c - 1, 0)) * CW), (kept, i * W + max(c - 1, 0)))
                    act.activation(inp[:, c % 2, PAD:PAD + SEQ], acc[c % 2][:, :], ACT.Copy).then_inc(raw, 1)

                def smooth(i, c):
                    after(act, (conved, (i * W + (c + 1)) * CW))
                    act.activation(part(F, i * W + c, SEQ), y[:, c % 2, :], ACT.Silu).then_inc(silu, 1)

                with act.Fori(0, QKV // W) as i:
                    copy(i, 0)
                    for c in range(1, W):
                        copy(i, c)
                        smooth(i, c - 1)
                    smooth(i, W - 1)
                with act.Fori(QKV // W, NC // W) as i:
                    for c in range(W):
                        after(act, (made, i * W + (c + 1)))
                        act.activation(part(F, i * W + c, SEQ), acc[c % 2][:, :], ACT.Silu).then_inc(raw, 1)
                act.wait_ge(sconv, 2)
                act.activation(Fs[:, :, :], Fs[:, :, :], ACT.Silu).then_inc(silu, 1)


def gdn_gate(core, ba, cols, srep, gout):
    nc = core.nc
    N = NT * H
    with Marks(core, "gate", inp=32, step=17, acts=6, summed=2) as s, ExitStack() as ctx:
        inp, step, acts, summed = (s[n] for n in ("inp", "step", "acts", "summed"))
        bias = core.sbuf(ctx, "bias", [P, H])
        alog = core.sbuf(ctx, "alog", [P, H])
        a = core.sbuf(ctx, "a", [P, NT + 1, H])
        neg = core.sbuf(ctx, "neg", [P, NT + 1, H])
        g = core.sbuf(ctx, "g", [P, NT + 1, H])
        beta = core.sbuf(ctx, "beta", [P, NT + 1, H])
        ex = core.sbuf(ctx, "ex", [P, 3, N])
        spread = core.sbuf(ctx, "spread", [NS, 2, H, NS])
        psum = core.psum(ctx, "sums", [P, 3, 2 * H * NS])
        with nc.Block() as block:
            @block.sync
            def _(sp):
                sp.dma_start(bias[:, :], core.i["dt_bias"].to_broadcast([P, H])).then_inc(inp, 16)
                sp.dma_start(alog[:, :], core.i["a_log"].to_broadcast([P, H])).then_inc(inp, 16)
                sp.dma_start(gout[:, :], core.i["g_out"]).then_inc(inp, 16)
                sp.wait_ge(inp, 48)

            @block.scalar
            def _(act):
                act.wait_ge(inp, 48)
                act.activation(beta[:, :, :], ba[:, :, 0:H], ACT.Sigmoid).then_inc(acts, 1)
                act.activation(alog[:, :], alog[:, :], ACT.Exp).then_inc(acts, 1)
                act.wait_ge(step, 3)
                act.activation(neg[:, :, :], neg[:, :, :], ACT.Exp).then_inc(acts, 1)
                act.wait_ge(step, 4)
                act.activation(neg[:, :, :], neg[:, :, :], ACT.Ln).then_inc(acts, 1)
                act.wait_ge(step, 10)
                act.activation(ex[:, :, :], ex[:, :, :], ACT.Exp).then_inc(acts, 1)
                act.wait_ge(acts, 5)
                act.wait_ge(summed, 2)
                act.activation(srep[:, 1, :], psum[:, 2, H * NS:], ACT.Exp).then_inc(acts, 1)

            @block.vector
            def _(dve):
                n = [0]

                def then(ins):
                    ins.then_inc(step, 1)
                    n[0] += 1
                    dve.wait_ge(step, n[0])

                dve.wait_ge(inp, 48)
                then(dve.tensor_tensor(a[:, :, :], ba[:, :, H:], bias[:, :].rearrange("p (o h) -> p o h", o=1).to_broadcast([P, NT + 1, H]), ALU.add))
                then(dve.tensor_scalar(neg[:, :, :], a[:, :, :], -1.0, None, ALU.mult))
                then(dve.tensor_tensor(neg[:, :, :], neg[:, :, :], a[:, :, :], ALU.min))
                dve.wait_ge(acts, 3)
                then(dve.tensor_scalar(neg[:, :, :], neg[:, :, :], 1.0, None, ALU.add))
                dve.wait_ge(acts, 4)
                then(dve.scalar_tensor_tensor(g[:, :, :], a[:, :, :], 0.0, neg[:, :, :], ALU.max, ALU.add))
                then(dve.scalar_tensor_tensor(g[:, :, :], g[:, :, :], -1.0,
                                              alog[:, :].rearrange("p (o h) -> p o h", o=1).to_broadcast([P, NT + 1, H]), ALU.mult, ALU.mult))
                dve.wait_ge(summed, 1)
                then(dve.tensor_copy(cols[:, 2, :], psum[:, 0, 0:N]))
                then(dve.tensor_copy(ex[:, 0, :], cols[:, 2, :]))
                then(dve.tensor_tensor(ex[:, 1, :], psum[:, 1, 0:N], cols[:, 2, :], ALU.subtract))
                then(dve.tensor_copy(ex[:, 2, :], psum[:, 1, 0:N]))
                then(dve.tensor_copy(cols[:, 0, :], beta[:, 0:NT, :].rearrange("p t h -> p (t h)")))
                then(dve.tensor_copy(cols[:, 1, :], g[:, 0:NT, :].rearrange("p t h -> p (t h)")))
                dve.wait_ge(acts, 5)
                then(dve.tensor_tensor(cols[:, 3, :], cols[:, 0, :], ex[:, 0, :], ALU.mult))
                then(dve.tensor_copy(cols[:, 4:6, :], ex[:, 1:3, :]))
                sel = core.const[:NS, C_ID, 0:NS].rearrange("p (o b) -> p o b", o=1).to_broadcast([NS, H, NS])
                for j, src in enumerate((beta, g)):
                    then(dve.tensor_tensor(spread[:, j, :, :], sel, src[:NS, NT, :].rearrange("p (h o) -> p h o", o=1).to_broadcast([NS, H, NS]), ALU.mult))
                dve.wait_ge(acts, 6)
                then(dve.tensor_copy(srep[:, 0, :], psum[:, 2, 0:H * NS]))
                then(dve.tensor_tensor(srep[:, 2, :], srep[:, 0, :], srep[:, 1, :], ALU.mult))

            @block.tensor
            def _(pe):
                pe.wait_ge(step, 6)
                rows = g[:, 0:NT, :].rearrange("p t h -> p (t h)")
                pe.matmul(psum[:, 0, 0:N], core.const[:, C_UP, :], rows, start=True, stop=True)
                pe.matmul(psum[:, 1, 0:N], core.ones, rows, start=True, stop=True).then_inc(summed, 1)
                pe.wait_ge(step, 16)
                pe.matmul(psum[:, 2, :], core.ones[:NS, :], spread[:, :, :, :].rearrange("p a h b -> p (a h b)"), start=True, stop=True).then_inc(summed, 1)


def gdn_seq(core, F, cols, gout):
    nc = core.nc
    LV = LEVELS - 1

    def mask(j):
        return core.const[:, j:j + 1, :].to_broadcast([P, NT, P])

    def flat(tile):
        return tile[:, :, :].rearrange("p t c -> p (t c)")

    def col(kind, h):
        c = cols[:, kind, :].rearrange("p (t h) -> p t h", h=H)[:, :, ds(h, 1)]
        return c.to_broadcast([P, NT, P])

    with Marks(core, "seq", rowed=4, squared=4, staged=2, summed=2, rooted=4, diff=4, decay=4, masks=4, normed=10, signed=2,
               crossed=2, turned=2, products=4, scaled=6, seeded=4, flipped=2 * LV, flip_out=2 * LV, lmask=2 * LV, joined=2 * LV,
               joined_out=2 * LV, stepped=2 * LV, grown=2 * LV, wk=2, wk_out=2, u_made=2 * NT, u_out=2 * NT, s_made=2 * NT,
               state=2 * NT, o_made=2 * NT, stored=32, o_square=2, o_stat=6, o_root=2, o_norm=2, o_turned=2,
               gated=2) as s, ExitStack() as ctx:
        def two(name, shape=(P, NT, P)):
            return [core.sbuf(ctx, name, list(shape)) for _ in range(2)]

        gU, bI = two("gU"), two("bI")
        sqk, sqq, vT = two("sqk"), two("sqq"), two("vT")
        kT, qT, qdT = two("kT"), two("qT"), two("qdT")
        eG, dec, nA, qk = two("eG"), two("dec"), two("nA"), two("qk")
        Kb, kd, Vb, u = two("Kb"), two("kd"), two("Vb"), two("u")
        T, U, X = two("T"), two("U"), two("X")
        S = two("S", (P, NT + 1, P))
        st = two("st", (P, 3, NT))
        pA, pB, pC, pD = ([core.psum(ctx, n, [P, NT, P]) for _ in range(2)] for n in ("pA", "pB", "pC", "pD"))
        at = s.at

        with nc.Block() as block:
            @block.gpsimd
            def _(pool):
                with pool.Fori(0, H // 2) as i:
                    for a in range(2):
                        after(pool, at("joined", i, 0))
                        pool.tensor_tensor(gU[a][:, :, :], mask(C_UP), col(1, 2 * i + a), ALU.mult).then_inc(s["rowed"], 1)
                        pool.tensor_tensor(bI[a][:, :, :], mask(C_ID), col(0, 2 * i + a), ALU.mult).then_inc(s["rowed"], 1)
                    for a in range(2):
                        after(pool, at("decay", i, 2 * a + 2))
                        pool.tensor_tensor(dec[a][:, :, :], dec[a][:, :, :], mask(C_UP), ALU.mult).then_inc(s["masks"], 1)
                        after(pool, at("masks", i, 2 * a + 1), at("o_stat", i, 0))
                        pool.tensor_tensor(X[a][:, :, :], dec[a][:, :, :], mask(C_STRICT), ALU.mult).then_inc(s["masks"], 1)
                    for j in range(LV):
                        for a in range(2):
                            if j == 0:
                                after(pool, at("products", i, 2 * a + 1))
                            if j >= 2:
                                after(pool, at("joined", i, 2 * (j - 2) + a + 1))
                            pool.tensor_tensor((gU, bI)[j % 2][a][:, :, :], nA[a][:, :, :], mask(C_LEVEL + 1 + j), ALU.mult).then_inc(s["lmask"], 1)

            @block.scalar
            def _(act):
                with act.Fori(0, H // 2) as i:
                    for a in range(2):
                        h = 2 * i + a
                        after(act, at("normed", i, 0))
                        act.activation(flat(sqk[a]), part(F, h + H, SEQ), ACT.Square).then_inc(s["squared"], 1)
                        act.activation(flat(sqq[a]), part(F, h, SEQ), ACT.Square).then_inc(s["squared"], 1)
                        act.activation(flat(vT[a]), part(F, h + 2 * H, SEQ), ACT.Copy).then_inc(s["staged"], 1)
                    for a in range(2):
                        after(act, at("summed", i, a + 1))
                        act.activation(sqk[a][:, :, :], pC[a][:, :, :], ACT.Sqrt, bias=core.eps).then_inc(s["rooted"], 1)
                        act.activation(sqq[a][:, :, :], pD[a][:, :, :], ACT.Sqrt, bias=core.eps).then_inc(s["rooted"], 1)
                    for a in range(2):
                        after(act, at("diff", i, 2 * a + 2))
                        act.activation(eG[a][:, :, :], pA[a][:, :, :], ACT.Exp).then_inc(s["decay"], 1)
                        act.activation(dec[a][:, :, :], dec[a][:, :, :], ACT.Exp).then_inc(s["decay"], 1)
                    for j in range(LV):
                        for a in range(2):
                            after(act, at("flipped", i, 2 * j + a + 1))
                            act.activation(T[a][:, :, :], pC[a][:, :, :], ACT.Copy).then_inc(s["flip_out"], 1)
                        for a in range(2):
                            after(act, at("joined", i, 2 * j + a + 1))
                            act.activation(X[a][:, :, :], pA[a][:, :, :], ACT.Copy).then_inc(s["joined_out"], 1)
                    for a in range(2):
                        after(act, at("wk", i, a + 1))
                        act.activation(T[a][:, :, :], pA[a][:, :, :], ACT.Copy, scale=-1.0).then_inc(s["wk_out"], 1)
                    for a in range(2):
                        after(act, at("o_made", i, 2 * (NT - 1) + a + 1))
                        act.activation(X[a][:, :, :], pC[a][:, :, :], ACT.Square).then_inc(s["o_square"], 1)
                    for a in range(2):
                        after(act, at("o_stat", i, 3 * a + 2))
                        act.activation(st[a][:, 1, :], st[a][:, 1, :], ACT.Sqrt).then_inc(s["o_root"], 1)

            @block.tensor
            def _(pe):
                def each(out, lhs, rhs):
                    for t in range(NT):
                        last = pe.matmul(out[:, t, :], lhs[:, t, :], rhs[:, t, :], start=True, stop=True)
                    return last

                def turn(out, src):
                    for t in range(NT):
                        last = pe.transpose(out[:, t, :], src[:, t, :], core.ident)
                    return last

                with pe.Fori(0, H // 2) as i:
                    for a in range(2):
                        after(pe, at("rowed", i, 2 * a + 2), at("gated", i, 0), at("squared", i, 2 * a + 2))
                        pe.matmul(flat(pA[a]), core.ones, flat(gU[a]), start=True, stop=True)
                        pe.matmul(flat(pB[a]), core.ones, flat(bI[a]), start=True, stop=True)
                        pe.matmul(flat(pC[a]), core.ones, flat(sqk[a]), start=True, stop=True)
                        pe.matmul(flat(pD[a]), core.ones, flat(sqq[a]), start=True, stop=True).then_inc(s["summed"], 1)
                    for a in range(2):
                        after(pe, at("normed", i, 5 * a + 5))
                        each(pC[a], kT[a], kT[a])
                        each(pD[a], kT[a], qT[a]).then_inc(s["crossed"], 1)
                        turn(pA[a], kT[a])
                        after(pe, at("signed", i, a + 1), at("staged", i, a + 1))
                        turn(pB[a], vT[a]).then_inc(s["turned"], 1)
                    for j in range(LV):
                        for a in range(2):
                            after(pe, at("seeded", i, 2 * a + 2) if j == 0 else at("grown", i, 2 * (j - 1) + a + 1))
                            turn(pC[a], U[a]).then_inc(s["flipped"], 1)
                        for a in range(2):
                            after(pe, at("flip_out", i, 2 * j + a + 1), at("lmask", i, 2 * j + a + 1))
                            if j == 0:
                                after(pe, at("scaled", i, 3 * a + 3))
                            each(pA[a], (gU, bI)[j % 2][a], T[a]).then_inc(s["joined"], 1)
                        for a in range(2):
                            after(pe, at("joined_out", i, 2 * j + a + 1))
                            each(pB[a], X[a], U[a]).then_inc(s["stepped"], 1)
                    for a in range(2):
                        after(pe, at("grown", i, 2 * (LV - 1) + a + 1))
                        each(pA[a], Kb[a], U[a]).then_inc(s["wk"], 1)
                    for t in range(NT):
                        for a in range(2):
                            if t:
                                after(pe, at("state", i, 2 * (t - 1) + a + 1), at("wk_out", i, a + 1))
                            last = pe.matmul(pB[a][:, t, :], U[a][:, t, :], Vb[a][:, t, :], start=True, stop=t == 0)
                            if t:
                                last = pe.matmul(pB[a][:, t, :], T[a][:, t, :], S[a][:, t, :], start=False, stop=True)
                            last.then_inc(s["u_made"], 1)
                        for a in range(2):
                            after(pe, at("u_out", i, 2 * t + a + 1))
                            pe.matmul(pD[a][:, t, :], kd[a][:, t, :], u[a][:, t, :], start=True, stop=True).then_inc(s["s_made"], 1)
                        for a in range(2):
                            if t:
                                pe.matmul(pC[a][:, t, :], qdT[a][:, t, :], S[a][:, t, :], start=True, stop=False)
                            pe.matmul(pC[a][:, t, :], qk[a][:, t, :], u[a][:, t, :], start=t == 0, stop=True).then_inc(s["o_made"], 1)
                    for a in range(2):
                        after(pe, at("o_norm", i, a + 1))
                        turn(pA[a], kT[a]).then_inc(s["o_turned"], 1)

            @block.vector
            def _(dve):
                with dve.Fori(0, H // 2) as i:
                    for a in range(2):
                        h = 2 * i + a
                        after(dve, at("summed", i, a + 1), at("products", i, 0))
                        dve.tensor_tensor(dec[a][:, :, :], pA[a][:, :, :], col(2, h), ALU.min).then_inc(s["diff"], 1)
                        after(dve, at("diff", i, 2 * a + 1))
                        dve.tensor_tensor(dec[a][:, :, :], dec[a][:, :, :], col(2, h), ALU.subtract).then_inc(s["diff"], 1)
                    for a in range(2):
                        h = 2 * i + a
                        after(dve, at("rooted", i, 2 * a + 1))
                        dve.reciprocal(flat(sqk[a]), flat(sqk[a])).then_inc(s["normed"], 1)
                        after(dve, at("normed", i, 5 * a + 1), at("o_turned", i, 0))
                        dve.tensor_tensor(flat(kT[a]), part(F, h + H, SEQ), flat(sqk[a]), ALU.mult).then_inc(s["normed"], 1)
                        after(dve, at("rooted", i, 2 * a + 2))
                        dve.reciprocal(flat(sqq[a]), flat(sqq[a])).then_inc(s["normed"], 1)
                        after(dve, at("normed", i, 5 * a + 3))
                        dve.scalar_tensor_tensor(flat(qT[a]), part(F, h, SEQ), HD ** -0.5, flat(sqq[a]), ALU.mult, ALU.mult).then_inc(s["normed"], 1)
                        after(dve, at("normed", i, 5 * a + 4), at("decay", i, 2 * a + 1))
                        dve.tensor_tensor(qdT[a][:, :, :], qT[a][:, :, :], eG[a][:, :, :], ALU.mult).then_inc(s["normed"], 1)
                        after(dve, at("masks", i, 2 * a + 2))
                        dve.scalar_tensor_tensor(flat(nA[a]), flat(pB[a]), -1.0, flat(X[a]), ALU.mult, ALU.mult).then_inc(s["signed"], 1)
                    for a in range(2):
                        h = 2 * i + a
                        after(dve, at("crossed", i, a + 1), at("signed", i, a + 1))
                        dve.tensor_tensor(nA[a][:, :, :], pC[a][:, :, :], nA[a][:, :, :], ALU.mult).then_inc(s["products"], 1)
                        dve.tensor_tensor(qk[a][:, :, :], pD[a][:, :, :], dec[a][:, :, :], ALU.mult).then_inc(s["products"], 1)
                        after(dve, at("products", i, 2 * a + 1))
                        dve.tensor_tensor(U[a][:, :, :], nA[a][:, :, :], mask(C_LEVEL), ALU.mult).then_inc(s["seeded"], 1)
                        after(dve, at("seeded", i, 2 * a + 1))
                        dve.tensor_tensor(U[a][:, :, :], U[a][:, :, :], mask(C_ID), ALU.add).then_inc(s["seeded"], 1)
                        after(dve, at("turned", i, a + 1))
                        dve.tensor_tensor(Kb[a][:, :, :], pA[a][:, :, :], col(3, h), ALU.mult).then_inc(s["scaled"], 1)
                        dve.tensor_tensor(kd[a][:, :, :], pA[a][:, :, :], col(4, h), ALU.mult).then_inc(s["scaled"], 1)
                        dve.tensor_tensor(Vb[a][:, :, :], pB[a][:, :, :], col(0, h), ALU.mult).then_inc(s["scaled"], 1)
                    for j in range(LV):
                        for a in range(2):
                            after(dve, at("stepped", i, 2 * j + a + 1))
                            dve.tensor_tensor(U[a][:, :, :], pB[a][:, :, :], U[a][:, :, :], ALU.add).then_inc(s["grown"], 1)
                    for t in range(NT):
                        for a in range(2):
                            after(dve, at("u_made", i, 2 * t + a + 1))
                            dve.tensor_copy(u[a][:, t, :], pB[a][:, t, :]).then_inc(s["u_out"], 1)
                        for a in range(2):
                            after(dve, at("s_made", i, 2 * t + a + 1), at("stored", i, 0))
                            if t == 0:
                                dve.tensor_copy(S[a][:, 1, :], pD[a][:, 0, :]).then_inc(s["state"], 1)
                            else:
                                after(dve, at("state", i, 2 * (t - 1) + a + 1))
                                dve.scalar_tensor_tensor(S[a][:, t + 1, :], S[a][:, t, :], part(cols, 2 * i + a + (5 * NT * H + t * H), 1),
                                                         pD[a][:, t, :], ALU.mult, ALU.add).then_inc(s["state"], 1)
                    for a in range(2):
                        after(dve, at("o_square", i, a + 1))
                        dve.tensor_reduce(st[a][:, 0, :], X[a][:, :, :], AX.X, ALU.add).then_inc(s["o_stat"], 1)
                        after(dve, at("o_stat", i, 3 * a + 1))
                        dve.tensor_scalar(st[a][:, 1, :], st[a][:, 0, :], 1.0 / HD, EPS, ALU.mult, ALU.add).then_inc(s["o_stat"], 1)
                        after(dve, at("o_root", i, a + 1))
                        dve.reciprocal(st[a][:, 2, :], st[a][:, 1, :]).then_inc(s["o_stat"], 1)
                        after(dve, at("o_stat", i, 3 * a + 3))
                        dve.tensor_tensor(kT[a][:, :, :], pC[a][:, :, :],
                                          st[a][:, 2, :].rearrange("p (t o) -> p t o", o=1).to_broadcast([P, NT, P]), ALU.mult).then_inc(s["o_norm"], 1)
                    for a in range(2):
                        h = 2 * i + a
                        after(dve, at("o_turned", i, a + 1))
                        dve.scalar_tensor_tensor(part(F, h, SEQ), flat(pA[a]), gout[:, 0:1], part(F, h + 3 * H, SEQ), ALU.mult, ALU.mult).then_inc(s["gated"], 1)

            @block.sync
            def _(sp):
                with sp.Fori(0, H // 2) as i:
                    for a in range(2):
                        after(sp, at("state", i, 2 * (NT - 1) + a + 1))
                        sp.dma_start(core.o["ssm_p"][ds(2 * i + a, 1), :, :].rearrange("o k v -> (o k) v"), S[a][:, NT, :]).then_inc(s["stored"], 16)
                sp.wait_ge(s["stored"], 16 * H)


def gdn_dec(core, Fs, srep, gout, os):
    nc = core.nc
    G, N = 4, H * NS
    with Marks(core, "dec", square=3, sums=2, root=2, prep=7, spread=4, state=1, landed0=16, landed1=16, u_made=2, tmp=6,
               o_made=2, o_out=2, stored=32, post=6) as s, ExitStack() as ctx:
        at = s.at
        q = core.sbuf(ctx, "q", [P, N])
        k = core.sbuf(ctx, "k", [P, N])
        nkb = core.sbuf(ctx, "nkb", [P, N])
        bv = core.sbuf(ctx, "bv", [P, N])
        sq = core.sbuf(ctx, "sq", [P, 2 * N])
        o = core.sbuf(ctx, "o", [P, N])
        S0 = [core.sbuf(ctx, "S0", [P, G, P]) for _ in range(2)]
        S1 = [core.sbuf(ctx, "S1", [P, G, P]) for _ in range(2)]
        t1 = [core.sbuf(ctx, "t1", [P, G, P]) for _ in range(2)]
        nkB = [core.sbuf(ctx, "nkB", [P, G, P]) for _ in range(2)]
        bvB = [core.sbuf(ctx, "bvB", [P, G, P]) for _ in range(2)]
        pS = core.psum(ctx, "pS", [P, 2 * N])
        pU = [core.psum(ctx, "pU", [P, G, P]) for _ in range(2)]
        pO = [core.psum(ctx, "pO", [P, G]) for _ in range(2)]
        f = Fs[:, :, :].rearrange("p c b -> p (c b)")

        def wide(tile, g):
            return part(tile, g, G).rearrange("p (j o) -> p j o", o=1).to_broadcast([P, G, P])

        with nc.Block() as block:
            @block.sync
            def _(sp):
                with sp.Fori(0, N // G // 2) as i:
                    for a in range(2):
                        after(sp, at("tmp", i, 0))
                        sp.dma_start(S0[a][:, :, :], core.i["state_ssm"][ds((2 * i + a) * G, G), :, :].rearrange("j k v -> k j v")).then_inc(s[f"landed{a}"], 16)
                    for a in range(2):
                        after(sp, at("tmp", i, 3 * a + 3))
                        sp.dma_start(core.o["ssm_s"][ds((2 * i + a) * G, G), :, :].rearrange("j k v -> k j v"), S1[a][:, :, :]).then_inc(s["stored"], 16)
                sp.wait_ge(s["stored"], 16 * (N // G))

            @block.gpsimd
            def _(pool):
                pool.wait_ge(s["prep"], 5)
                with pool.Fori(0, N // G // 2) as i:
                    for a in range(2):
                        after(pool, at("u_made", i, 0))
                        pool.tensor_copy(nkB[a][:, :, :], wide(nkb, 2 * i + a)).then_inc(s["spread"], 1)
                        pool.tensor_copy(bvB[a][:, :, :], wide(bv, 2 * i + a)).then_inc(s["spread"], 1)

            @block.scalar
            def _(act):
                act.activation(sq[:, :], f[:, 0:2 * N], ACT.Square).then_inc(s["square"], 1)
                act.wait_ge(s["sums"], 1)
                act.activation(sq[:, :], pS[:, :], ACT.Sqrt, bias=core.eps).then_inc(s["root"], 1)
                with act.Fori(0, N // G // 2) as i:
                    for a in range(2):
                        after(act, at("o_made", i, a + 1))
                        act.activation(part(o, 2 * i + a, G), pO[a][:, :], ACT.Copy).then_inc(s["o_out"], 1)
                act.wait_ge(s["o_out"], N // G)
                act.activation(sq[:, 0:N], o[:, :], ACT.Square).then_inc(s["square"], 1)
                act.wait_ge(s["post"], 1)
                act.activation(sq[:, 0:N], sq[:, 0:N], ACT.Sqrt).then_inc(s["root"], 1)

            @block.tensor
            def _(pe):
                pe.wait_ge(s["square"], 1)
                pe.matmul(pS[:, :], core.ones, sq[:, :], start=True, stop=True).then_inc(s["sums"], 1)
                pe.wait_ge(s["prep"], 5)
                with pe.Fori(0, N // G // 2) as i:
                    for a in range(2):
                        after(pe, (s[f"landed{a}"], i * 16 + 16), at("spread", i, 2 * a + 2), at("tmp", i, 0))
                        for j in range(G):
                            pe.matmul(pU[a][:, j, :], nkB[a][:, j, :], S0[a][:, j, :], start=True, stop=False)
                            last = pe.matmul(pU[a][:, j, :], bvB[a][:, j, :], core.ident, start=False, stop=True)
                        last.then_inc(s["u_made"], 1)
                    for a in range(2):
                        after(pe, at("tmp", i, 3 * a + 3), at("o_out", i, 0))
                        for j in range(G):
                            last = pe.matmul(pO[a][:, j:j + 1], S1[a][:, j, :], q[:, ds((2 * i + a) * G + j, 1)], start=True, stop=True)
                        last.then_inc(s["o_made"], 1)
                pe.wait_ge(s["square"], 2)
                pe.matmul(pS[:, 0:N], core.ones, sq[:, 0:N], start=True, stop=True).then_inc(s["sums"], 1)

            @block.vector
            def _(dve):
                dve.wait_ge(s["root"], 1)
                dve.reciprocal(sq[:, :], sq[:, :]).then_inc(s["prep"], 1)
                dve.wait_ge(s["prep"], 1)
                dve.scalar_tensor_tensor(q[:, :], f[:, 0:N], HD ** -0.5, sq[:, 0:N], ALU.mult, ALU.mult).then_inc(s["prep"], 1)
                dve.tensor_tensor(k[:, :], f[:, N:2 * N], sq[:, N:2 * N], ALU.mult).then_inc(s["prep"], 1)
                dve.wait_ge(s["prep"], 3)
                dve.scalar_tensor_tensor(nkb[:, :], k[:, :], -1.0, srep[:, 2, :], ALU.mult, ALU.mult).then_inc(s["prep"], 1)
                dve.tensor_tensor(bv[:, :], f[:, 2 * N:3 * N], srep[:, 0, :], ALU.mult).then_inc(s["prep"], 1)
                with dve.Fori(0, N // G // 2) as i:
                    for a in range(2):
                        g = 2 * i + a
                        after(dve, at("u_made", i, a + 1), at("stored", i, 0), at("o_made", i, 0))
                        dve.tensor_tensor(t1[a][:, :, :], pU[a][:, :, :], wide(k, g), ALU.mult).then_inc(s["tmp"], 1)
                        dve.tensor_tensor(S1[a][:, :, :], S0[a][:, :, :],
                                          srep[:, 1, :][:, ds(g * G, G)].rearrange("p (j o) -> p j o", o=1).to_broadcast([P, G, P]), ALU.mult).then_inc(s["tmp"], 1)
                        after(dve, at("tmp", i, 3 * a + 2))
                        dve.tensor_tensor(S1[a][:, :, :], S1[a][:, :, :], t1[a][:, :, :], ALU.add).then_inc(s["tmp"], 1)
                dve.wait_ge(s["sums"], 2)
                dve.tensor_scalar(sq[:, 0:N], pS[:, 0:N], 1.0 / HD, EPS, ALU.mult, ALU.add).then_inc(s["post"], 1)
                dve.wait_ge(s["root"], 2)
                dve.reciprocal(sq[:, 0:N], sq[:, 0:N]).then_inc(s["post"], 1)
                dve.wait_ge(s["post"], 2)
                dve.tensor_tensor(o[:, :], o[:, :], sq[:, 0:N], ALU.mult).then_inc(s["post"], 1)
                dve.wait_ge(s["post"], 3)
                dve.scalar_tensor_tensor(os[:, :], o[:, :], gout[:, 0:1], f[:, 3 * N:4 * N], ALU.mult, ALU.mult).then_inc(s["post"], 1)


def out_proj(core, rows, weight):
    nc = core.nc
    HALF = D // 2
    B = 4
    with Marks(core, "out", landed0=16, landed1=16, made=1, added=1) as s, ExitStack() as ctx:
        w = core.sbuf(ctx, "w", [P, KD, D])
        bank = [core.psum(ctx, "bank", [P, HALF]) for _ in range(B)]
        with nc.Block() as block:
            @block.sync
            def _(sp):
                for c in range(2):
                    sp.dma_start(w[:, :, HALF * c:HALF * c + HALF], weight.rearrange("(k p) n -> p k n", p=P)[:, :, HALF * c:HALF * c + HALF]).then_inc(s[f"landed{c}"], 16)

            @block.tensor
            def _(pe):
                for c in range(2):
                    pe.wait_ge(s[f"landed{c}"], 16)
                    for t in range(NT + 1):
                        j = c * (NT + 1) + t
                        n = P if t < NT else NS
                        if j >= B:
                            pe.wait_ge(s["added"], j - B + 1)
                        for k in range(KD):
                            last = pe.matmul(bank[j % B][:n, :], rows(k, t), w[:, k, HALF * c:HALF * c + HALF], start=k == 0, stop=k == KD - 1)
                        last.then_inc(s["made"], 1)

            @block.vector
            def _(dve):
                for c in range(2):
                    for t in range(NT + 1):
                        j = c * (NT + 1) + t
                        x, n = rows_of(core, t)
                        x = x[:, HALF * c:HALF * c + HALF]
                        dve.wait_ge(s["made"], j + 1)
                        dve.tensor_tensor(x, bank[j % B][:n, :], x, ALU.add).then_inc(s["added"], 1)


GRP_C = 4
WEIGH_G = 1
TOP_STEPS = 27
TOP_HALF = 10
TOP_LOW = 18


class TopK:

    def __init__(self, core, ctx, n):
        sb = core.sbuf
        self.n = n
        self.sv = sb(ctx, "sv", [n, 2, TOPK])
        self.si = sb(ctx, "si", [n, 2, TOPK], U32)
        self.sif = sb(ctx, "sif", [n, 2, TOPK])
        self.rest = sb(ctx, "rest", [n, 2, NK])
        self.cand = sb(ctx, "cand", [n, TOPK, TOPK])
        self.crest = sb(ctx, "crest", [n, TOPK, TOPK])
        self.tv = sb(ctx, "tv", [n, TOPK])
        self.ti = sb(ctx, "ti", [n, TOPK], U32)
        self.tab = sb(ctx, "tab", [n, 2, TOPK], U32)
        self.tabf = sb(ctx, "tabf", [n, 2, TOPK])
        self.hit = sb(ctx, "hit", [n, 2, TOPK, TOPK])
        self.pick = sb(ctx, "pick", [n, 2, TOPK])
        self.low = sb(ctx, "low", [n, 1])
        self.e = sb(ctx, "e", [n, TOPK])
        self.z = sb(ctx, "z", [n, 2])


def top_k(dve, s, name, v, k, scores, counting, index, half):
    n = k.n
    done = [TOP_HALF * half]

    def step(ins):
        ins.then_inc(s[name], 1)
        done[0] += 1

    def then(ins):
        step(ins)
        apart(dve, s.at(name, v, done[0]))

    def best(lots):
        for values, numbers, data, rest in lots:
            last = dve.max(values[:, 0:8], data)
            (then if data is lots[-1][2] else step)(last)
        for values, numbers, data, rest in lots:
            step(dve.max_index(numbers[:, 0:8], values[:, 0:8], data))
        for values, numbers, data, rest in lots:
            last = dve.match_replace(rest, values[:, 0:8], data, -3.0e38)
            (then if data is lots[-1][2] else step)(last)
        for values, numbers, data, rest in lots:
            last = dve.max(values[:, 8:16], rest)
            (then if data is lots[-1][2] else step)(last)
        for values, numbers, data, rest in lots:
            last = dve.max_index(numbers[:, 8:16], values[:, 8:16], rest)
            (then if data is lots[-1][2] else step)(last)

    def wide(col):
        return col.rearrange("p (a o) -> p a o", o=1).to_broadcast([n, TOPK, TOPK])

    if half == 0:
        best([(k.sv[:, p, :], k.si[:, p, :], scores[:n, p, :], k.rest[:, p, :]) for p in range(2)])
        assert done[0] == TOP_HALF, done[0]
        return
    step(dve.tensor_copy(k.sif[:, :, :], k.si[:, :, :]))
    then(dve.tensor_tensor(k.cand[:, :, :], wide(k.sv[:, 0, :]), k.sv[:, 1:2, :].to_broadcast([n, TOPK, TOPK]), ALU.add))
    best([(k.tv[:, :], k.ti[:, :], k.cand[:, :, :].rearrange("p a b -> p (a b)"), k.crest[:, :, :].rearrange("p a b -> p (a b)"))])
    step(dve.tensor_scalar(k.low[:, :], k.tv[:, 0:1], -1.0, None, ALU.mult))
    assert done[0] == TOP_LOW
    step(dve.tensor_scalar(k.tab[:, 0, :], k.ti[:, :], 4, None, ALU.logical_shift_right))
    then(dve.tensor_scalar(k.tab[:, 1, :], k.ti[:, :], TOPK - 1, None, ALU.bitwise_and))
    then(dve.tensor_copy(k.tabf[:, :, :], k.tab[:, :, :]))
    for p in range(2):
        last = dve.tensor_tensor(k.hit[:, p, :, :], wide(k.tabf[:, p, :]),
                                 counting[:n, :].rearrange("p (o b) -> p o b", o=1).to_broadcast([n, TOPK, TOPK]), ALU.is_equal)
        (then if p else step)(last)
    for p in range(2):
        last = dve.tensor_tensor(k.hit[:, p, :, :], k.hit[:, p, :, :], k.sif[:, p:p + 1, :].to_broadcast([n, TOPK, TOPK]), ALU.mult)
        (then if p else step)(last)
    then(dve.tensor_reduce(k.pick[:, :, :], k.hit[:, :, :, :], AX.X, ALU.add))
    step(dve.scalar_tensor_tensor(index, k.pick[:, 0, :], float(NK), k.pick[:, 1, :], ALU.mult, ALU.add))
    assert done[0] == TOP_STEPS, done[0]


def peer(core, xn, xns, xnT, weight, keys, uv):
    nc = core.nc
    HALF = D // 2
    GRPS = TOPK // GRP_C
    UNITS = NT * H
    with Marks(core, "peer", inp=48, w0=16, w1=16, q_made=2, q_out=4, scored=1, top=TOP_STEPS, exped=1, gate=2, spread=1,
               dot=TOPK, gelu=GRPS, diag=TOPK, pv=TOPK, added=1, sscored=1, stop=TOP_STEPS, sexped=1, sgate=2, flip=1,
               flipped=2, rowed=1, sdot=1, sgelu=1, sact=2, spv=1, sadded=1,
               **{f"landed{r}": 32 for r in range(RING)}) as s, ExitStack() as ctx:
        at = s.at
        w = core.sbuf(ctx, "w", [P, 2, KD, P])
        q = core.sbuf(ctx, "q", [P, 2, ROWS])
        sk = core.sbuf(ctx, "sk", [P, 2 * H, NK])
        counting = core.sbuf(ctx, "counting", [P, TOPK])
        same = core.sbuf(ctx, "same", [P, NS, NS])
        ring = core.sbuf(ctx, "ring", [P, RING, 2 * D])
        k = TopK(core, ctx, P)
        idx = [core.sbuf(ctx, "idx", [P, TOPK], U32) for _ in range(2)]
        gate = core.sbuf(ctx, "gate", [P, TOPK])
        gated = [core.sbuf(ctx, "gated", [P, TOPK, P]) for _ in range(2)]
        hs = [core.sbuf(ctx, "hs", [P, TOPK]) for _ in range(2)]
        hg = [core.sbuf(ctx, "hg", [P, TOPK]) for _ in range(2)]
        diag = core.sbuf(ctx, "diag", [P, RING, P])
        ks = TopK(core, ctx, NS)
        sidx = core.sbuf(ctx, "sidx", [NS, H * TOPK])
        sgate = core.sbuf(ctx, "sgate", [NS, H * TOPK])
        sidxT = core.sbuf(ctx, "sidxT", [P, NS], U32)
        sgateT = core.sbuf(ctx, "sgateT", [P, NS])
        shs = core.sbuf(ctx, "shs", [P, 3, NS])
        sac = core.sbuf(ctx, "sac", [P, NS, NS])
        pS = core.psum(ctx, "pS", [P, 2, NK])
        pT = core.psum(ctx, "pT", [P, 2, NK])
        pq = core.psum(ctx, "pq", [P, SEQ])
        pqs = core.psum(ctx, "pqs", [P, NS])
        po = [core.psum(ctx, "po", [P, D]) for _ in range(2)]

        def turns(eng, head):
            head(0, True, False)
            with eng.Fori(1, H - 1) as h:
                head(h, False, False)
            head(H - 1, False, True)

        with nc.Block() as block:
            @block.sync
            def _(sp):
                for p in range(2):
                    sp.dma_start(w[:, p, :, :], weight[p]).then_inc(s[f"w{p}"], 16)
                sp.dma_start(sk[:, :, :], keys).then_inc(s["inp"], 16)
                sp.dma_start(counting[:, :], core.i["counting"]).then_inc(s["inp"], 16)
                sp.dma_start(same[:, :, :], core.i["same"]).then_inc(s["inp"], 16)
                with sp.Fori(1, H) as h:
                    for p in range(2):
                        after(sp, at("q_made", h - 1, p + 1))
                        sp.dma_start(w[:, p, :, :], weight[ds(2 * h + p, 1), :, :, :].rearrange("o p k n -> (o p) k n")).then_inc(s[f"w{p}"], 16)

            @block.gpsimd
            def _(pool):
                def head(h, first, last):
                    for t in range(NT):
                        u = NT * h + t
                        apart(pool, at("top", u, TOP_STEPS))
                        for c in range(TOPK):
                            if c >= RING or t or not first:
                                apart(pool, at("pv", u, c - RING + 1))
                            pool.indirect_dma_start(out=ring[:, c % RING, :], out_offset=None, in_=uv,
                                                    in_offset=bass.IndirectOffsetOnAxis(ap=idx[t % 2][:, c:c + 1], axis=0)).then_inc(s[f"landed{c % RING}"], 16)

                turns(pool, head)
                pool.wait_ge(s["flipped"], 2)
                for j in range(NS):
                    pool.wait_ge(s["pv"], UNITS * TOPK - RING + j + 1)
                    pool.indirect_dma_start(out=ring[:, j, :], out_offset=None, in_=uv,
                                            in_offset=bass.IndirectOffsetOnAxis(ap=sidxT[:, j:j + 1], axis=0)).then_inc(s[f"landed{j}"], 16)

            @block.scalar
            def _(act):
                def queries(h, p):
                    after(act, at("q_made", h, p + 1))
                    if not isinstance(h, int) or h:
                        after(act, at("scored", NT * h - 1, 1), at("sscored", h, 0))
                    act.activation(q[:, p, 0:SEQ], pq[:, :], ACT.Copy).then_inc(s["q_out"], 1)
                    act.activation(q[:, p, SEQ:], pqs[:, :], ACT.Copy).then_inc(s["q_out"], 1)

                def weigh(v):
                    after(act, at("top", v, TOP_LOW), at("gate", v, 0))
                    act.activation(k.e[:, :], k.tv[:, :], ACT.Exp, bias=k.low[:, 0:1], accum_out=k.z[:, 0:1]).then_inc(s["exped"], 1)

                queries(0, 0)
                queries(0, 1)
                weigh(0)

                def head(h, first, last):
                    for t in range(NT):
                        u, a = NT * h + t, t % 2
                        if t == 2 and not last:
                            queries(h + 1, 0)
                        for g in range(GRPS):
                            after(act, at("dot", u, GRP_C * (g + 1)))
                            act.activation(hg[a][:, GRP_C * g:GRP_C * g + GRP_C], hs[a][:, GRP_C * g:GRP_C * g + GRP_C], ACT.Gelu).then_inc(s["gelu"], 1)
                            after(act, at("gelu", u, g + 1), at("spread", u, 1))
                            for c in range(GRP_C * g, GRP_C * g + GRP_C):
                                if c == RING or c == 0:
                                    after(act, at("pv", u, c - RING + GRP_C) if c or t or not first else (s["pv"], 0))
                                act.activation(diag[:, c % RING, :], gated[a][:, c, :], ACT.Copy, scale=hg[a][:, c:c + 1]).then_inc(s["diag"], 1)
                            if g == WEIGH_G and not (last and t == NT - 1):
                                weigh(u + 1)
                            if g == WEIGH_G and t == 2:
                                after(act, at("stop", h, TOP_LOW), at("sgate", h, 0))
                                act.activation(ks.e[:, :], ks.tv[:, :], ACT.Exp, bias=ks.low[:, 0:1], accum_out=ks.z[:, 0:1]).then_inc(s["sexped"], 1)
                        if t == 2 and not last:
                            queries(h + 1, 1)

                turns(act, head)
                act.wait_ge(s["sdot"], NS)
                act.activation(shs[:, 1, :], shs[:, 0, :], ACT.Gelu).then_inc(s["sgelu"], 1)

            @block.vector
            def _(dve):
                def weighed(v, b):
                    after(dve, at("exped", v, 1))
                    dve.reciprocal(k.z[:, 1:2], k.z[:, 0:1]).then_inc(s["gate"], 1)
                    after(dve, at("gate", v, 1))
                    dve.tensor_scalar(gate[:, :], k.e[:, :], k.z[:, 1:2], None, ALU.mult).then_inc(s["gate"], 1)
                    after(dve, at("gate", v, 2))
                    dve.tensor_tensor(gated[b][:, :, :], core.const[:, C_ID:C_ID + 1, :].to_broadcast([P, TOPK, P]),
                                      gate[:, :].rearrange("p (c o) -> p c o", o=1).to_broadcast([P, TOPK, P]), ALU.mult).then_inc(s["spread"], 1)

                def retrieve(v, b, half):
                    if half == 0:
                        apart(dve, at("scored", v, 1), at("exped", v, 0))
                    top_k(dve, s, "top", v, k, pS, counting, idx[b][:, :], half)

                dve.wait_ge(s["inp"], 48)
                retrieve(0, 0, 0)
                retrieve(0, 0, 1)
                weighed(0, 0)

                def add(u, t):
                    after(dve, at("pv", u, TOPK))
                    dve.tensor_tensor(core.x[:, t, :], po[t % 2][:, :], core.x[:, t, :], ALU.add).then_inc(s["added"], 1)

                def head(h, first, last):
                    for t in range(NT):
                        u, a = NT * h + t, t % 2
                        more = not (last and t == NT - 1)
                        for c in range(TOPK):
                            after(dve, at(f"landed{c % RING}", u, 16 * (c // RING + 1)))
                            dve.scalar_tensor_tensor(ring[:, c % RING, 0:D], ring[:, c % RING, 0:D], 1.0, xn[:, t, :],
                                                     ALU.mult, ALU.mult, accum_out=hs[a][:, c:c + 1]).then_inc(s["dot"], 1)
                            if c == 3 and more:
                                retrieve(u + 1, 1 - a, 0)
                            if c == 7 and more:
                                retrieve(u + 1, 1 - a, 1)
                            if c == 11:
                                if t or not first:
                                    add(u - 1, (t - 1) % NT)
                                if more:
                                    weighed(u + 1, 1 - a)
                            if c == 13 and t == 0:
                                apart(dve, at("sscored", h, 1), at("sexped", h, 0))
                                top_k(dve, s, "stop", h, ks, pT, counting, part(sidx, h, TOPK), 0)
                            if c == 13 and t == 1:
                                top_k(dve, s, "stop", h, ks, pT, counting, part(sidx, h, TOPK), 1)
                            if c == 13 and t == 2:
                                after(dve, at("sexped", h, 1))
                                dve.reciprocal(ks.z[:, 1:2], ks.z[:, 0:1]).then_inc(s["sgate"], 1)
                                after(dve, at("sgate", h, 1))
                                dve.tensor_scalar(part(sgate, h, TOPK), ks.e[:, :], ks.z[:, 1:2], None, ALU.mult).then_inc(s["sgate"], 1)

                turns(dve, head)
                add(UNITS - 1, NT - 1)
                dve.wait_ge(s["flip"], 1)
                dve.tensor_copy(sidxT[:, :], pT[:, 0, 0:NS]).then_inc(s["flipped"], 1)
                dve.tensor_copy(sgateT[:, :], pT[:, 1, 0:NS]).then_inc(s["flipped"], 1)
                for b in range(NS):
                    dve.wait_ge(s["rowed"], b + 1)
                    dve.wait_ge(s[f"landed{b}"], 32 * UNITS + 16)
                    dve.scalar_tensor_tensor(ring[:, b, 0:D], ring[:, b, 0:D], 1.0, po[b % 2][:, :], ALU.mult, ALU.mult,
                                             accum_out=shs[:, 0, b:b + 1]).then_inc(s["sdot"], 1)
                dve.wait_ge(s["sgelu"], 1)
                dve.wait_ge(s["flipped"], 2)
                dve.tensor_tensor(shs[:, 2, :], shs[:, 1, :], sgateT[:, :], ALU.mult).then_inc(s["sact"], 1)
                dve.wait_ge(s["sact"], 1)
                dve.tensor_tensor(sac[:, :, :], same[:, :, :], shs[:, 2, :].rearrange("p (b o) -> p b o", o=1).to_broadcast([P, NS, NS]), ALU.mult).then_inc(s["sact"], 1)
                dve.wait_ge(s["spv"], 1)
                dve.tensor_tensor(core.xs[:, :], po[0][:NS, :], core.xs[:, :], ALU.add).then_inc(s["sadded"], 1)

            @block.tensor
            def _(pe):
                def queries(h, p, k0, k1):
                    if k0 == 0:
                        after(pe, at(f"w{p}", h, 16), at("q_out", h, 2 * p))
                    for j in range(k0, k1):
                        pe.matmul(pq[:, :], w[:, p, j, :], xnT[:, j, 0:SEQ], start=j == 0, stop=j == KD - 1)
                        last = pe.matmul(pqs[:, :], w[:, p, j, :], xnT[:, j, SEQ:ROWS], start=j == 0, stop=j == KD - 1)
                    if k1 == KD:
                        last.then_inc(s["q_made"], 1)

                def score(v, h, t):
                    after(pe, at("q_out", h, 4), at("top", v, 0))
                    for p in range(2):
                        last = pe.matmul(pS[:, p, :], q[:, p, P * t:P * t + P], sk[:, :, :].rearrange("p s n -> p (s n)")[:, ds(h * (2 * NK) + p * NK, NK)], start=True, stop=True)
                    last.then_inc(s["scored"], 1)

                queries(0, 0, 0, KD)
                queries(0, 1, 0, KD)
                pe.wait_ge(s["inp"], 48)
                score(0, 0, 0)

                def head(h, first, last_head):
                    for t in range(NT):
                        u, a = NT * h + t, t % 2
                        if t < NT - 1:
                            score(u + 1, h, t + 1)
                        elif not last_head:
                            score(u + 1, h + 1, 0)
                        if t >= 2 or not first:
                            after(pe, at("added", u - 1, 0))
                        for c in range(TOPK):
                            after(pe, at("diag", u, c + 1))
                            for e in range(2):
                                last = pe.matmul(po[a][:, HALF * e:HALF * e + HALF], diag[:, c % RING, :], ring[:, c % RING, D + HALF * e:D + HALF * e + HALF],
                                                 start=c == 0, stop=c == TOPK - 1)
                            last.then_inc(s["pv"], 1)
                            if c == 1 and t == 0:
                                apart(pe, at("stop", h, 0))
                                for p in range(2):
                                    last = pe.matmul(pT[:NS, p, :], q[:, p, SEQ:], sk[:, :, :].rearrange("p s n -> p (s n)")[:, ds(h * (2 * NK) + p * NK, NK)], start=True, stop=True)
                                last.then_inc(s["sscored"], 1)
                            if t == 1 and c % 4 == 3 and not last_head:
                                queries(h + 1, 0, c // 2 - 1, c // 2 + 1)
                            if t == 2 and 3 <= c < 11 and not last_head:
                                queries(h + 1, 1, c - 3, c - 2)

                turns(pe, head)
                pe.wait_ge(s["sgate"], 2 * H)
                pe.transpose(pT[:, 0, 0:NS], sidx[:, :], core.const[:NS, C_ID, 0:NS])
                pe.transpose(pT[:, 1, 0:NS], sgate[:, :], core.const[:NS, C_ID, 0:NS]).then_inc(s["flip"], 1)
                pe.wait_ge(s["added"], UNITS)
                for b in range(NS):
                    if b >= 2:
                        pe.wait_ge(s["sdot"], b - 1)
                    for e in range(2):
                        last = pe.matmul(po[b % 2][:, HALF * e:HALF * e + HALF], core.const[:NS, C_ID, b:b + 1].to_broadcast([NS, P]),
                                         xns[:, HALF * e:HALF * e + HALF], start=True, stop=True)
                    last.then_inc(s["rowed"], 1)
                pe.wait_ge(s["sact"], 2)
                for e in range(2):
                    for b in range(NS):
                        last = pe.matmul(po[0][:NS, HALF * e:HALF * e + HALF], sac[:, b, :], ring[:, b, D + HALF * e:D + HALF * e + HALF], start=b == 0, stop=b == NS - 1)
                last.then_inc(s["spv"], 1)


SCALE = QK ** -0.5


def turned_by(x, cos, sin, t1, t2, rope):
    def half(a, j):
        return a[:, :, j:j + 1, :]
    return [lambda dve: dve.tensor_tensor(t1, x, cos, ALU.mult),
            lambda dve: dve.tensor_tensor(half(t2, 0), half(x, 1), half(sin, 0), ALU.mult),
            lambda dve: dve.tensor_tensor(half(t2, 1), half(x, 0), half(sin, 1), ALU.mult),
            lambda dve: dve.tensor_tensor(rope, t1, t2, ALU.add)]


def mla_in(core, xnT, lat, kr, cqT, ckvT, krTs, cos, sin):
    nc = core.nc
    T = NT + 1
    HR = RD // 2
    with Marks(core, "min", w=32, gain=64, proj=1, square=2, mean=1, root=1, inv=1, normed=2, rope=4, turned=1, copied=3,
               stored=32) as s, ExitStack() as ctx:
        at = s.at
        w = core.sbuf(ctx, "w", [P, KD, MIN])
        gq = core.sbuf(ctx, "gq", [P, QL])
        gk = core.sbuf(ctx, "gk", [P, KL])
        junk = core.sbuf(ctx, "junk", [P, QL + KL])
        st = core.sbuf(ctx, "st", [P, T, 3, 2])
        cq = core.sbuf(ctx, "cq", [P, T, QL])
        t1 = core.sbuf(ctx, "t1", [P, T, RD])
        t2 = core.sbuf(ctx, "t2", [P, T, RD])
        pq = [core.psum(ctx, "pq", [P, QL]) for _ in range(2)]
        pk = [core.psum(ctx, "pk", [P, KL + RD]) for _ in range(2)]
        pt = core.psum(ctx, "pt", [P, 4, P])
        pu = core.psum(ctx, "pu", [P, 3, P])
        with nc.Block() as block:
            @block.sync
            def _(sp):
                wd = core.i["w_mla_in"].rearrange("(k p) n -> p k n", p=P)
                sp.dma_start(w[:, :, 0:QL], wd[:, :, 0:QL]).then_inc(s["w"], 16)
                sp.dma_start(w[:, :, QL:], wd[:, :, QL:]).then_inc(s["w"], 16)
                sp.dma_start(gq[:, :], core.i["g_cq"].to_broadcast([P, QL])).then_inc(s["gain"], 16)
                sp.dma_start(gk[:, :], core.i["g_ckv"].to_broadcast([P, KL])).then_inc(s["gain"], 16)
                sp.dma_start(cos[:, :, :], core.i["cos"]).then_inc(s["gain"], 16)
                sp.dma_start(sin[:, :, :], core.i["sin"]).then_inc(s["gain"], 16)
                sp.wait_ge(s["normed"], 2 * T)
                sp.wait_ge(s["rope"], 4 * T)
                for name, tile in (("lat", lat), ("kr", kr)):
                    sp.dma_start(core.o[name + "_p"].rearrange("(t p) r -> p t r", p=P), tile[:, 0:NT, :]).then_inc(s["stored"], 16)
                    sp.dma_start(core.o[name + "_s"], tile[:NS, NT, :]).then_inc(s["stored"], 16)
                sp.wait_ge(s["stored"], 64)

            @block.tensor
            def _(pe):
                pe.wait_ge(s["w"], 32)
                for t in range(T + 1):
                    if t < T:
                        n = P if t < NT else NS
                        if t >= 2:
                            after(pe, at("rope", t - 1, 0), at("normed", t - 1, 0))
                        for k in range(KD):
                            pe.matmul(pq[t % 2][:n, :], xnT[:, k, P * t:P * t + n], w[:, k, 0:QL], start=k == 0, stop=k == KD - 1)
                        for k in range(KD):
                            last = pe.matmul(pk[t % 2][:n, :], xnT[:, k, P * t:P * t + n], w[:, k, QL:], start=k == 0, stop=k == KD - 1)
                        last.then_inc(s["proj"], 1)
                    if t:
                        u = t - 1
                        n = P if u < NT else NS
                        after(pe, at("normed", u, 2), at("rope", u, 4), at("copied", u, 0))
                        eye = core.const[:n, C_ID, :n]
                        for j in range(4):
                            pe.transpose(pt[:, j, :n], cq[:n, u, P * j:P * j + P], eye)
                        for j in range(2):
                            last = pe.transpose(pu[:, j, :n], lat[:n, u, P * j:P * j + P], eye)
                        if u == NT:
                            last = pe.transpose(pu[:RD, 2, :n], kr[:n, u, :], eye)
                        last.then_inc(s["turned"], 1)

            @block.scalar
            def _(act):
                for t in range(T + 1):
                    if t < T:
                        n = P if t < NT else NS
                        after(act, at("proj", t, 1))
                        if t:
                            after(act, at("square", t, 0))
                        act.activation(junk[:n, 0:QL], pq[t % 2][:n, :], ACT.Square, accum_out=st[:n, t, 0, 0:1]).then_inc(s["square"], 1)
                        act.activation(junk[:n, QL:], pk[t % 2][:n, 0:KL], ACT.Square, accum_out=st[:n, t, 0, 1:2]).then_inc(s["square"], 1)
                        after(act, at("mean", t, 1))
                        act.activation(st[:n, t, 1, :], st[:n, t, 1, :], ACT.Sqrt).then_inc(s["root"], 1)
                    if t:
                        u = t - 1
                        n = P if u < NT else NS
                        after(act, at("turned", u, 1))
                        act.activation(cqT[:, :, P * u:P * u + n], pt[:, :, :n], ACT.Copy).then_inc(s["copied"], 1)
                        act.activation(ckvT[:, :, P * u:P * u + n], pu[:, 0:2, :n], ACT.Copy).then_inc(s["copied"], 1)
                        act.activation(krTs[:, :], pu[:RD, 2, 0:NS] if u == NT else core.const[:RD, C_ID, 0:NS], ACT.Copy).then_inc(s["copied"], 1)
                        if u < NT:
                            after(act, at("copied", u, 3))

            @block.vector
            def _(dve):
                dve.wait_ge(s["gain"], 64)
                for t in range(T):
                    n = P if t < NT else NS
                    after(dve, at("square", t, 2))
                    dve.tensor_scalar(st[:n, t, 1, 0:1], st[:n, t, 0, 0:1], 1.0 / QL, EPS, ALU.mult, ALU.add)
                    dve.tensor_scalar(st[:n, t, 1, 1:2], st[:n, t, 0, 1:2], 1.0 / KL, EPS, ALU.mult, ALU.add).then_inc(s["mean"], 1)
                    after(dve, at("root", t, 1))
                    dve.reciprocal(st[:n, t, 2, :], st[:n, t, 1, :]).then_inc(s["inv"], 1)
                    after(dve, at("inv", t, 1))
                    dve.scalar_tensor_tensor(cq[:n, t, :], pq[t % 2][:n, :], st[:n, t, 2, 0:1], gq[:n, :], ALU.mult, ALU.mult).then_inc(s["normed"], 1)
                    dve.scalar_tensor_tensor(lat[:n, t, :], pk[t % 2][:n, 0:KL], st[:n, t, 2, 1:2], gk[:n, :], ALU.mult, ALU.mult).then_inc(s["normed"], 1)

                    def four(a):
                        return a.rearrange("p (o j c) -> p o j c", o=1, j=2)
                    ops = turned_by(four(pk[t % 2][:n, KL:]), four(cos[:n, t, :]), four(sin[:n, t, :]), four(t1[:n, t, :]), four(t2[:n, t, :]), four(kr[:n, t, :]))
                    for j, op in enumerate(ops):
                        if j == 3:
                            after(dve, at("rope", t, 3))
                        op(dve).then_inc(s["rope"], 1)


def mla_qkv(core, lat, kr, cqT, ckvT, cos, sin, q, kn, kr8, v, ksc, wuv):
    nc = core.nc
    T = NT + 1
    QW = H * QK
    with Marks(core, "qkv", w=48, gain=32, gains=1, q_made=1, q_out=1, k_made=1, v_made=1, v_out=1, k_square=2, q_square=1, rope=4, stat=11,
               root=2, k_out=3, q_done=2, stored=32) as s, ExitStack() as ctx:
        at = s.at
        wq = core.sbuf(ctx, "wq", [P, 4, QW])
        wk = core.sbuf(ctx, "wk", [P, 2, H * HD])
        g = core.sbuf(ctx, "g", [P, 3, QK])
        sq = core.sbuf(ctx, "sq", [P, H, QK])
        sqk = core.sbuf(ctx, "sqk", [P, H, HD])
        t1 = core.sbuf(ctx, "t1", [P, H, RD])
        t2 = core.sbuf(ctx, "t2", [P, H, RD])
        krs = core.sbuf(ctx, "krs", [P, T])
        junk = core.sbuf(ctx, "junk", [P, RD])
        st = core.sbuf(ctx, "st", [P, 6, H])
        pq = core.psum(ctx, "pq", [P, QW])
        pk = core.psum(ctx, "pk", [P, H, HD])
        pv = core.psum(ctx, "pv", [P, H, HD])
        with nc.Block() as block:
            @block.sync
            def _(sp):
                sp.dma_start(wk[:, :, :], core.i["w_uk"].rearrange("(k p) n -> p k n", p=P)).then_inc(s["w"], 16)
                sp.dma_start(wuv[:, :, :], core.i["w_uv"].rearrange("(k p) n -> p k n", p=P)).then_inc(s["w"], 16)
                sp.dma_start(wq[:, :, :], core.i["w_uq"].rearrange("(k p) n -> p k n", p=P)).then_inc(s["w"], 16)
                sp.dma_start(g[:, 0, :], core.i["g_q"].to_broadcast([P, QK])).then_inc(s["gain"], 16)
                sp.dma_start(g[:, 1, :], core.i["g_k"].to_broadcast([P, QK])).then_inc(s["gain"], 16)
                sp.wait_ge(s["stat"], 11 * T)
                sp.dma_start(core.o["ksc_p"].rearrange("(t p) r -> p t r", p=P), ksc[:, 0:NT, :]).then_inc(s["stored"], 16)
                sp.dma_start(core.o["ksc_s"], ksc[:NS, NT, :]).then_inc(s["stored"], 16)
                sp.wait_ge(s["stored"], 32)

            @block.tensor
            def _(pe):
                pe.wait_ge(s["w"], 48)
                for t in range(T):
                    n = P if t < NT else NS

                    def project(out, k_count, xT, w, width):
                        for c in range(0, width, SEQ):
                            for k in range(k_count):
                                last = pe.matmul(out[:n, c:c + SEQ], xT[:, k, P * t:P * t + n], w[:, k, c:c + SEQ], start=k == 0, stop=k == k_count - 1)
                        return last

                    after(pe, at("k_out", t, 0))
                    project(pk[:, :, :].rearrange("p h d -> p (h d)"), 2, ckvT, wk, H * HD).then_inc(s["k_made"], 1)
                    after(pe, at("q_out", t, 0))
                    project(pq, 4, cqT, wq, QW).then_inc(s["q_made"], 1)
                    if t < NT:
                        after(pe, at("v_out", t, 0))
                        project(pv[:, :, :].rearrange("p h d -> p (h d)"), 2, ckvT, wuv, H * HD).then_inc(s["v_made"], 1)

            @block.scalar
            def _(act):
                for t in range(T):
                    n = P if t < NT else NS
                    after(act, at("k_made", t, 1), at("stat", t, 0), at("k_square", t, 0))
                    act.activation(sqk[:n, :, :], pk[:n, :, :], ACT.Square).then_inc(s["k_square"], 1)
                    act.activation(junk[:n, :], kr[:n, t, :], ACT.Square, accum_out=krs[:n, t:t + 1]).then_inc(s["k_square"], 1)
                    after(act, at("q_made", t, 1))
                    act.activation(q[:n, t, :, :], pq[:n, :].rearrange("p (h d) -> p h d", h=H), ACT.Copy).then_inc(s["q_out"], 1)
                    if t < NT:
                        after(act, at("v_made", t, 1))
                        act.activation(v[:n, t, :, :], pv[:n, :, :], ACT.Copy).then_inc(s["v_out"], 1)
                    after(act, at("stat", t, 3))
                    act.activation(st[:n, 0, :], st[:n, 1, :], ACT.Sqrt).then_inc(s["root"], 1)
                    after(act, at("rope", t, 4))
                    act.activation(sq[:n, :, :], q[:n, t, :, :], ACT.Square).then_inc(s["q_square"], 1)
                    after(act, at("stat", t, 10))
                    act.activation(st[:n, 4, :], st[:n, 4, :], ACT.Sqrt).then_inc(s["root"], 1)

            @block.vector
            def _(dve):
                dve.wait_ge(s["gain"], 32)
                dve.tensor_tensor(g[:, 2, :], g[:, 0, :], g[:, 1, :], ALU.mult).then_inc(s["gains"], 1)
                for t in range(T):
                    n = P if t < NT else NS

                    def wide(a, width):
                        return a.rearrange("p (h o) -> p h o", o=1).to_broadcast([n, H, width])

                    after(dve, at("k_square", t, 2))
                    dve.tensor_reduce(st[:n, 0, :], sqk[:n, :, :], AX.X, ALU.add).then_inc(s["stat"], 1)
                    after(dve, at("stat", t, 1))
                    dve.tensor_scalar(st[:n, 1, :], st[:n, 0, :], krs[:n, t:t + 1], 1.0 / QK, ALU.add, ALU.mult).then_inc(s["stat"], 1)
                    after(dve, at("stat", t, 2))
                    dve.tensor_scalar(st[:n, 1, :], st[:n, 1, :], EPS, None, ALU.add).then_inc(s["stat"], 1)
                    after(dve, at("q_out", t, 1), at("rope", t, 0))

                    def four(a):
                        return a.rearrange("p h (j c) -> p h j c", j=2)
                    rot = four(q[:n, t, :, HD:])
                    c4, s4 = (a[:n, t:t + 1, :].rearrange("p o (j c) -> p o j c", j=2).to_broadcast([n, H, 2, RD // 2]) for a in (cos, sin))
                    for j, op in enumerate(turned_by(rot, c4, s4, four(t1[:n, :, :]), four(t2[:n, :, :]), rot)):
                        if j == 3:
                            after(dve, at("rope", t, 3))
                        op(dve).then_inc(s["rope"], 1)
                    after(dve, at("root", t, 1))
                    dve.reciprocal(ksc[:n, t, :], st[:n, 0, :]).then_inc(s["stat"], 1)
                    after(dve, at("stat", t, 4))
                    dve.tensor_tensor(st[:n, 2, :], ksc[:n, t, :], ksc[:n, t, :], ALU.mult).then_inc(s["stat"], 1)
                    after(dve, at("stat", t, 5))
                    dve.tensor_tensor(st[:n, 2, :], st[:n, 2, :], st[:n, 1, :], ALU.mult).then_inc(s["stat"], 1)
                    after(dve, at("stat", t, 6))
                    dve.tensor_scalar(st[:n, 2, :], st[:n, 2, :], -0.5, 1.5, ALU.mult, ALU.add).then_inc(s["stat"], 1)
                    after(dve, at("stat", t, 7))
                    dve.tensor_tensor(ksc[:n, t, :], ksc[:n, t, :], st[:n, 2, :], ALU.mult).then_inc(s["stat"], 1)
                    after(dve, at("stat", t, 8))
                    dve.tensor_scalar(st[:n, 2, :], ksc[:n, t, :], SCALE, None, ALU.mult).then_inc(s["k_out"], 1)
                    after(dve, at("k_out", t, 1))
                    if t < NT:
                        dve.tensor_tensor(kn[:n, t, :, :], pk[:n, :, :], wide(st[:n, 2, :], HD), ALU.mult).then_inc(s["k_out"], 1)
                        dve.tensor_tensor(kr8[:n, t, :, :], kr[:n, t:t + 1, :].to_broadcast([n, H, RD]), wide(st[:n, 2, :], RD), ALU.mult).then_inc(s["k_out"], 1)
                    after(dve, at("q_square", t, 1))
                    dve.tensor_reduce(st[:n, 3, :], sq[:n, :, :], AX.X, ALU.add).then_inc(s["stat"], 1)
                    after(dve, at("stat", t, 9))
                    dve.tensor_scalar(st[:n, 4, :], st[:n, 3, :], 1.0 / QK, EPS, ALU.mult, ALU.add).then_inc(s["stat"], 1)
                    after(dve, at("root", t, 2))
                    dve.reciprocal(st[:n, 5, :], st[:n, 4, :]).then_inc(s["stat"], 1)
                    after(dve, at("stat", t, 11))
                    dve.tensor_tensor(q[:n, t, :, :], q[:n, t, :, :], wide(st[:n, 5, :], QK), ALU.mult).then_inc(s["q_done"], 1)
                    after(dve, at("q_done", t, 1), at("gains", 0, 1))
                    dve.tensor_tensor(q[:n, t, :, :], q[:n, t, :, :], g[:n, 2:3, :].to_broadcast([n, H, QK]), ALU.mult).then_inc(s["q_done"], 1)


def mla_seq(core, q, kn, kr8, v, oT):
    nc = core.nc
    with Marks(core, "att", q_staged=4, k_staged=6, q_turned=2, k_turned=2, q_copied=4, k_copied=4, scored=2 * NT, low=2 * NT, exped=2 * NT,
               inv=2 * NT, p_done=2 * NT, p_turned=2 * NT, p_even=NT, p_odd=NT, summed=2, out=2) as s, ExitStack() as ctx:
        at = s.at

        def two(name, shape):
            return [core.sbuf(ctx, name, list(shape)) for _ in range(2)]

        qn, qr, knh, krh, vh = (two(n, (P, NT, w)) for n, w in (("qn", P), ("qr", RD), ("knh", P), ("krh", RD), ("vh", P)))
        qnT, knT = two("qnT", (P, SEQ)), two("knT", (P, SEQ))
        qrT, krT = two("qrT", (RD, SEQ)), two("krT", (RD, SEQ))
        p = two("p", (P, NT, SEQ))
        pT = two("pT", (P, NT, SEQ))
        st = two("st", (P, 3, NT))
        bank = [[core.psum(ctx, "bank", [P, SEQ]) for _ in range(4)] for _ in range(2)]

        def head(tile, h, lo, hi):
            return tile[:, 0:NT, ds(h, 1), lo:hi].rearrange("p t o d -> p t (o d)")

        with nc.Block() as block:
            @block.gpsimd
            def _(pool):
                with pool.Fori(0, H // 2) as i:
                    for a in range(2):
                        after(pool, at("summed", i, 0))
                        for dst, src, w in ((knh, kn, HD), (krh, kr8, RD), (vh, v, HD)):
                            pool.tensor_copy(dst[a][:, :, :], head(src, 2 * i + a, 0, w)).then_inc(s["k_staged"], 1)

            @block.scalar
            def _(act):
                with act.Fori(0, H // 2) as i:
                    for a in range(2):
                        apart(act, at("q_turned", i, 0))
                        act.activation(qn[a][:, :, :], head(q, 2 * i + a, 0, HD), ACT.Copy).then_inc(s["q_staged"], 1)
                        act.activation(qr[a][:, :, :], head(q, 2 * i + a, HD, QK), ACT.Copy).then_inc(s["q_staged"], 1)
                    for a in range(2):
                        after(act, at("q_turned", i, a + 1))
                        act.activation(qnT[a][:, :], bank[a][0][:, :], ACT.Copy).then_inc(s["q_copied"], 1)
                        act.activation(qrT[a][:, :], bank[a][1][:RD, :], ACT.Copy).then_inc(s["q_copied"], 1)
                    for t in range(NT):
                        for a in range(2):
                            n = P * (t + 1)
                            after(act, at("low", i, 2 * t + a + 1))
                            act.activation(p[a][:, t, 0:n], bank[a][t][:, 0:n], ACT.Exp, bias=st[a][:, 0, t:t + 1],
                                           accum_out=st[a][:, 1, t:t + 1]).then_inc(s["exped"], 1)
                    for t in range(0, NT, 2):
                        for a in range(2):
                            after(act, at("p_turned", i, 2 * t + a + 1))
                            act.activation(pT[a][:, t, 0:P * (t + 1)], bank[a][t][:, 0:P * (t + 1)], ACT.Copy).then_inc(s["p_even"], 1)
                    for a in range(2):
                        apart(act, at("summed", i, a + 1))
                        act.activation(part(oT, 2 * i + a, SEQ), bank[a][0][:, :], ACT.Copy).then_inc(s["out"], 1)

            @block.vector
            def _(dve):
                with dve.Fori(0, H // 2) as i:
                    for a in range(2):
                        after(dve, at("k_turned", i, a + 1))
                        dve.tensor_copy(knT[a][:, :], bank[a][2][:, :]).then_inc(s["k_copied"], 1)
                        dve.tensor_copy(krT[a][:, :], bank[a][3][:RD, :]).then_inc(s["k_copied"], 1)
                    for t in range(NT):
                        for a in range(2):
                            after(dve, at("scored", i, 2 * t + a + 1))
                            dve.tensor_reduce(st[a][:, 0, t:t + 1], bank[a][t][:, 0:P * (t + 1)], AX.X, ALU.max, negate=True).then_inc(s["low"], 1)
                    for t in range(NT):
                        for a in range(2):
                            n = P * (t + 1)
                            after(dve, at("exped", i, 2 * t + a + 1))
                            dve.reciprocal(st[a][:, 2, t:t + 1], st[a][:, 1, t:t + 1]).then_inc(s["inv"], 1)
                            after(dve, at("inv", i, 2 * t + a + 1))
                            dve.tensor_scalar(p[a][:, t, 0:n], p[a][:, t, 0:n], st[a][:, 2, t:t + 1], None, ALU.mult).then_inc(s["p_done"], 1)
                    for t in range(1, NT, 2):
                        for a in range(2):
                            after(dve, at("p_turned", i, 2 * t + a + 1))
                            dve.tensor_copy(pT[a][:, t, 0:P * (t + 1)], bank[a][t][:, 0:P * (t + 1)]).then_inc(s["p_odd"], 1)

            @block.tensor
            def _(pe):
                def turn(out, src, width):
                    for t in range(NT):
                        last = pe.transpose(out[:width, P * t:P * t + P], src[:, t, 0:width], core.ident)
                    return last

                with pe.Fori(0, H // 2) as i:
                    for a in range(2):
                        after(pe, at("q_staged", i, 2 * a + 2), at("out", i, 0))
                        turn(bank[a][0], qn[a], HD)
                        turn(bank[a][1], qr[a], RD).then_inc(s["q_turned"], 1)
                        after(pe, at("k_staged", i, 3 * a + 3))
                        turn(bank[a][2], knh[a], HD)
                        turn(bank[a][3], krh[a], RD).then_inc(s["k_turned"], 1)
                    for t in range(NT):
                        n = P * (t + 1)
                        for a in range(2):
                            if t == 0:
                                after(pe, at("q_copied", i, 2 * a + 2), at("k_copied", i, 2 * a + 2))
                            out = bank[a][t]
                            rows = slice(P * t, P * t + P)
                            pe.matmul(out[:, 0:n], qnT[a][:, rows], knT[a][:, 0:n], start=True, stop=False)
                            pe.matmul(out[:, 0:n], qrT[a][:, rows], krT[a][:, 0:n], start=False, stop=False)
                            pe.matmul(out[:, rows], core.ident, core.const[:, C_NEG, :], start=False, stop=True).then_inc(s["scored"], 1)
                    for t in range(NT):
                        for a in range(2):
                            after(pe, at("p_done", i, 2 * t + a + 1))
                            for j in range(t + 1):
                                last = pe.transpose(bank[a][t][:, P * j:P * j + P], p[a][:, t, P * j:P * j + P], core.ident)
                            last.then_inc(s["p_turned"], 1)
                    for a in range(2):
                        after(pe, at("p_even", i, NT - 2 + a + 1), at("p_odd", i, NT - 2 + a + 1))
                        for t in range(NT):
                            for j in range(t + 1):
                                last = pe.matmul(bank[a][0][:, P * t:P * t + P], vh[a][:, j, :], pT[a][:, t, P * j:P * j + P], start=j == 0, stop=j == t)
                        last.then_inc(s["summed"], 1)


def mla_dec(core, q, ckvT, krTs, ksc, wuv, os):
    nc = core.nc
    N = NS * H
    BQ = 4
    NG = PER // BQ
    T0 = SEQ
    TURNS = NS // 2
    with Marks(core, "pag", inp=96, step=14, turned=1, lat_made=1, self_made=1,
               idx=2, lc0=16, lc1=16, lr0=16, lr1=16, lk0=16, lk1=16,
               flip=2 * NG, half0=2 * NG, half1=2 * NG, keyr=2 * NG, scored=2, soft0=10, soft1=10, maxed=2, spread=2, exped=4,
               pv=2, v_out=2, v_turned=2, o=6, final=1) as s, ExitStack() as ctx:
        at = s.at
        wukT = core.sbuf(ctx, "wukT", [P, H, KL])
        ptab = core.sbuf(ctx, "ptab", [P, NS], mybir.dt.int32)
        rest = core.sbuf(ctx, "rest", [P, 1])
        ptf = core.sbuf(ctx, "ptf", [P, NS + 2])
        idx = [core.sbuf(ctx, "idx", [P, 1], U32) for _ in range(2)]
        c = [core.sbuf(ctx, "c", [P, PER, KL]) for _ in range(2)]
        kr = [core.sbuf(ctx, "kr", [P, PER, RD]) for _ in range(2)]
        ks = [core.sbuf(ctx, "ks", [P, PER, H]) for _ in range(2)]
        qnT = core.sbuf(ctx, "qnT", [P, H, NS])
        qr2 = core.sbuf(ctx, "qr2", [P, NS, 2, H])
        qlat = core.sbuf(ctx, "qlat", [P, 2, NS, H])
        prod = core.sbuf(ctx, "prod", [P, 3, NS, H])
        spread = core.sbuf(ctx, "spread", [NS, NS, H])
        sself = core.sbuf(ctx, "sself", [P, N])
        krep = core.sbuf(ctx, "krep", [P, N])
        cT = [core.sbuf(ctx, "cT", [P, 2, BQ, P]) for _ in range(2)]
        rT = [core.sbuf(ctx, "rT", [P, BQ // 2, P]) for _ in range(2)]
        S = [core.sbuf(ctx, "S", [P, PER, H]) for _ in range(2)]
        m = [core.sbuf(ctx, "m", [P, 6, H]) for _ in range(2)]
        mx = [core.sbuf(ctx, "mx", [H, 1 + H]) for _ in range(2)]
        vs = core.sbuf(ctx, "vs", [H, KL])
        olat = core.sbuf(ctx, "olat", [P, 2, NS, H])
        b0 = [core.psum(ctx, "b0", [P, BQ, P]) for _ in range(2)]
        b1 = [core.psum(ctx, "b1", [P, BQ, P]) for _ in range(2)]
        b2 = core.psum(ctx, "b2", [P, BQ // 2, P])
        pS = core.psum(ctx, "pS", [P, PER, H])
        pM = core.psum(ctx, "pM", [P, P + 4 * H])
        pO = core.psum(ctx, "pO", [P, KL])
        M_SPREAD, M_SUM, M_VALUE = (slice(P + k * H, P + (k + w) * H) for k, w in ((0, 1), (1, 1), (2, 2)))

        def flat(tile):
            return tile[:, :, :].rearrange("p a b -> p (a b)")

        def before(i, a):
            return (i, 0) if a else (i - 1, 1)

        def turns(eng, turn):
            turn(0, True)
            with eng.Fori(1, TURNS) as i:
                turn(i, False)

        with nc.Block() as block:
            @block.sync
            def _(sp):
                with nc.allow_non_contiguous_dma(reason="a page number for each partition"):
                    for r in range(GRP):
                        sp.dma_start(ptab[r:P:GRP, :], core.i["page_table"].rearrange("b g -> g b")).then_inc(s["inp"], 16)
                sp.dma_start(rest[:, :], core.i["rest"]).then_inc(s["inp"], 16)
                sp.dma_start(wukT[:, :, :], core.i["w_ukT"]).then_inc(s["inp"], 16)

            @block.gpsimd
            def _(pool):
                def gather(a):
                    for dst, src, name in ((c, "cache_latent", "lc"), (kr, "cache_krope", "lr"), (ks, "cache_kscale", "lk")):
                        pool.indirect_dma_start(out=flat(dst[a]), out_offset=None, in_=core.i[src],
                                                in_offset=bass.IndirectOffsetOnAxis(ap=idx[a][:, 0:1], axis=0)).then_inc(s[f"{name}{a}"], 16)

                for a in range(2):
                    pool.wait_ge(s["idx"], a + 1)
                    gather(a)
                with pool.Fori(1, TURNS) as i:
                    for a in range(2):
                        apart(pool, at("idx", i, a + 1), at("pv", i - 1, a + 1))
                        gather(a)

            @block.scalar
            def _(act):
                def soften(i, a):
                    after(act, at(f"soft{a}", i, 7))
                    act.activation(S[a][:, :, :], S[a][:, :, :], ACT.Exp).then_inc(s["exped"], 1)
                    act.activation(m[a][:, 3, :], m[a][:, 2, :], ACT.Exp).then_inc(s["exped"], 1)

                def value_out(i, a):
                    after(act, at("pv", i, a + 1), at("v_turned", i, a))
                    act.activation(vs[:, :], pO[:H, :], ACT.Copy).then_inc(s["v_out"], 1)

                def turn(i, first):
                    for a in range(2):
                        for g in range(NG):
                            after(act, at("flip", i, NG * a + g + 1))
                            act.activation(cT[g % 2][:, 0, :, :], b0[g % 2][:, :, :], ACT.Copy).then_inc(s["half0"], 1)
                            act.activation(rT[g % 2][:, :, :], b2[:, :, :], ACT.Copy).then_inc(s["keyr"], 1)
                            if a or not first:
                                if g == 3:
                                    soften(*before(i, a))
                                if g == 6:
                                    value_out(*before(i, a))

                turns(act, turn)
                soften(TURNS - 1, 1)
                value_out(TURNS - 1, 1)

            @block.tensor
            def _(pe):
                pe.wait_ge(s["inp"], 96)
                eye = core.const[:NS, C_ID, 0:NS]
                for h in range(H):
                    pe.transpose(pM[:, NS * h:NS * h + NS], q[:NS, NT, h, 0:HD], eye)
                for h in range(H):
                    pe.transpose(pS[:, h, :], q[:NS, NT, h, QK - P:QK], eye)
                    last = pe.transpose(pS[:RD, H + h, :], q[:NS, NT, h, HD:QK], eye)
                last.then_inc(s["turned"], 1)
                pe.wait_ge(s["step"], 7)
                for h in range(H):
                    for e in range(2):
                        last = pe.matmul(pO[:, e * N + NS * h:e * N + NS * h + NS], wukT[:, h, P * e:P * e + P], qnT[:, h, :], start=True, stop=True)
                last.then_inc(s["lat_made"], 1)
                pe.wait_ge(s["step"], 13)
                own = pS[:, 0:NS, :].rearrange("p b h -> p (b h)")
                pe.matmul(own, core.ones, prod[:, 0, :, :].rearrange("p b h -> p (b h)"), start=True, stop=False)
                pe.matmul(own, core.ones, prod[:, 1, :, :].rearrange("p b h -> p (b h)"), start=False, stop=False)
                pe.matmul(own, core.ones[:RD, :], prod[:RD, 2, :, :].rearrange("p b h -> p (b h)"), start=False, stop=True)
                pe.matmul(pM[:, 0:N], core.ones[:NS, :], spread[:, :, :].rearrange("p b h -> p (b h)"), start=True, stop=True).then_inc(s["self_made"], 1)
                pe.wait_ge(s["step"], 15)

                def flips(a, g):
                    for j in range(BQ):
                        yield pe.transpose(b0[g % 2][:, j, :], c[a][:, BQ * g + j, 0:P], core.ident)
                        yield pe.transpose(b1[g % 2][:, j, :], c[a][:, BQ * g + j, P:], core.ident)
                    for j in range(BQ // 2):
                        yield pe.transpose(b2[:, j, :], kr[a][:, BQ * g + 2 * j:BQ * g + 2 * j + 2, :].rearrange("p j r -> p (j r)"), core.ident)

                def scores(b, g):
                    for jj in range(BQ // 2):
                        j0 = BQ * g + 2 * jj
                        yield pe.matmul(pS[:, j0:j0 + 2, :].rearrange("p j h -> p (j h)"), rT[g % 2][:, jj, :], part(qr2, b, 2 * H), start=True, stop=False)
                        for j in (2 * jj, 2 * jj + 1):
                            for e in range(2):
                                yield pe.matmul(pS[:, BQ * g + j, :], cT[g % 2][:, e, j, :], part(qlat, NS * e + b, H), start=False, stop=e == 1 and j % 2 == 1)

                def step(i, a, g, first):
                    n = NG * a + g
                    if g == 0:
                        after(pe, (s[f"lc{a}"], i * 16 + 16), (s[f"lr{a}"], i * 16 + 16))
                    if n or not first:
                        after(pe, at("half0", i, n), at("half1", i, n), at("keyr", i, n))
                    if g == 1 and (a or not first):
                        b = before(i, a)
                        after(pe, at(f"soft{b[1]}", b[0], 1))
                    scored = None
                    older = scores(2 * i + a, g - 1) if g else scores(2 * i + a - 1, NG - 1)
                    for turned in flips(a, g):
                        if g or a or not first:
                            scored = next(older)
                    turned.then_inc(s["flip"], 1)
                    if g == 0 and scored is not None:
                        scored.then_inc(s["scored"], 1)

                def maximum(i, a):
                    after(pe, at(f"soft{a}", i, 2), at("o", i, 3 * a))
                    pe.transpose(pM[:H, 0:P], m[a][:, 0, :], core.ident).then_inc(s["maxed"], 1)

                def spread_maximum(i, a):
                    after(pe, at(f"soft{a}", i, 4))
                    pe.matmul(pM[:, M_SPREAD], core.ones[:H, :], mx[a][:, 1:1 + H], start=True, stop=True).then_inc(s["spread"], 1)

                def values(i, a):
                    after(pe, at("exped", i, 2 * a + 2), at("v_out", i, a))
                    for j in range(PER):
                        last = pe.matmul(pO[:H, :], S[a][:, j, :], c[a][:, j, :], start=j == 0, stop=j == PER - 1)
                    last.then_inc(s["pv"], 1)

                def sums(i, a):
                    after(pe, at(f"soft{a}", i, 8), at("v_out", i, a + 1))
                    pe.matmul(pM[:, M_SUM], core.ones, m[a][:, 4, :], start=True, stop=True)
                    for e in range(2):
                        last = pe.transpose(pM[:, P + (2 + e) * H:P + (3 + e) * H], vs[:, P * e:P * e + P], core.const[:H, C_ID, 0:H])
                    last.then_inc(s["v_turned"], 1)

                def turn(i, first):
                    for a in range(2):
                        for g in range(NG):
                            step(i, a, g, first)
                            if a or not first:
                                {1: maximum, 2: spread_maximum, 4: values, 7: sums}.get(g, lambda i, a: None)(*before(i, a))

                turns(pe, turn)
                after(pe, at("half0", TURNS, 0), at("half1", TURNS, 0), at("keyr", TURNS, 0))
                for last in scores(NS - 1, NG - 1):
                    pass
                last.then_inc(s["scored"], 1)
                for stage in (maximum, spread_maximum, values, sums):
                    stage(TURNS - 1, 1)
                pe.wait_ge(s["o"], 3 * NS)
                for h in range(H):
                    for e in range(2):
                        last = pe.matmul(pO[:, NS * h:NS * h + NS], wuv[:, e, HD * h:HD * h + HD], olat[:, e, :, h], start=e == 0, stop=e == 1)
                last.then_inc(s["final"], 1)

            @block.vector
            def _(dve):
                done = [0]

                def then(ins):
                    ins.then_inc(s["step"], 1)
                    done[0] += 1
                    dve.wait_ge(s["step"], done[0])

                def number(v, a):
                    dve.tensor_copy(idx[a][:, :], part(ptf, v, 1)).then_inc(s["idx"], 1)

                then(dve.memset(qr2[:, :, :, :], 0.0))
                then(dve.memset(ptf[:, :], 0.0))
                dve.wait_ge(s["inp"], 96)
                then(dve.tensor_copy(ptf[:, 0:NS], ptab[:, :]))
                then(dve.scalar_tensor_tensor(ptf[:, 0:NS], ptf[:, 0:NS], float(GRP), rest[:, 0:1].to_broadcast([P, NS]), ALU.mult, ALU.add))
                for a in range(2):
                    number(a, a)
                dve.wait_ge(s["turned"], 1)
                then(dve.tensor_copy(qnT[:, :, :], pM[:, 0:N].rearrange("p (h b) -> p h b", h=H)))
                then(dve.tensor_copy(qr2[:RD, :, 0, :], pS[:RD, H:2 * H, :].rearrange("p h b -> p b h")))
                then(dve.tensor_copy(qr2[RD:, :, 1, :], pS[RD:, 0:H, :].rearrange("p h b -> p b h")))
                dve.wait_ge(s["lat_made"], 1)
                for e in range(2):
                    then(dve.tensor_copy(qlat[:, e, :, :], pO[:, e * N:e * N + N].rearrange("p (h b) -> p b h", h=H)))
                for e in range(2):
                    then(dve.tensor_tensor(prod[:, e, :, :], qlat[:, e, :, :], ckvT[:, e, T0:T0 + NS].rearrange("p (b o) -> p b o", o=1).to_broadcast([P, NS, H]), ALU.mult))
                then(dve.tensor_tensor(prod[:RD, 2, :, :], qr2[:RD, :, 0, :], krTs[:, :].rearrange("p (b o) -> p b o", o=1).to_broadcast([RD, NS, H]), ALU.mult))
                then(dve.tensor_tensor(spread[:, :, :], core.const[:NS, C_ID, 0:NS].rearrange("p (b o) -> p b o", o=1).to_broadcast([NS, NS, H]),
                                       ksc[:NS, NT:NT + 1, :].to_broadcast([NS, NS, H]), ALU.mult))
                dve.wait_ge(s["self_made"], 1)
                then(dve.tensor_copy(krep[:, :], pM[:, 0:N]))
                then(dve.scalar_tensor_tensor(sself[:, :], pS[:, 0:NS, :].rearrange("p b h -> p (b h)"), SCALE, krep[:, :], ALU.mult, ALU.mult))

                def soft(a, ins):
                    ins.then_inc(s[f"soft{a}"], 1)

                def minus(a, k):
                    return m[a][:, k:k + 1, :].to_broadcast([P, PER, H])

                def largest(i, a):
                    after(dve, at("scored", i, a + 1), (s[f"lk{a}"], i * 16 + 16), at("pv", i, 0))
                    soft(a, dve.scalar_tensor_tensor(flat(S[a]), flat(pS), SCALE, flat(ks[a]), ALU.mult, ALU.mult))
                    after(dve, at(f"soft{a}", i, 1))
                    soft(a, dve.tensor_reduce(m[a][:, 0, :], S[a][:, :, :].rearrange("p j h -> p h j"), AX.X, ALU.max))

                def over_all(i, a):
                    after(dve, at("maxed", i, a + 1))
                    soft(a, dve.tensor_reduce(mx[a][:, 0:1], pM[:H, 0:P], AX.X, ALU.max))
                    after(dve, at(f"soft{a}", i, 3))
                    soft(a, dve.tensor_scalar(mx[a][:, 1:1 + H], core.const[:H, C_ID, 0:H], mx[a][:, 0:1], None, ALU.mult))

                def lowered(i, a):
                    after(dve, at("spread", i, a + 1))
                    soft(a, dve.tensor_tensor(m[a][:, 1, :], pM[:, M_SPREAD], part(sself, 2 * i + a, H), ALU.max))
                    after(dve, at(f"soft{a}", i, 5))
                    soft(a, dve.tensor_tensor(m[a][:, 2, :], part(sself, 2 * i + a, H), m[a][:, 1, :], ALU.subtract))
                    soft(a, dve.tensor_tensor(S[a][:, :, :], S[a][:, :, :], minus(a, 1), ALU.subtract))

                def summed(i, a):
                    after(dve, at("exped", i, 2 * a + 2))
                    soft(a, dve.tensor_reduce(m[a][:, 4, :], S[a][:, :, :].rearrange("p j h -> p h j"), AX.X, ALU.add))

                def divided(i, a):
                    after(dve, at("v_turned", i, a + 1))
                    soft(a, dve.tensor_tensor(m[a][:, 5, :], pM[:, M_SUM], m[a][:, 3, :], ALU.add))
                    after(dve, at(f"soft{a}", i, 9))
                    soft(a, dve.reciprocal(m[a][:, 5, :], m[a][:, 5, :]))
                    for e in range(2):
                        dve.scalar_tensor_tensor(part(olat, e * NS + 2 * i + a, H), m[a][:, 3, :], part(ckvT, e * ROWS + T0 + 2 * i + a, 1),
                                                 pM[:, P + (2 + e) * H:P + (3 + e) * H], ALU.mult, ALU.add).then_inc(s["o"], 1)
                    after(dve, at(f"soft{a}", i, 10), at("o", i, 3 * a + 2))
                    both = olat[:, :, ds(2 * i + a, 1), :].rearrange("p e o h -> p e (o h)")
                    dve.tensor_tensor(both, both, m[a][:, 5:6, :].to_broadcast([P, 2, H]), ALU.mult).then_inc(s["o"], 1)

                def turn(i, first):
                    for a in range(2):
                        for g in range(NG):
                            after(dve, at("flip", i, NG * a + g + 1))
                            dve.tensor_copy(cT[g % 2][:, 1, :, :], b1[g % 2][:, :, :]).then_inc(s["half1"], 1)
                            if a or not first:
                                {0: largest, 1: over_all, 2: lowered, 5: summed, 7: divided}.get(g, lambda i, a: None)(*before(i, a))
                            if g == 3:
                                apart(dve, at(f"lc{a}", i, 16), at(f"lr{a}", i, 16), at(f"lk{a}", i, 16))
                                number(2 * i + 2 + a, a)

                turns(dve, turn)
                for stage in (largest, over_all, lowered, summed, divided):
                    stage(TURNS - 1, 1)
                dve.wait_ge(s["final"], 1)
                dve.tensor_copy(os[:, :], pO[:, 0:N]).then_inc(s["step"], 1)



def load(core):
    nc = core.nc
    with Marks(core, "load", all=48, eps=1) as s, nc.Block() as block:
        @block.sync
        def _(sp):
            sp.dma_start(core.const[:, :, :], core.i["const"]).then_inc(s["all"], 16)
            sp.dma_start(core.x[:, :, :], core.i["x_prompt"].rearrange("(t p) d -> p t d", p=P)).then_inc(s["all"], 16)
            sp.dma_start(core.xs[:, :], core.i["x_sample"]).then_inc(s["all"], 16)
            sp.wait_ge(s["all"], 48)

        @block.vector
        def _(dve):
            dve.memset(core.eps, EPS).then_inc(s["eps"], 1)


def store(core):
    nc = core.nc
    with Marks(core, "store", all=32) as s, nc.Block() as block:
        @block.sync
        def _(sp):
            sp.dma_start(core.o["y_prompt"].rearrange("(t p) d -> p t d", p=P), core.x[:, :, :]).then_inc(s["all"], 16)
            sp.dma_start(core.o["y_sample"], core.xs[:, :]).then_inc(s["all"], 16)
            sp.wait_ge(s["all"], 32)


def gdn_layer(core):
    with ExitStack() as ctx:
        F = core.sbuf(ctx, "F", [P, KINDS * H, SEQ])
        Fs = core.sbuf(ctx, "Fs", [P, KINDS * H, NS])
        os = core.sbuf(ctx, "os", [P, H * NS])
        gout = core.sbuf(ctx, "gout", [P, 1])
        cols = core.sbuf(ctx, "cols", [P, 6, NT * H])
        srep = core.sbuf(ctx, "srep", [P, 3, H * NS])
        with ExitStack() as early:
            ba = core.sbuf(early, "ba", [P, NT + 1, 2 * H])
            taps = core.sbuf(early, "taps", [P, QKV, CW, NS])
            xnT = core.sbuf(early, "xnT", [P, KD, ROWS])
            with ExitStack() as rows:
                xn = core.sbuf(rows, "xn", [P, NT, D])
                xns = core.sbuf(rows, "xns", [NS, D])
                norm(core, core.i["norm_mix"][0:1, :], xn, xns, xnT)
            gdn_in(core, xnT, F, Fs, taps, ba)
            gdn_gate(core, ba, cols, srep, gout)
        gdn_dec(core, Fs, srep, gout, os)
        gdn_seq(core, F, cols, gout)
        out_proj(core, lambda k, t: F[:, k, P * t:P * t + P] if t < NT else os[:, k * NS:k * NS + NS], core.i["w_gdn_out"])


def mla_layer(core):
    with ExitStack() as ctx:
        oT = core.sbuf(ctx, "oT", [P, H, SEQ])
        os = core.sbuf(ctx, "os", [P, H * NS])
        ckvT = core.sbuf(ctx, "ckvT", [P, 2, ROWS])
        krTs = core.sbuf(ctx, "krTs", [RD, NS])
        ksc = core.sbuf(ctx, "ksc", [P, NT + 1, H])
        wuv = core.sbuf(ctx, "wuv", [P, 2, H * HD])
        q = core.sbuf(ctx, "q", [P, NT + 1, H, QK])
        with ExitStack() as keys:
            kn = core.sbuf(keys, "kn", [P, NT, H, HD])
            kr8 = core.sbuf(keys, "kr8", [P, NT, H, RD])
            v = core.sbuf(keys, "v", [P, NT, H, HD])
            with ExitStack() as early:
                lat = core.sbuf(early, "lat", [P, NT + 1, KL])
                kr = core.sbuf(early, "kr", [P, NT + 1, RD])
                cqT = core.sbuf(early, "cqT", [P, QL // P, ROWS])
                cos = core.sbuf(early, "cos", [P, NT + 1, RD])
                sin = core.sbuf(early, "sin", [P, NT + 1, RD])
                with ExitStack() as normed:
                    xnT = core.sbuf(normed, "xnT", [P, KD, ROWS])
                    with ExitStack() as rows:
                        xn = core.sbuf(rows, "xn", [P, NT, D])
                        xns = core.sbuf(rows, "xns", [NS, D])
                        norm(core, core.i["norm_mix"][1:2, :], xn, xns, xnT)
                    mla_in(core, xnT, lat, kr, cqT, ckvT, krTs, cos, sin)
                mla_qkv(core, lat, kr, cqT, ckvT, cos, sin, q, kn, kr8, v, ksc, wuv)
            mla_seq(core, q, kn, kr8, v, oT)
        mla_dec(core, q, ckvT, krTs, ksc, wuv, os)
        out_proj(core, lambda k, t: oT[:, k, P * t:P * t + P] if t < NT else os[:, k * NS:k * NS + NS], core.i["w_mla_out"])


def peer_layer(core, layer):
    with ExitStack() as ctx:
        xn = core.sbuf(ctx, "xn", [P, NT, D])
        xns = core.sbuf(ctx, "xns", [NS, D])
        xnT = core.sbuf(ctx, "xnT", [P, KD, ROWS])
        norm(core, core.i["norm_ffn"][layer:layer + 1, :], xn, xns, xnT)
        peer(core, xn, xns, xnT, core.i[f"w_peer{layer}"], core.i[f"keys{layer}"], core.i[f"uv{layer}"])


def program(nc, ins, outs):
    with ExitStack() as ctx:
        core = Core(nc, ctx, ins, outs)
        load(core)
        gdn_layer(core)
        peer_layer(core, 0)
        mla_layer(core)
        peer_layer(core, 1)
        store(core)


def host(x):
    import numpy as np

    def c(a):
        return np.ascontiguousarray(a)

    def slices(w):
        k, n = w.shape
        return c(w.reshape(k // P, P, n // P, P).transpose(2, 1, 0, 3))

    j, i = np.arange(P)[:, None], np.arange(P)[None, :]
    tiles = [i == j, j >= 0, i >= j, i > j, np.where(i <= j, 0.0, NEG)]
    tiles += [(i // (2 << l) == j // (2 << l)) & ((i >> l) % 2 == 1) & ((j >> l) % 2 == 0) for l in range(LEVELS)]
    w = np.asarray(x["gdn_w_in"])[0]
    where = np.concatenate([np.arange(SEQ).reshape(NT, P), np.full((1, P), PAST)]).T.astype(np.float32)
    freq = np.float32(ROPE_THETA) ** (-np.arange(RD // 2, dtype=np.float32) / np.float32(RD // 2))
    angle = where[:, :, None] * freq
    cos, sin = np.cos(angle), np.sin(angle)
    return {
        "const": c(np.stack([np.broadcast_to(t, (P, P)).astype(np.float32) for t in tiles], 1)),
        "x_prompt": c(x["x_prompt"][0]), "x_sample": c(x["x_sample"][:, 0]),
        "norm_mix": c(x["norm_mix"]), "norm_ffn": c(x["norm_ffn"]),
        "w_gdn": slices(w[:, :KINDS * H * P]), "w_ba": c(w[:, KINDS * H * P:].reshape(KD, P, 2 * H).transpose(1, 0, 2)),
        "conv_w": c(x["gdn_conv_w"][0].reshape(CW, QKV, P).transpose(2, 1, 0).reshape(P, QKV * CW)),
        "state_conv": c(x["state_conv"][0].reshape(NS, CW - 1, QKV, P).transpose(3, 2, 1, 0)),
        "dt_bias": c(x["gdn_dt_bias"]), "a_log": c(x["gdn_a_log"]), "g_out": c(x["gdn_out_norm"][0].reshape(P, 1)),
        "state_ssm": c(x["state_ssm"][0].transpose(1, 0, 2, 3).reshape(H * NS, P, P)),
        "w_gdn_out": c(x["gdn_w_out"][0]),
        "counting": c(np.broadcast_to(np.arange(TOPK, dtype=np.float32), (P, TOPK))),
        "same": c(np.broadcast_to(np.eye(NS, dtype=np.float32), (P, NS, NS))),
        "w_mla_in": c(x["mla_w_in"][0]), "g_cq": c(x["mla_cq_norm"]), "g_ckv": c(x["mla_ckv_norm"]),
        "cos": c(np.concatenate([cos, cos], 2)), "sin": c(np.concatenate([-sin, sin], 2)),
        "w_uk": c(x["mla_w_uk"][0].reshape(KL, H * HD)), "w_ukT": c(x["mla_w_uk"][0].transpose(2, 1, 0)),
        "w_uv": c(x["mla_w_uv"][0].reshape(KL, H * HD)), "w_uq": c(x["mla_w_uq"][0]),
        "g_q": c(x["mla_q_norm"]), "g_k": c(x["mla_k_norm"]), "w_mla_out": c(x["mla_w_out"][0]),
        "page_table": c(x["page_table"]), "rest": (np.arange(P) % GRP).astype(np.float32).reshape(P, 1),
        "cache_latent": c(x["cache_latent"][0].reshape(-1, PER * KL)), "cache_krope": c(x["cache_krope"][0].reshape(-1, PER * RD)),
        "cache_kscale": c(x["cache_kscale"][0].reshape(-1, PER * H)),
        **{f"w_peer{l}": slices(x["peer_w_q"][l]) for l in range(2)},
        **{f"keys{l}": c(x["peer_sub_keys"][l].reshape(2 * H, NK, P).transpose(2, 0, 1)) for l in range(2)},
        **{f"uv{l}": np.concatenate([x["peer_u"][l], x["peer_v"][l]], 1) for l in range(2)},
    }


OUTS = {
    "y_prompt": (SEQ, D), "y_sample": (NS, D),
    "lat_p": (SEQ, KL), "kr_p": (SEQ, RD), "ksc_p": (SEQ, H), "lat_s": (NS, KL), "kr_s": (NS, RD), "ksc_s": (NS, H),
    "ssm_p": (H, P, P), "conv_p": (P, QKV, CW - 1), "ssm_s": (H * NS, P, P), "conv_s": (P, QKV, CW - 1, NS),
}


def kernel(**inputs):
    import numpy as np
    import concourse.bacc as bacc
    from concourse.bass_utils import run_bass_kernel_spmd

    nc = bacc.Bacc("TRN2", target_bir_lowering=False, num_devices=1)
    arrays = {f"in_{n}": a for n, a in host({n: np.asarray(a) for n, a in inputs.items()}).items()}
    ins = {n[3:]: nc.dram_tensor(n, a.shape, mybir.dt.from_np(a.dtype), kind="ExternalInput").ap() for n, a in arrays.items()}
    outs = {n: nc.dram_tensor(f"out_{n}", shape, F32, kind="ExternalOutput").ap() for n, shape in OUTS.items()}
    program(nc, ins, outs)
    result = run_bass_kernel_spmd(nc, [arrays], core_ids=[0]).results[0]
    o = {n: np.asarray(result[f"out_{n}"]) for n in OUTS}
    return (o["y_prompt"][None], o["y_sample"][:, None],
            o["lat_p"][None, None], o["kr_p"][None, None], o["ksc_p"][None, None],
            o["ssm_p"][None, None], o["conv_p"].transpose(2, 1, 0).reshape(1, 1, CW - 1, QKV * P),
            o["lat_s"][None, :, None], o["kr_s"][None, :, None], o["ksc_s"][None, :, None],
            o["ssm_s"].reshape(H, NS, P, P).transpose(1, 0, 2, 3)[None],
            o["conv_s"].transpose(3, 2, 1, 0).reshape(1, NS, CW - 1, QKV * P))
```
